# Optimizing a Trainium2 kernel written in Bass

```python
import math
import jax, jax.numpy as jnp
from jax import lax
import numpy as np

D_MODEL = 1024
BATCH = 1
SEQ = 1024
DEPTH = 1

ATTN_HEADS = 8
ATTN_HEAD_DIM = 64
ATTN_V_DIM = 2 * ATTN_HEAD_DIM
ROPE_THETA = 500000.0
ROPE_DIM = ATTN_HEAD_DIM // 4
Q_BLOCK = 128
GMLP_WIDTH = D_MODEL
GMLP_GROUPS = 8
GMLP_GROUP_DIM = GMLP_WIDTH // GMLP_GROUPS
GMLP_CHUNK = 128
PEER_HEADS = 8
PEER_KEYS = 128
PEER_EXPERTS = PEER_KEYS * PEER_KEYS
PEER_TOPK = 16
PEER_QDIM = 256
PEER_HALF = PEER_QDIM // 2
PEER_TOKEN_BLOCK = 128
NORM_EPS = 1e-6
N_MOD = 6

Q_COLS = ATTN_HEADS * 2 * ATTN_HEAD_DIM
K_COLS = ATTN_HEADS * 2 * ATTN_HEAD_DIM
V_COLS = ATTN_HEADS * ATTN_V_DIM
Z_COLS = 2 * GMLP_WIDTH
GATE_COLS = 2 * D_MODEL
IN_COLS = Q_COLS + K_COLS + V_COLS + Z_COLS + GATE_COLS
SPLITS = [Q_COLS, Q_COLS + K_COLS, Q_COLS + K_COLS + V_COLS, Q_COLS + K_COLS + V_COLS + Z_COLS]

kernel_name = "hybrid_diffattn_gmlp_peer_encoder"

def rms_norm(x, g):
    xf = x.astype(jnp.float32)
    y = xf * lax.rsqrt(jnp.mean(xf * xf, axis=-1, keepdims=True) + NORM_EPS)
    return (y * g.astype(jnp.float32)).astype(x.dtype)

def layer_norm(x, g, b):
    xf = x.astype(jnp.float32)
    mu = jnp.mean(xf, axis=-1, keepdims=True)
    var = jnp.mean(jnp.square(xf - mu), axis=-1, keepdims=True)
    y = (xf - mu) * lax.rsqrt(var + NORM_EPS)
    return (y * g.astype(jnp.float32) + b.astype(jnp.float32)).astype(x.dtype)

def rope_tables(positions, dtype):
    inv_freq = ROPE_THETA ** (-jnp.arange(0, ROPE_DIM, 2, dtype=jnp.float32) / ROPE_DIM)
    ang = positions.astype(jnp.float32)[..., None] * inv_freq
    return (jnp.cos(ang)[:, :, None, None, :].astype(dtype),
            jnp.sin(ang)[:, :, None, None, :].astype(dtype))

def partial_rope(t, cos, sin):
    half = ROPE_DIM // 2
    r1 = t[..., :half]
    r2 = t[..., half:ROPE_DIM]
    return jnp.concatenate([r1 * cos - r2 * sin, r2 * cos + r1 * sin, t[..., ROPE_DIM:]], axis=-1)

def diff_attention(q, k, v, lam):
    B, S = q.shape[0], q.shape[1]
    nb = S // Q_BLOCK
    scale = ATTN_HEAD_DIM ** -0.5
    qb = (q * scale).reshape(B, nb, Q_BLOCK, ATTN_HEADS, 2, ATTN_HEAD_DIM).transpose(1, 0, 2, 3, 4, 5)

    def block(qi):
        s = jnp.einsum('bqhtd,bkhtd->bhtqk', qi, k).astype(jnp.float32)
        p = jax.nn.softmax(s, axis=-1)
        a = p[:, :, 0] - lam * p[:, :, 1]
        return jnp.einsum('bhqk,bkhe->bqhe', a.astype(v.dtype), v)

    o = lax.map(block, qb)
    return o.transpose(1, 0, 2, 3, 4).reshape(B, S, ATTN_HEADS, ATTN_V_DIM)

def spatial_gating(z, ln_g, ln_b, w_s, b_s):
    u, v = jnp.split(z, 2, axis=-1)
    v = layer_norm(v, ln_g, ln_b)
    B, S = v.shape[0], v.shape[1]
    vc = v.reshape(B, S // GMLP_CHUNK, GMLP_CHUNK, GMLP_GROUPS, GMLP_GROUP_DIM)
    sv = jnp.einsum('gpq,bcqgh->bcpgh', w_s, vc) + b_s.T[None, None, :, :, None]
    return u * sv.reshape(B, S, GMLP_WIDTH)

def peer(h, w_q, sub_keys, exp_u, exp_v):
    B, S, D = h.shape
    q = (h @ w_q).reshape(B, S, PEER_HEADS, 2, PEER_HALF)
    s = jnp.einsum('bshtd,htnd->bshtn', q, sub_keys).astype(jnp.float32)
    s_top, i_top = lax.top_k(s, PEER_TOPK)
    cand = s_top[..., 0, :, None] + s_top[..., 1, None, :]
    cand_idx = i_top[..., 0, :, None] * PEER_KEYS + i_top[..., 1, None, :]
    cand = cand.reshape(B, S, PEER_HEADS, PEER_TOPK * PEER_TOPK)
    cand_idx = cand_idx.reshape(B, S, PEER_HEADS, PEER_TOPK * PEER_TOPK)
    best, sel = lax.top_k(cand, PEER_TOPK)
    idx = jnp.take_along_axis(cand_idx, sel, axis=-1)
    g = jax.nn.softmax(best, axis=-1).astype(h.dtype)
    T = B * S
    E = PEER_HEADS * PEER_TOPK
    nb = T // PEER_TOKEN_BLOCK
    xt = h.reshape(nb, PEER_TOKEN_BLOCK, D)
    it = idx.reshape(nb, PEER_TOKEN_BLOCK, E)
    gt = g.reshape(nb, PEER_TOKEN_BLOCK, E)

    def block(args):
        xb, ib, gb = args
        u = exp_u[ib]
        a = jax.nn.gelu(jnp.einsum('td,ted->te', xb, u)) * gb
        return jnp.einsum('te,ted->td', a, exp_v[ib])

    y = lax.map(block, (xt, it, gt))
    return y.reshape(B, S, D)

def setup_inputs(seed: int = 0) -> dict:
    key = jax.random.key(seed)
    ks = jax.random.split(key, 32)
    f32 = jnp.float32
    L, D = DEPTH, D_MODEL

    def nrm(k, shape, std):
        return jax.random.normal(k, shape, f32) * std

    def gain(k, shape):
        return 1.0 + 0.02 * jax.random.normal(k, shape, f32)

    x = jax.random.normal(ks[0], (BATCH, SEQ, D), f32)
    c = jax.random.normal(ks[1], (BATCH, D), f32)
    offset = jax.random.randint(ks[2], (BATCH, 1), 0, 1024, dtype=jnp.int32)
    positions = jnp.arange(SEQ, dtype=jnp.int32)[None, :] + offset
    return {
        "x": x,
        "c": c,
        "positions": positions,
        "w_ada": nrm(ks[3], (L, D, N_MOD * D), 0.5 * D ** -0.5),
        "b_ada": nrm(ks[4], (L, N_MOD * D), 0.02),
        "g_pre_mix": gain(ks[5], (L, D)),
        "g_post_mix": gain(ks[6], (L, D)),
        "w_in": nrm(ks[7], (L, D, IN_COLS), D ** -0.5),
        "lambda_q1": nrm(ks[8], (L, ATTN_HEAD_DIM), 0.1),
        "lambda_k1": nrm(ks[9], (L, ATTN_HEAD_DIM), 0.1),
        "lambda_q2": nrm(ks[10], (L, ATTN_HEAD_DIM), 0.1),
        "lambda_k2": nrm(ks[11], (L, ATTN_HEAD_DIM), 0.1),
        "g_subln": gain(ks[12], (L, ATTN_V_DIM)),
        "w_attn_branch": nrm(ks[13], (L, V_COLS, D), V_COLS ** -0.5),
        "gmlp_ln_g": gain(ks[14], (L, GMLP_WIDTH)),
        "gmlp_ln_b": nrm(ks[15], (L, GMLP_WIDTH), 0.02),
        "w_spatial": nrm(ks[16], (L, GMLP_GROUPS, GMLP_CHUNK, GMLP_CHUNK), GMLP_CHUNK ** -0.5),
        "b_spatial": gain(ks[17], (L, GMLP_GROUPS, GMLP_CHUNK)),
        "w_gmlp_branch": nrm(ks[18], (L, GMLP_WIDTH, D), GMLP_WIDTH ** -0.5),
        "w_out": nrm(ks[19], (L, D, D), D ** -0.5),
        "g_pre_ffn": gain(ks[20], (L, D)),
        "g_post_ffn": gain(ks[21], (L, D)),
        "w_peer_q": nrm(ks[22], (L, D, PEER_HEADS * PEER_QDIM), D ** -0.5),
        "peer_sub_keys": nrm(ks[23], (L, PEER_HEADS, 2, PEER_KEYS, PEER_HALF), PEER_HALF ** -0.5),
        "peer_u": nrm(ks[24], (L, PEER_EXPERTS, D), D ** -0.5),
        "peer_v": nrm(ks[25], (L, PEER_EXPERTS, D), PEER_HEADS ** -0.5),
    }

def reference(x, c, positions, w_ada, b_ada, g_pre_mix, g_post_mix, w_in,
              lambda_q1, lambda_k1, lambda_q2, lambda_k2, g_subln, w_attn_branch,
              gmlp_ln_g, gmlp_ln_b, w_spatial, b_spatial, w_gmlp_branch, w_out,
              g_pre_ffn, g_post_ffn, w_peer_q, peer_sub_keys, peer_u, peer_v):
    B, S, D = x.shape
    cos, sin = rope_tables(positions, x.dtype)
    c_act = jax.nn.silu(c)
    for l in range(DEPTH):
        mod = c_act @ w_ada[l] + b_ada[l]
        sh1, sc1, gt1, sh2, sc2, gt2 = [m[:, None, :] for m in jnp.split(mod, N_MOD, axis=-1)]

        h = rms_norm(x, g_pre_mix[l]) * (1.0 + sc1) + sh1
        p = h @ w_in[l]
        q, k, v, z, gates = jnp.split(p, SPLITS, axis=-1)

        q = partial_rope(q.reshape(B, S, ATTN_HEADS, 2, ATTN_HEAD_DIM), cos, sin)
        k = partial_rope(k.reshape(B, S, ATTN_HEADS, 2, ATTN_HEAD_DIM), cos, sin)
        v = v.reshape(B, S, ATTN_HEADS, ATTN_V_DIM)
        lambda_init = 0.8 - 0.6 * math.exp(-0.3 * l)
        lam = (jnp.exp(jnp.sum(lambda_q1[l].astype(jnp.float32) * lambda_k1[l].astype(jnp.float32)))
               - jnp.exp(jnp.sum(lambda_q2[l].astype(jnp.float32) * lambda_k2[l].astype(jnp.float32)))
               + lambda_init)
        o = diff_attention(q, k, v, lam)
        o = rms_norm(o, g_subln[l]) * (1.0 - lambda_init)
        y_attn = o.reshape(B, S, V_COLS) @ w_attn_branch[l]

        sg = spatial_gating(jax.nn.gelu(z), gmlp_ln_g[l], gmlp_ln_b[l], w_spatial[l], b_spatial[l])
        y_gmlp = sg @ w_gmlp_branch[l]

        gate_a, gate_g = jnp.split(jax.nn.sigmoid(gates), 2, axis=-1)
        mix = (gate_a * y_attn + gate_g * y_gmlp) @ w_out[l]
        x = x + gt1 * rms_norm(mix, g_post_mix[l])

        h2 = rms_norm(x, g_pre_ffn[l]) * (1.0 + sc2) + sh2
        y = peer(h2, w_peer_q[l], peer_sub_keys[l], peer_u[l], peer_v[l])
        x = x + gt2 * rms_norm(y, g_post_ffn[l])
    return x


_drawn_inputs = setup_inputs


def setup_inputs(seed=0):
    import zlib

    import numpy as np

    out = dict(_drawn_inputs(seed))
    spreads = {}
    factors = {'lambda_k1': 6.761,
     'lambda_q2': 7.069,
     'g_subln': 2.896,
     'gmlp_ln_g': 2.996,
     'gmlp_ln_b': 2.927,
     'b_spatial': 3.056,
     'g_post_ffn': 8.0}
    for name, (base, spread) in spreads.items():
        noise = np.random.default_rng([zlib.crc32(name.encode()), seed]).standard_normal(out[name].shape)
        drawn = base * np.exp(spread * noise) if base else spread * noise
        out[name] = __import__('jax').numpy.asarray(drawn.astype(out[name].dtype))
    for name, factor in factors.items():
        out[name] = (out[name] * factor).astype(out[name].dtype)
    return out
```

```python
import math
from contextlib import ExitStack

import numpy as np

import concourse.bass as bass
from concourse import mybir

F32 = mybir.dt.float32
F32R = mybir.dt.float32r
I32 = mybir.dt.int32
U32 = mybir.dt.uint32
ALU = mybir.AluOpType
ACT = mybir.ActivationFunctionType
AXX = mybir.AxisListType.X

P = 128
T = 1024
D = 1024
KT = D // P
TB = T // P
HALF = 512
HEADS = 8
MAP_DIM = 64
TOPK = 16
SIDES = 2 * HEADS
KEYS = 128
NMOD = 6 * KT
EPS = 1e-6
LAMBDA_INIT = 0.8 - 0.6 * math.exp(-0.3 * 0)
SCALE = MAP_DIM ** -0.5
ROPE_DIM = MAP_DIM // 4
ROPE_THETA = 500000.0
LOWEST = -3.0e38

Q0, K0, V0, ZU0, ZV0, GA0, GG0 = 0, 8, 16, 24, 32, 40, 48


class Layer:

    def __init__(self, nc, a):
        self.nc, self.a = nc, a
        self.ctx = ExitStack()
        self.stage_sems = []

    def sb(self, ctx, name, shape, dt=F32):
        return ctx.enter_context(self.nc.sbuf_tensor(name, shape, dt))

    def sem(self, name):
        self.stage_sems.append(self.nc.alloc_semaphore(name=name))
        return self.stage_sems[-1]

    def stage_end(self):
        self.nc.all_engine_barrier()
        self.nc.clear_and_free_semaphores(self.stage_sems)
        self.nc.all_engine_barrier()
        self.stage_sems = []

    def scratch(self, name, shape):
        return self.nc.dram_tensor(name, shape, F32, kind="Internal").ap()

    def build(self):
        nc = self.nc
        with self.ctx:
            c = self.ctx
            self.ident = self.sb(c, "ident", [P, P])
            self.ones_mean = self.sb(c, "ones_mean", [P, P])
            self.ones_head = self.sb(c, "ones_head", [P, P])
            self.vecs = self.sb(c, "vecs", [P, NMOD])
            self.subln_gain = self.sb(c, "subln_gain", [P, 1])
            self.mod = self.sb(c, "mod", [P, NMOD])
            self.coef = self.sb(c, "coef", [P, 4 * KT])
            self.lam = self.sb(c, "lam", [P, 1])
            self.psum = c.enter_context(nc.psum_tensor("psum", [P, 8, HALF], F32))
            self.gate_scr = self.scratch("gate_scratch", [2 * KT, P, T])
            self.u_scr = self.scratch("gelu_u_scratch", [KT, P, T])
            self.o_scr = self.scratch("attention_scratch", [HEADS, P, T])
            self.sg_scr = self.scratch("spatial_scratch", [KT, P, T])
            self.x1_scr = self.scratch("residual_scratch", [KT, P, T])
            self.route_scr = self.scratch("route_scratch", [KEYS, P, T])

            with ExitStack() as rope_scope:
                self.cos = self.sb(rope_scope, "cos", [P, T])
                self.sin = self.sb(rope_scope, "sin", [P, T])
                self.rotate = self.sb(rope_scope, "rotate", [P, P])
                self.conditioning()
                self.stage_end()
                h_hi = self.sb(rope_scope, "h_hi", [P, KT, T], F32R)
                h_lo = self.sb(rope_scope, "h_lo", [P, KT, T], F32R)
                with ExitStack() as s:
                    x = self.sb(s, "x", [P, KT, T])
                    self.load(x, self.a["xT"].rearrange("(k p) t -> p k t", p=P), "x")
                    self.rms_modulate("pre_mix", x, self.coef[:, 0:KT], self.mod[:, 0:KT], h_hi, h_lo)
                    self.stage_end()
                self.attention(h_hi, h_lo)
                self.stage_end()
                self.gmlp(h_hi, h_lo)
                self.stage_end()
                self.gates(h_hi, h_lo)
                self.stage_end()
            with ExitStack() as mixing:
                wide = self.sb(mixing, "mixed", [P, KT, T])
                with ExitStack() as s:
                    m_hi = self.sb(s, "m_hi", [P, KT, T], F32R)
                    m_lo = self.sb(s, "m_lo", [P, KT, T], F32R)
                    self.branches(wide, m_hi, m_lo)
                    self.stage_end()
                    self.out_projection(wide, m_hi, m_lo)
                    self.stage_end()
                self.residual(wide, self.sb(mixing, "x1_made", [P, KT, T]))
                self.stage_end()
            h2_hi = self.sb(c, "h2_hi", [P, KT, T], F32R)
            h2_lo = self.sb(c, "h2_lo", [P, KT, T], F32R)
            with ExitStack() as s:
                x1 = self.sb(s, "x1", [P, KT, T])
                self.load(x1, self.x1_scr.rearrange("k p t -> p k t"), "x1")
                self.rms_modulate("pre_ffn", x1, self.coef[:, 2 * KT:3 * KT], self.mod[:, 3 * KT:4 * KT], h2_hi, h2_lo)
                self.stage_end()
            self.route(h2_hi, h2_lo)
            y = self.sb(c, "y", [P, KT, T])
            self.experts(h2_hi, h2_lo, y)
            self.stage_end()
            self.finish(y)
            self.stage_end()

    def load(self, tile, src, name):
        loaded = self.sem(f"{name}_loaded")
        with self.nc.Block() as block:
            @block.sync
            def _(sp):
                sp.dma_start(tile[:], src).then_inc(loaded, 16)
                sp.wait_ge(loaded, 16)

    def conditioning(self):
        nc, a = self.nc, self.a
        NBUF = 4
        small = self.sem("small_loaded")
        ada_loaded = [self.sem(f"ada_loaded{i}") for i in range(NBUF)]
        c_ready = self.sem("c_ready")
        mod_dot = self.sem("mod_dot")
        chain = self.sem("conditioning_chain")
        lam_dots = self.sem("lam_dots")
        lam_exp = self.sem("lam_exp")
        angles = self.sem("angles")
        tables = self.sem("rope_tables")
        with ExitStack() as s:
            ada = self.sb(s, "ada", [P, NBUF, 2, D])
            cb = self.sb(s, "cb", [P, D])
            junk = self.sb(s, "junk", [P, 2, D])
            b_ada = self.sb(s, "b_ada", [P, NMOD])
            lams = self.sb(s, "lams", [P, 4, MAP_DIM])
            lam2 = self.sb(s, "lam2", [P, 4])
            pos = self.sb(s, "pos", [P, T], I32)
            freq = self.sb(s, "freq", [P, 1])
            ang = self.sb(s, "ang", [P, T])
            turns = self.sb(s, "turns", [P, T])
            folded = self.sb(s, "folded", [P, T])
            NSMALL = 9
            with nc.Block() as block:
                @block.sync
                def _(sp):
                    sp.dma_start(cb[:], a["c"].to_broadcast([P, D])).then_inc(small, 16)
                    sp.dma_start(self.ident[:], a["ident"]).then_inc(small, 16)
                    sp.dma_start(self.rotate[:], a["rotate"]).then_inc(small, 16)
                    sp.dma_start(self.vecs[:], a["vecs"]).then_inc(small, 16)
                    sp.dma_start(self.subln_gain[:], a["g_subln"]).then_inc(small, 16)
                    sp.dma_start(b_ada[:], a["b_ada"]).then_inc(small, 16)
                    sp.dma_start(freq[:], a["freq"]).then_inc(small, 16)
                    sp.dma_start(lams[:].rearrange("p a d -> p (a d)"), a["lams"].to_broadcast([P, 4 * MAP_DIM])).then_inc(small, 16)
                    sp.dma_start(pos[:], a["positions"].to_broadcast([P, T])).then_inc(small, 16)
                    for g in range(NMOD // 2):
                        if g >= NBUF:
                            sp.wait_ge(mod_dot, 2 * (g - NBUF + 1))
                        sp.dma_start(ada[:, g % NBUF], a["w_adaT"][:, 2 * g:2 * g + 2, :]).then_inc(ada_loaded[g % NBUF], 16)

                @block.scalar
                def _(act):
                    act.wait_ge(small, 16 * NSMALL)
                    act.activation(cb[:], cb[:], ACT.Silu).then_inc(c_ready, 1)
                    act.wait_ge(lam_dots, 2)
                    act.activation(lam2[:, 2:4], lam2[:, 0:2], ACT.Exp).then_inc(lam_exp, 1)
                    act.wait_ge(angles, 1)
                    act.activation(self.sin[:], ang[:], ACT.Sin).then_inc(tables, 1)
                    act.activation(self.cos[:], folded[:], ACT.Sin).then_inc(tables, 1)

                @block.vector
                def _(dve):
                    n = [0]

                    def link(ins):
                        n[0] += 1
                        ins.then_inc(chain, 1)
                        dve.wait_ge(chain, n[0])

                    dve.memset(self.ones_mean[:], 1.0 / D)
                    link(dve.memset(self.ones_head[:], 1.0 / P))
                    dve.wait_ge(small, 16 * NSMALL)
                    for i in range(2):
                        dve.tensor_tensor_reduce(out=junk[:, i, 0:MAP_DIM], in0=lams[:, 2 * i], in1=lams[:, 2 * i + 1],
                                                 scale=1.0, scalar=0.0, op0=ALU.mult, op1=ALU.add,
                                                 accum_out=lam2[:, i:i + 1]).then_inc(lam_dots, 1)
                    link(dve.tensor_copy(ang[:], pos[:]))
                    link(dve.tensor_scalar(ang[:], ang[:], freq[:, 0:1], None, ALU.mult))
                    magic = 1.5 * 2.0 ** 23
                    link(dve.tensor_scalar(turns[:], ang[:], 1.0 / (2.0 * math.pi), None, ALU.mult))
                    link(dve.tensor_scalar(turns[:], turns[:], magic, None, ALU.add))
                    link(dve.tensor_scalar(turns[:], turns[:], magic, None, ALU.subtract))
                    c1 = 6.28125
                    c2 = float(np.float32(round((2 * math.pi - c1) * 2 ** 20) / 2 ** 20))
                    c3 = 2 * math.pi - c1 - c2
                    for part in (c1, c2, c3):
                        link(dve.scalar_tensor_tensor(ang[:], turns[:], -part, ang[:], ALU.mult, ALU.add))
                    limit = float(np.nextafter(np.float32(math.pi), np.float32(0)))
                    link(dve.tensor_scalar(ang[:], ang[:], limit, -limit, ALU.min, ALU.max))
                    link(dve.tensor_scalar(folded[:], ang[:], -1.0, None, ALU.mult))
                    link(dve.tensor_tensor(folded[:], folded[:], ang[:], ALU.max))
                    dve.tensor_scalar(folded[:], folded[:], -1.0, math.pi / 2, ALU.mult, ALU.add).then_inc(angles, 1)
                    dve.wait_ge(c_ready, 1)
                    for j in range(NMOD):
                        g = j // 2
                        dve.wait_ge(ada_loaded[g % NBUF], 16 * (g // NBUF + 1))
                        if j >= 2:
                            dve.wait_ge(mod_dot, j - 1)
                        elif j == 0:
                            dve.wait_ge(lam_dots, 2)
                        dve.tensor_tensor_reduce(out=junk[:, j % 2], in0=ada[:, g % NBUF, j % 2], in1=cb[:], scale=1.0,
                                                 scalar=0.0, op0=ALU.mult, op1=ALU.add,
                                                 accum_out=self.mod[:, j:j + 1]).then_inc(mod_dot, 1)
                    dve.wait_ge(mod_dot, NMOD)
                    link(dve.tensor_tensor(self.mod[:], self.mod[:], b_ada[:], ALU.add))
                    K = KT
                    sc1, gt1, sc2, gt2 = (self.mod[:, K * i:K * i + K] for i in (1, 2, 4, 5))
                    pre1, post1, pre2, post2 = (self.vecs[:, K * i:K * i + K] for i in range(4))
                    dve.scalar_tensor_tensor(self.coef[:, 0:K], sc1, 1.0, pre1, ALU.add, ALU.mult)
                    dve.tensor_tensor(self.coef[:, K:2 * K], gt1, post1, ALU.mult)
                    dve.scalar_tensor_tensor(self.coef[:, 2 * K:3 * K], sc2, 1.0, pre2, ALU.add, ALU.mult)
                    dve.tensor_tensor(self.coef[:, 3 * K:4 * K], gt2, post2, ALU.mult)
                    dve.tensor_scalar(self.subln_gain[:], self.subln_gain[:], 1.0 - LAMBDA_INIT, None, ALU.mult)
                    dve.wait_ge(lam_exp, 1)
                    link(dve.tensor_tensor(self.lam[:], lam2[:, 2:3], lam2[:, 3:4], ALU.subtract))
                    link(dve.tensor_scalar(self.lam[:], self.lam[:], LAMBDA_INIT, None, ALU.add))

    def mean_square(self, name, src, rstd, ones, sq, tiles=KT):
        nc = self.nc
        squared = self.sem(f"{name}_squared")
        summed = self.sem(f"{name}_summed")
        chain = self.sem(f"{name}_rstd")
        ms = self.psum[:, 0:2].rearrange("p b t -> p (b t)")
        with nc.Block() as block:
            @block.scalar
            def _(act):
                for k in range(tiles):
                    if k >= 2:
                        act.wait_ge(summed, k - 1)
                    act.activation(sq[:, k % 2], src[:, k], ACT.Square).then_inc(squared, 1)
                act.wait_ge(chain, 1)
                act.activation(rstd[:], rstd[:], ACT.Sqrt).then_inc(chain, 1)

            @block.tensor
            def _(pe):
                for k in range(tiles):
                    pe.wait_ge(squared, k + 1)
                    for half in range(2):
                        last = pe.matmul(self.psum[:, half], ones[:], sq[:, k % 2, half * HALF:(half + 1) * HALF],
                                         start=(k == 0), stop=(k == tiles - 1))
                    last.then_inc(summed, 1)

            @block.vector
            def _(dve):
                dve.wait_ge(summed, tiles)
                dve.tensor_scalar(rstd[:], ms, EPS, None, ALU.add).then_inc(chain, 1)
                dve.wait_ge(chain, 2)
                dve.reciprocal(rstd[:], rstd[:]).then_inc(chain, 1)

    def rms_modulate(self, name, x, gain, shift, hi, lo):
        nc = self.nc
        scaled = self.sem(f"{name}_scaled")
        full = self.sem(f"{name}_full")
        hi_done = self.sem(f"{name}_hi")
        lo_done = self.sem(f"{name}_lo")
        with ExitStack() as s:
            rstd = self.sb(s, f"{name}_rstd_t", [P, T])
            sq = self.sb(s, f"{name}_sq", [P, 2, T])
            self.mean_square(name, x, rstd, self.ones_mean, sq)
            with nc.Block() as block:
                @block.vector
                def _(dve):
                    for k in range(KT):
                        if k >= 2:
                            dve.wait_ge(lo_done, k - 1)
                        dve.tensor_tensor(sq[:, k % 2], x[:, k], rstd[:], ALU.mult).then_inc(scaled, 1)
                        dve.wait_ge(scaled, k + 1)
                        dve.tensor_scalar(sq[:, k % 2], sq[:, k % 2], gain[:, k:k + 1], shift[:, k:k + 1],
                                          ALU.mult, ALU.add).then_inc(full, 1)
                        dve.wait_ge(hi_done, k + 1)
                        dve.tensor_tensor(lo[:, k], sq[:, k % 2], hi[:, k].bitcast(F32), ALU.subtract).then_inc(lo_done, 1)

                @block.scalar
                def _(act):
                    for k in range(KT):
                        act.wait_ge(full, k + 1)
                        act.activation(hi[:, k], sq[:, k % 2], ACT.Copy).then_inc(hi_done, 1)

    def product3(self, pe, out, w_hi, w_lo, x_hi, x_lo, start, stop):
        pe.matmul(out, w_hi, x_hi, start=start, stop=False)
        pe.matmul(out, w_hi, x_lo, start=False, stop=False)
        return pe.matmul(out, w_lo, x_hi, start=False, stop=stop)

    def projection(self, name, wt, first, x_hi, x_lo, tiles, act_out=None, dve_out=None, pe_after=None, dve_after=None, pool_program=None):
        nc = self.nc
        loaded = [self.sem(f"{name}_w_loaded{i}") for i in range(2)]
        w_hi_done = self.sem(f"{name}_w_hi_done")
        w_split = self.sem(f"{name}_w_split")
        product = self.sem(f"{name}_product")
        emptied = self.sem(f"{name}_emptied")
        acc = [self.psum[:, 2 * s:2 * s + 2].rearrange("p b t -> p (b t)") for s in range(2)]
        turns = tiles // 2
        with ExitStack() as c:
            raw = self.sb(c, f"{name}_w_raw", [P, 2, D])
            w_hi = self.sb(c, f"{name}_w_hi_t", [P, 2, KT, P], F32R)
            w_lo = self.sb(c, f"{name}_w_lo_t", [P, 2, KT, P], F32R)
            flat = lambda w, s: w[:, s].rearrange("p k n -> p (k n)")
            with nc.Block() as block:
                @block.sync
                def _(sp):
                    def turn(j0):
                        at = [sp.snap(j0 + s) if not isinstance(j0, int) else j0 + s for s in range(2)]
                        free = [sp.snap(j0 + s + 1) if not isinstance(j0, int) else j0 + s + 1 for s in range(2)]
                        src = [sp.snap(j0 + s + first) if not isinstance(j0, int) else j0 + s + first for s in range(2)]
                        for s in range(2):
                            sp.wait_ge(w_split, free[s])
                            sp.dma_start(raw[:, s], wt[bass.ds(src[s], 1)].rearrange("o p n -> (o p) n")).then_inc(loaded[s], 16)
                    with sp.Fori(0, turns) as it:
                        turn(it * 2)

                @block.scalar
                def _(act):
                    def split(j, s):
                        act.wait_ge(loaded[s], j * 8 + (16 - 8 * s))
                        act.wait_ge(product, j + 1)
                        act.activation(flat(w_hi, s), raw[:, s], ACT.Copy).then_inc(w_hi_done, 1)

                    def empty(j, s):
                        if act_out:
                            act.wait_ge(product, j + 3)
                            act_out(act, j, s, acc[s], emptied)
                    for s in range(2):
                        split(s, s)
                    if turns > 1:
                        with act.Fori(0, turns - 1) as it:
                            for s in range(2):
                                empty(it * 2 + s, s)
                                split(it * 2 + (2 + s), s)
                    for s in range(2):
                        empty(tiles - 2 + s, s)

                @block.vector
                def _(dve):
                    dve.sem_inc(w_split, 2)

                    def split(j, s):
                        dve.wait_ge(w_hi_done, j + 1)
                        dve.tensor_tensor(flat(w_lo, s), raw[:, s], flat(w_hi, s).bitcast(F32), ALU.subtract).then_inc(w_split, 1)

                    def empty(j, s):
                        if dve_out:
                            dve.wait_ge(product, j + 3)
                            dve_out(dve, j, s, acc[s], emptied)
                    for s in range(2):
                        split(s, s)
                    if dve_after is None:
                        with dve.Fori(0, turns - 1) as it:
                            for s in range(2):
                                empty(it * 2 + s, s)
                                split(it * 2 + (2 + s), s)
                        for s in range(2):
                            empty(tiles - 2 + s, s)
                    else:
                        empty(0, 0)
                        split(2, 0)
                        with dve.Fori(0, turns - 2) as it:
                            for s in range(2):
                                empty(it * 2 + (1 + s), 1 - s)
                                split(it * 2 + (3 + s), 1 - s)
                                dve_after(dve, it * 2 + s, s)
                        empty(tiles - 3, 1)
                        split(tiles - 1, 1)
                        dve_after(dve, tiles - 4, 0)
                        empty(tiles - 2, 0)
                        dve_after(dve, tiles - 3, 1)
                        empty(tiles - 1, 1)
                        dve_after(dve, tiles - 2, 0)
                        dve_after(dve, tiles - 1, 1)

                @block.tensor
                def _(pe):
                    pe.sem_inc(product, 2)
                    pe.sem_inc(emptied, 2)

                    def tile(j, s):
                        pe.wait_ge(w_split, j + 3)
                        pe.wait_ge(emptied, j + 1)
                        for half in range(2):
                            t = slice(half * HALF, (half + 1) * HALF)
                            for k in range(KT):
                                last = self.product3(pe, self.psum[:, 2 * s + half], w_hi[:, s, k], w_lo[:, s, k],
                                                     x_hi[:, k, t], x_lo[:, k, t], k == 0, k == KT - 1)
                        last.then_inc(product, 1)
                    if pe_after is None:
                        with pe.Fori(0, turns) as it:
                            for s in range(2):
                                tile(it * 2 + s, s)
                    else:
                        tile(0, 0)
                        with pe.Fori(0, turns - 1) as it:
                            for s in range(2):
                                tile(it * 2 + (1 + s), 1 - s)
                                pe_after(pe, it * 2 + s, s, emptied)
                        tile(tiles - 1, 1)
                        pe_after(pe, tiles - 2, 0, emptied)
                        pe_after(pe, tiles - 1, 1, emptied)

                if pool_program:
                    @block.gpsimd
                    def _(pool):
                        pool_program(pool, emptied)

    def attention(self, h_hi, h_lo):
        nc, w = self.nc, self.a["w_in"]
        ps = self.psum
        acc = [ps[:, 2 * s:2 * s + 2].rearrange("p b t -> p (b t)") for s in range(2)]
        turned = ps[:, 4:6].rearrange("p b t -> p (b t)")
        o_acc = ps[:, 6]
        KINDS = ("k", "q", "v")
        TILE0 = {"k": K0, "q": Q0, "v": V0}
        w_loaded = [self.sem(f"att_w_loaded_{x}") for x in KINDS]
        w_hi_done = self.sem("att_w_hi_done")
        w_split = self.sem("att_w_split")
        projected = self.sem("att_projected")
        copied = self.sem("att_copied")
        rotated = self.sem("att_rotated")
        full = self.sem("att_full")
        hi_done = self.sem("att_hi_done")
        operands = self.sem("att_operands")
        scored = self.sem("att_scored")
        negmax = self.sem("att_negmax")
        exped = self.sem("att_exped")
        mixing = self.sem("att_mixing")
        mixed = self.sem("att_mixed")
        a_turned = self.sem("att_a_turned")
        a_hi_done = self.sem("att_a_hi")
        a_split = self.sem("att_a_split")
        out_summed = self.sem("att_out_summed")
        out_copied = self.sem("att_out_copied")
        stored = [self.sem(f"att_stored{i}") for i in range(2)]
        with ExitStack() as c:
            raw = self.sb(c, "att_raw", [P, 3, D])
            w_hi = self.sb(c, "att_w_hi_t", [P, 3, KT, P], F32R)
            w_lo = self.sb(c, "att_w_lo_t", [P, 3, KT, P], F32R)
            x_hi = self.sb(c, "att_x_hi", [P, 3, T], F32R)
            x_lo = self.sb(c, "att_x_lo", [P, 3, T], F32R)
            prob = self.sb(c, "att_prob", [P, 2, T])
            flat_x = self.sb(c, "att_flat", [P, 2, T])
            a_hi = self.sb(c, "att_a_hi_t", [P, KT, HALF], F32R)
            a_lo = self.sb(c, "att_a_lo_t", [P, KT, HALF], F32R)
            nmax = self.sb(c, "att_nmax", [P, 2])
            z = self.sb(c, "att_z", [P, 2])
            zr = self.sb(c, "att_zr", [P, 2])
            o = self.sb(c, "att_o", [P, 2, HALF])
            flat = lambda t, s: t[:, s].rearrange("p k n -> p (k n)")
            with nc.Block() as block:
                @block.sync
                def _(sp):
                    with sp.Fori(0, HEADS) as h:
                        src = [sp.snap(h + TILE0[x]) for x in KINDS]
                        free = [sp.snap(h * 3 + (i + 1)) for i in range(3)]
                        to = sp.snap(h + 0)
                        ready = [sp.snap(h * 2 + (i + 1)) for i in range(2)]
                        for i in range(3):
                            sp.wait_ge(w_split, free[i])
                            sp.dma_start(raw[:, i], w[bass.ds(src[i], 1)].rearrange("o p n -> (o p) n")).then_inc(w_loaded[i], 16)
                        for half in range(2):
                            sp.wait_ge(out_copied, ready[half])
                            sp.dma_start(self.o_scr[bass.ds(to, 1), :, half * HALF:(half + 1) * HALF].rearrange("o p n -> (o p) n"),
                                         o[:, half]).then_inc(stored[half], 16)
                    for half in range(2):
                        sp.wait_ge(stored[half], 16 * (HEADS + 1))

                @block.scalar
                def _(act):
                    with act.Fori(0, HEADS) as h:
                        for i in range(3):
                            act.wait_ge(w_loaded[i], h * 16 + 16)
                            act.wait_ge(projected, h * 3 + 3)
                            act.activation(flat(w_hi, i), raw[:, i], ACT.Copy).then_inc(w_hi_done, 1)
                        for i in range(3):
                            act.wait_ge(projected, h * 3 + (i + 4))
                            if i == 2:
                                act.wait_ge(hi_done, h * 3 + 1)
                                act.wait_ge(operands, h * 3 + 1)
                            act.activation(flat_x[:, i % 2], acc[i % 2], ACT.Copy).then_inc(copied, 1)
                            if i >= 1:
                                j = i - 1
                                act.wait_ge(full, h * 6 + 3 * (j + 1))
                                act.activation(x_hi[:, j], flat_x[:, j], ACT.Copy).then_inc(hi_done, 1)
                        act.wait_ge(rotated, h * 3 + 3)
                        act.activation(x_hi[:, 2], turned, ACT.Copy).then_inc(hi_done, 1)

                        def exps(b):
                            for m in range(2):
                                act.wait_ge(negmax, h * 16 + (2 * b + m + 1))
                                if b:
                                    act.wait_ge(mixed, h * 8 + b)
                                act.activation(prob[:, m], acc[m], ACT.Exp, bias=nmax[:, m:m + 1], scale=1.0,
                                               accum_out=z[:, m:m + 1]).then_inc(exped, 1)

                        def turned_hi(b):
                            act.wait_ge(a_turned, h * 8 + (b + 1))
                            if b % 4 == 0:
                                act.wait_ge(out_summed, h * 2 + (b // 4 + 2))
                            act.activation(a_hi[:, :, (b % 4) * P:(b % 4 + 1) * P], turned.rearrange("p (k q) -> p k q", q=P),
                                           ACT.Copy).then_inc(a_hi_done, 1)
                            if b % 4 == 3:
                                half = b // 4
                                act.wait_ge(out_summed, h * 2 + (half + 3))
                                act.wait_ge(stored[half], h * 16 + 16)
                                act.activation(o[:, half], o_acc, ACT.Copy).then_inc(out_copied, 1)
                        for b in range(TB):
                            exps(b)
                            if b:
                                turned_hi(b - 1)
                        turned_hi(TB - 1)

                @block.vector
                def _(dve):
                    dve.sem_inc(w_split, 3)
                    with dve.Fori(0, HEADS) as h:
                        for i in range(3):
                            dve.wait_ge(w_hi_done, h * 3 + (i + 1))
                            dve.tensor_tensor(flat(w_lo, i), raw[:, i], flat(w_hi, i).bitcast(F32), ALU.subtract).then_inc(w_split, 1)
                        for i in range(2):
                            scale = 1.0 if i == 0 else SCALE
                            dve.wait_ge(rotated, h * 3 + (i + 1))
                            dve.scalar_tensor_tensor(prob[:, 0], turned, scale, self.sin[:], ALU.mult, ALU.mult).then_inc(full, 1)
                            dve.scalar_tensor_tensor(flat_x[:, i], flat_x[:, i], scale, self.cos[:], ALU.mult, ALU.mult).then_inc(full, 1)
                            dve.wait_ge(full, h * 6 + (3 * i + 2))
                            dve.tensor_tensor(flat_x[:, i], flat_x[:, i], prob[:, 0], ALU.add).then_inc(full, 1)
                            dve.wait_ge(full, h * 6 + (3 * i + 3))
                            dve.wait_ge(hi_done, h * 3 + (i + 1))
                            dve.tensor_tensor(x_lo[:, i], flat_x[:, i], x_hi[:, i].bitcast(F32), ALU.subtract).then_inc(operands, 1)
                        dve.wait_ge(hi_done, h * 3 + 3)
                        dve.tensor_tensor(x_lo[:, 2], turned, x_hi[:, 2].bitcast(F32), ALU.subtract).then_inc(operands, 1)

                        def maxima(b):
                            for m in range(2):
                                dve.wait_ge(scored, h * 16 + (2 * b + m + 1))
                                if b:
                                    dve.wait_ge(exped, h * 16 + 2 * (b - 1) + (m + 1))
                                dve.tensor_reduce(nmax[:, m:m + 1], acc[m], AXX, ALU.max, negate=True).then_inc(negmax, 1)

                        def combine(b):
                            dve.wait_ge(exped, h * 16 + (2 * b + 2))
                            dve.reciprocal(zr[:], z[:]).then_inc(mixing, 1)
                            dve.wait_ge(mixing, h * 24 + (3 * b + 1))
                            dve.tensor_scalar(zr[:, 1:2], zr[:, 1:2], self.lam[:, 0:1], None, ALU.mult).then_inc(mixing, 1)
                            dve.wait_ge(mixing, h * 24 + (3 * b + 2))
                            dve.tensor_scalar(prob[:, 1], prob[:, 1], zr[:, 1:2], None, ALU.mult).then_inc(mixing, 1)
                            dve.wait_ge(mixing, h * 24 + (3 * b + 3))
                            if b >= 2:
                                dve.wait_ge(a_turned, h * 8 + (b - 1))
                            dve.scalar_tensor_tensor(flat_x[:, b % 2], prob[:, 0], zr[:, 0:1], prob[:, 1], ALU.mult, ALU.subtract)\
                               .then_inc(mixed, 1)

                        def turned_lo(b):
                            dve.wait_ge(a_hi_done, h * 8 + (b + 1))
                            cols = slice((b % 4) * P, (b % 4 + 1) * P)
                            dve.tensor_tensor(a_lo[:, :, cols], turned.rearrange("p (k q) -> p k q", q=P),
                                              a_hi[:, :, cols].bitcast(F32), ALU.subtract).then_inc(a_split, 1)
                        maxima(0)
                        for b in range(TB):
                            combine(b)
                            if b + 1 < TB:
                                maxima(b + 1)
                            turned_lo(b)

                @block.tensor
                def _(pe):
                    pe.sem_inc(projected, 3)
                    pe.sem_inc(out_summed, 2)
                    for half in range(2):
                        pe.sem_inc(stored[half], 16)
                    with pe.Fori(0, HEADS) as h:
                        def project(i):
                            pe.wait_ge(w_split, h * 3 + (i + 4))
                            if i == 2:
                                pe.wait_ge(copied, h * 3 + 1)
                            for half in range(2):
                                t = slice(half * HALF, (half + 1) * HALF)
                                for k in range(KT):
                                    last = self.product3(pe, ps[:, 2 * (i % 2) + half], w_hi[:, i, k], w_lo[:, i, k],
                                                         h_hi[:, k, t], h_lo[:, k, t], k == 0, k == KT - 1)
                            last.then_inc(projected, 1)

                        def rotate(i):
                            pe.wait_ge(copied, h * 3 + (i + 1))
                            if i == 1:
                                pe.wait_ge(full, h * 6 + 3)
                            for half in range(2):
                                last = pe.matmul(ps[:, 4 + half], self.rotate[:], flat_x[:, i, half * HALF:(half + 1) * HALF],
                                                 start=True, stop=True)
                            last.then_inc(rotated, 1)
                        project(0)
                        project(1)
                        rotate(0)
                        project(2)
                        rotate(1)
                        pe.wait_ge(copied, h * 3 + 3)
                        pe.wait_ge(full, h * 6 + 6)
                        for k in range(TB):
                            last = pe.transpose(turned[:, k * P:(k + 1) * P], flat_x[:, 0, k * P:(k + 1) * P], self.ident[:])
                        last.then_inc(rotated, 1)

                        def scores(b):
                            for m in range(2):
                                rows = slice(m * MAP_DIM, (m + 1) * MAP_DIM)
                                q = slice(b * P, (b + 1) * P)
                                if b:
                                    pe.wait_ge(exped, h * 16 + (2 * b + m - 1))
                                for half in range(2):
                                    k = slice(half * HALF, (half + 1) * HALF)
                                    last = self.product3(pe, ps[:, 2 * m + half], x_hi[rows, 1, q], x_lo[rows, 1, q],
                                                         x_hi[rows, 0, k], x_lo[rows, 0, k], True, True)
                                last.then_inc(scored, 1)

                        def turn(b):
                            pe.wait_ge(mixed, h * 8 + (b + 1))
                            if b:
                                pe.wait_ge(a_split, h * 8 + b)
                            for k in range(TB):
                                last = pe.transpose(turned[:, k * P:(k + 1) * P], flat_x[:, b % 2, k * P:(k + 1) * P], self.ident[:])
                            last.then_inc(a_turned, 1)

                        def times_v(half):
                            pe.wait_ge(a_split, h * 8 + 4 * (half + 1))
                            if half:
                                pe.wait_ge(out_copied, h * 2 + 1)
                            for k in range(TB):
                                last = self.product3(pe, o_acc, x_hi[:, 2, k * P:(k + 1) * P], x_lo[:, 2, k * P:(k + 1) * P],
                                                     a_hi[:, k], a_lo[:, k], k == 0, k == TB - 1)
                            last.then_inc(out_summed, 1)
                        pe.wait_ge(operands, h * 3 + 2)
                        scores(0)
                        pe.wait_ge(operands, h * 3 + 3)
                        for b in range(TB):
                            if b + 1 < TB:
                                scores(b + 1)
                            turn(b)
                            if b % 4 == 3:
                                times_v(b // 4)

    def to_scratch(self, name, first, tiles, func, dst, h_hi, h_lo):
        stored = [self.sem(f"{name}_stored{i}") for i in range(2)]
        with ExitStack() as c:
            buf = self.sb(c, f"{name}_buf", [P, 2, T])

            def act_out(act, j, s, acc, emptied):
                act.wait_ge(stored[s], j * 8 + (16 - 8 * s))
                act.activation(buf[:, s], acc, func).then_inc(emptied, 1)
                act.wait_ge(emptied, j + 3)
                act.dma_start(dst[bass.ds(j, 1)].rearrange("o p t -> (o p) t"), buf[:, s]).then_inc(stored[s], 16)
            with self.nc.Block() as block:
                @block.tensor
                def _(pe):
                    for s in range(2):
                        pe.sem_inc(stored[s], 16)
            self.projection(name, self.a["w_in"], first, h_hi, h_lo, tiles, act_out=act_out)
            with self.nc.Block() as block:
                @block.sync
                def _(sp):
                    for s in range(2):
                        sp.wait_ge(stored[s], 16 * (tiles // 2 + 1))

    def gates(self, h_hi, h_lo):
        self.to_scratch("gates", GA0, 2 * KT, ACT.Sigmoid, self.gate_scr, h_hi, h_lo)

    def gmlp(self, h_hi, h_lo):
        nc, a, ps = self.nc, self.a, self.psum
        self.to_scratch("zu", ZU0, KT, ACT.Gelu_apprx_tanh, self.u_scr, h_hi, h_lo)
        with ExitStack() as c:
            zv = self.sb(c, "zv", [P, KT, T])

            def act_out(act, j, s, acc, emptied):
                act.activation(zv[:, bass.ds(j, 1)].rearrange("p o t -> p (o t)"), acc, ACT.Gelu_apprx_tanh).then_inc(emptied, 1)
            self.projection("zv", a["w_in"], ZV0, h_hi, h_lo, KT, act_out=act_out)
            rstd = self.sb(c, "zv_rstd_t", [P, T])
            mean_done = self.sem("zv_mean")
            centred = self.sem("zv_centred")
            with nc.Block() as block:
                @block.tensor
                def _(pe):
                    for k in range(KT):
                        for half in range(2):
                            last = pe.matmul(ps[:, half], self.ones_mean[:], zv[:, k, half * HALF:(half + 1) * HALF],
                                             start=(k == 0), stop=(k == KT - 1))
                    last.then_inc(mean_done, 1)

                @block.vector
                def _(dve):
                    dve.wait_ge(mean_done, 1)
                    for k in range(KT):
                        dve.tensor_tensor(zv[:, k], zv[:, k], ps[:, 0:2].rearrange("p b t -> p (b t)"), ALU.subtract).then_inc(centred, 1)
            with ExitStack() as s:
                self.mean_square("zv", zv, rstd, self.ones_mean, self.sb(s, "zv_sq", [P, 2, T]))
            self.spatial(zv, rstd)

    def spatial(self, zv, rstd):
        nc, a, ps = self.nc, self.a, self.psum
        G = KT
        turned = ps[:, 0:2].rearrange("p b t -> p (b t)")
        sv = ps[:, 2:4].rearrange("p b t -> p (b t)")
        tables = self.sem("spatial_tables")
        u_loaded = self.sem("spatial_u_loaded")
        w_hi_done = self.sem("spatial_w_hi")
        w_split = self.sem("spatial_w_split")
        normed = self.sem("spatial_normed")
        v_turned = self.sem("spatial_turned")
        v_hi_done = self.sem("spatial_v_hi")
        v_split = self.sem("spatial_v_split")
        mixed = self.sem("spatial_mixed")
        gated = self.sem("spatial_gated")
        stored = self.sem("spatial_stored")
        ln_g, ln_b = self.vecs[:, 4 * KT:5 * KT], self.vecs[:, 5 * KT:6 * KT]
        with ExitStack() as c:
            w = self.sb(c, "sp_w", [P, G, P])
            w_hi = self.sb(c, "sp_w_hi", [P, G, P], F32R)
            w_lo = self.sb(c, "sp_w_lo", [P, G, P], F32R)
            bias = self.sb(c, "sp_bias", [P, G, P])
            u = self.sb(c, "sp_u", [P, T])
            v = self.sb(c, "sp_v", [P, T])
            v_hi = self.sb(c, "sp_v_hi", [P, T], F32R)
            v_lo = self.sb(c, "sp_v_lo", [P, T], F32R)
            sg = self.sb(c, "sp_sg", [P, T])
            with nc.Block() as block:
                @block.sync
                def _(sp):
                    sp.dma_start(w[:].rearrange("q g p -> q (g p)"), a["w_spatial"]).then_inc(tables, 16)
                    sp.dma_start(bias[:].rearrange("q g p -> q (g p)"), a["b_spatial"].to_broadcast([P, G * P])).then_inc(tables, 16)
                    with sp.Fori(0, G) as g:
                        at = sp.snap(g + 0)
                        free = sp.snap(g * 2 + 1)
                        ready = sp.snap(g * 2 + 3)
                        sp.wait_ge(gated, free)
                        sp.dma_start(u[:], self.u_scr[bass.ds(at, 1)].rearrange("o p t -> (o p) t")).then_inc(u_loaded, 16)
                        sp.wait_ge(gated, ready)
                        sp.dma_start(self.sg_scr[bass.ds(at, 1)].rearrange("o p t -> (o p) t"), sg[:]).then_inc(stored, 16)
                    sp.wait_ge(stored, 16 * (G + 1))

                @block.scalar
                def _(act):
                    act.wait_ge(tables, 32)
                    act.activation(w_hi[:], w[:], ACT.Copy).then_inc(w_hi_done, 1)
                    with act.Fori(0, G) as g:
                        act.wait_ge(v_turned, g + 1)
                        act.wait_ge(mixed, g + 1)
                        act.activation(v_hi[:], turned, ACT.Copy).then_inc(v_hi_done, 1)

                @block.vector
                def _(dve):
                    dve.sem_inc(gated, 1)
                    dve.wait_ge(w_hi_done, 1)
                    dve.tensor_tensor(w_lo[:], w[:], w_hi[:].bitcast(F32), ALU.subtract).then_inc(w_split, 1)
                    with dve.Fori(0, G) as g:
                        dve.tensor_tensor(v[:], zv[:, bass.ds(g, 1)].rearrange("p o t -> p (o t)"), rstd[:], ALU.mult).then_inc(normed, 1)
                        dve.wait_ge(normed, g * 2 + 1)
                        dve.tensor_scalar(v[:], v[:], ln_g[:, bass.ds(g, 1)], ln_b[:, bass.ds(g, 1)], ALU.mult, ALU.add).then_inc(normed, 1)
                        dve.wait_ge(v_hi_done, g + 1)
                        dve.tensor_tensor(v_lo[:], turned, v_hi[:].bitcast(F32), ALU.subtract).then_inc(v_split, 1)
                        dve.wait_ge(mixed, g + 2)
                        dve.wait_ge(stored, g * 16 + 16)
                        dve.tensor_tensor(sg[:].rearrange("h (c p) -> h c p", p=P), sv.rearrange("h (c p) -> h c p", p=P),
                                          bias[:, bass.ds(g, 1)].to_broadcast([P, TB, P]), ALU.add).then_inc(gated, 1)
                        dve.wait_ge(gated, g * 2 + 2)
                        dve.wait_ge(u_loaded, g * 16 + 16)
                        dve.tensor_tensor(sg[:], sg[:], u[:], ALU.mult).then_inc(gated, 1)

                @block.tensor
                def _(pe):
                    pe.sem_inc(mixed, 1)
                    pe.sem_inc(stored, 16)
                    pe.wait_ge(w_split, 1)
                    with pe.Fori(0, G) as g:
                        pe.wait_ge(normed, g * 2 + 2)
                        for k in range(TB):
                            last = pe.transpose(turned[:, k * P:(k + 1) * P], v[:, k * P:(k + 1) * P], self.ident[:])
                        last.then_inc(v_turned, 1)
                        pe.wait_ge(v_split, g + 1)
                        for k in range(TB):
                            cols = slice(k * P, (k + 1) * P)
                            wh = w_hi[:, bass.ds(g, 1)].rearrange("q o p -> q (o p)")
                            wl = w_lo[:, bass.ds(g, 1)].rearrange("q o p -> q (o p)")
                            pe.matmul(sv[:, cols], v_hi[:, cols], wh, start=True, stop=False)
                            pe.matmul(sv[:, cols], v_hi[:, cols], wl, start=False, stop=False)
                            last = pe.matmul(sv[:, cols], v_lo[:, cols], wh, start=False, stop=True)
                        last.then_inc(mixed, 1)

    def split(self, name, src, hi, lo):
        hi_done = self.sem(f"{name}_split_hi")
        lo_done = self.sem(f"{name}_split_lo")
        with self.nc.Block() as block:
            @block.scalar
            def _(act):
                for k in range(KT):
                    act.activation(hi[:, k], src[:, k], ACT.Copy).then_inc(hi_done, 1)

            @block.vector
            def _(dve):
                for k in range(KT):
                    dve.wait_ge(hi_done, k + 1)
                    dve.tensor_tensor(lo[:, k], src[:, k], hi[:, k].bitcast(F32), ALU.subtract).then_inc(lo_done, 1)

    def branches(self, wide, m_hi, m_lo):
        with ExitStack() as c:
            with ExitStack() as s:
                o = self.sb(s, "o_all", [P, HEADS, T])
                self.load(o, self.o_scr.rearrange("h p t -> p h t"), "o")
                self.head_norm(o)
                self.split("o", o, m_hi, m_lo)
            self.branch("attn", "w_attn", 0, wide, m_hi, m_lo)
            sg = self.sb(c, "sg_all", [P, KT, T])
            self.load(sg, self.sg_scr.rearrange("h p t -> p h t"), "sg")
            self.split("sg", sg, m_hi, m_lo)
            self.branch("spat", "w_gmlp", KT, wide, m_hi, m_lo)
            self.split("mix", wide, m_hi, m_lo)

    def head_norm(self, o):
        nc, ps = self.nc, self.psum
        squared = self.sem("head_squared")
        summed = self.sem("head_summed")
        eps_added = self.sem("head_eps")
        rooted = self.sem("head_rooted")
        inverse = self.sem("head_inverse")
        normed = self.sem("head_normed")
        with ExitStack() as c:
            sq = self.sb(c, "head_sq", [P, 2, T])
            rstd = self.sb(c, "head_rstd", [P, 2, T])
            with nc.Block() as block:
                @block.scalar
                def _(act):
                    def square(h):
                        if h >= 2:
                            act.wait_ge(summed, h - 1)
                        act.activation(sq[:, h % 2], o[:, h], ACT.Square).then_inc(squared, 1)
                    square(0)
                    for h in range(HEADS):
                        if h + 1 < HEADS:
                            square(h + 1)
                        act.wait_ge(eps_added, h + 1)
                        act.activation(rstd[:, h % 2], rstd[:, h % 2], ACT.Sqrt).then_inc(rooted, 1)

                @block.tensor
                def _(pe):
                    for h in range(HEADS):
                        pe.wait_ge(squared, h + 1)
                        if h >= 2:
                            pe.wait_ge(eps_added, h - 1)
                        for half in range(2):
                            last = pe.matmul(ps[:, 2 * (h % 2) + half], self.ones_head[:], sq[:, h % 2, half * HALF:(half + 1) * HALF],
                                             start=True, stop=True)
                        last.then_inc(summed, 1)

                @block.vector
                def _(dve):
                    def add_eps(h):
                        dve.wait_ge(summed, h + 1)
                        if h >= 2:
                            dve.wait_ge(normed, 2 * (h - 1))
                        dve.tensor_scalar(rstd[:, h % 2], ps[:, 2 * (h % 2):2 * (h % 2) + 2].rearrange("p b t -> p (b t)"),
                                          EPS, None, ALU.add).then_inc(eps_added, 1)
                    add_eps(0)
                    for h in range(HEADS):
                        if h + 1 < HEADS:
                            add_eps(h + 1)
                        dve.wait_ge(rooted, h + 1)
                        dve.reciprocal(rstd[:, h % 2], rstd[:, h % 2]).then_inc(inverse, 1)
                        dve.wait_ge(inverse, h + 1)
                        dve.tensor_tensor(o[:, h], o[:, h], rstd[:, h % 2], ALU.mult).then_inc(normed, 1)
                        dve.wait_ge(normed, 2 * h + 1)
                        dve.tensor_scalar(o[:, h], o[:, h], self.subln_gain[:, 0:1], None, ALU.mult).then_inc(normed, 1)

    def branch(self, name, weights, gate0, wide, x_hi, x_lo):
        g_loaded = [self.sem(f"{name}_gate_loaded{i}") for i in range(2)]
        gated = self.sem(f"{name}_gated")
        with ExitStack() as c:
            gate = self.sb(c, f"{name}_gate", [P, 2, T])
            term = self.sb(c, f"{name}_term", [P, 2, T])

            def dve_out(dve, j, s, acc, emptied):
                dve.wait_ge(g_loaded[s], j * 8 + (16 - 8 * s))
                to = wide[:, bass.ds(j, 1)].rearrange("p o t -> p (o t)")
                if gate0 == 0:
                    dve.tensor_tensor(to, acc, gate[:, s], ALU.mult).then_inc(emptied, 1)
                else:
                    dve.tensor_tensor(term[:, s], acc, gate[:, s], ALU.mult).then_inc(emptied, 1)
                    dve.wait_ge(emptied, j + 3)
                    dve.tensor_tensor(to, to, term[:, s], ALU.add).then_inc(gated, 1)

            def pool_program(pool, emptied):
                with pool.Fori(0, KT // 2) as it:
                    at = [pool.snap(it * 2 + (s + gate0)) for s in range(2)]
                    for s in range(2):
                        pool.wait_ge(emptied, it * 2 + (s + 1))
                        pool.dma_start(gate[:, s], self.gate_scr[bass.ds(at[s], 1)].rearrange("o p t -> (o p) t")).then_inc(g_loaded[s], 16)
            self.projection(name, self.a[weights], 0, x_hi, x_lo, KT, dve_out=dve_out, pool_program=pool_program)

    def out_projection(self, wide, m_hi, m_lo):
        def act_out(act, j, s, acc, emptied):
            act.activation(wide[:, bass.ds(j, 1)].rearrange("p o t -> p (o t)"), acc, ACT.Copy).then_inc(emptied, 1)
        self.projection("out", self.a["w_out"], 0, m_hi, m_lo, KT, act_out=act_out)

    def add_normed(self, name, y, coef, base_dram, x1, dst_dram):
        nc = self.nc
        loaded = self.sem(f"{name}_base_loaded")
        scaled = self.sem(f"{name}_scaled")
        added = self.sem(f"{name}_added")
        stored = self.sem(f"{name}_stored")
        with ExitStack() as c:
            rstd = self.sb(c, f"{name}_rstd_t", [P, T])
            sq = self.sb(c, f"{name}_sq", [P, 2, T])
            self.mean_square(name, y, rstd, self.ones_mean, sq)
            with nc.Block() as block:
                @block.sync
                def _(sp):
                    sp.dma_start(x1[:], base_dram).then_inc(loaded, 16)
                    for k in range(KT):
                        sp.wait_ge(added, k + 1)
                        sp.dma_start(dst_dram[:, k], x1[:, k]).then_inc(stored, 16)
                    sp.wait_ge(stored, 16 * KT)

                @block.vector
                def _(dve):
                    for k in range(KT):
                        dve.tensor_tensor(y[:, k], y[:, k], rstd[:], ALU.mult).then_inc(scaled, 1)
                    dve.wait_ge(loaded, 16)
                    for k in range(KT):
                        dve.wait_ge(scaled, k + 1)
                        dve.scalar_tensor_tensor(x1[:, k], y[:, k], coef[:, k:k + 1], x1[:, k], ALU.mult, ALU.add).then_inc(added, 1)

    def residual(self, wide, x1):
        self.add_normed("mix", wide, self.coef[:, KT:2 * KT], self.a["xT"].rearrange("(k p) t -> p k t", p=P), x1,
                        self.x1_scr.rearrange("k p t -> p k t"))

    def finish(self, wide):
        with ExitStack() as c:
            x1 = self.sb(c, "x_out", [P, KT, T])
            self.add_normed("final", wide, self.coef[:, 3 * KT:4 * KT], self.x1_scr.rearrange("k p t -> p k t"), x1,
                            self.a["out"].rearrange("(k p) t -> p k t", p=P))

    def route(self, h2_hi, h2_lo):
        with ExitStack() as c:
            vals = self.sb(c, "top_vals", [P, TB, SIDES, TOPK])
            idxs = self.sb(c, "top_idxs", [P, TB, SIDES, TOPK])
            self.side_tops(h2_hi, h2_lo, vals, idxs)
            self.stage_end()
            self.scatter_weights(vals, idxs)
            self.stage_end()

    def side_tops(self, h2_hi, h2_lo, vals, idxs):
        nc, a, ps = self.nc, self.a, self.psum
        keys_loaded = self.sem("keys_loaded")
        keys_hi_done = self.sem("keys_hi")
        keys_split = self.sem("keys_split")
        q_hi_done = self.sem("rq_hi")
        q_split = self.sem("rq_emptied_too")
        scored = self.sem("rq_scored")
        tops = self.sem("rq_tops")
        held = self.sem("rq_held")
        NTOPS = 5 * TB + 2
        with ExitStack() as c:
            k_raw = self.sb(c, "k_raw", [P, SIDES, KEYS])
            k_hi = self.sb(c, "k_hi", [P, SIDES, KEYS], F32R)
            k_lo = self.sb(c, "k_lo", [P, SIDES, KEYS], F32R)
            with nc.Block() as block:
                @block.sync
                def _(sp):
                    sp.dma_start(k_raw[:].rearrange("d s n -> d (s n)"), a["keysT"]).then_inc(keys_loaded, 16)

                @block.scalar
                def _(act):
                    act.wait_ge(keys_loaded, 16)
                    act.activation(k_hi[:], k_raw[:], ACT.Copy).then_inc(keys_hi_done, 1)

                @block.vector
                def _(dve):
                    dve.wait_ge(keys_hi_done, 1)
                    dve.tensor_tensor(k_lo[:], k_raw[:], k_hi[:].bitcast(F32), ALU.subtract).then_inc(keys_split, 1)
            q_hi = self.sb(c, "rq_hi_t", [P, 2, T], F32R)
            q_lo = self.sb(c, "rq_lo_t", [P, 2, T], F32R)
            work = self.sb(c, "rq_work", [P, TB, KEYS])
            top_v = self.sb(c, "rq_top_v", [P, TB, TOPK])
            top_i = self.sb(c, "rq_top_i", [P, TB, TOPK], U32)
            score = [ps[:, 4 + 2 * s:6 + 2 * s].rearrange("p b (c n) -> p (b c) n", n=KEYS) for s in range(2)]

            def act_out(act, j, s, acc, emptied):
                act.wait_ge(scored, j + 1)
                act.activation(q_hi[:, s], acc, ACT.Copy).then_inc(q_hi_done, 1)

            def dve_out(dve, j, s, acc, emptied):
                dve.wait_ge(q_hi_done, j + 1)
                dve.tensor_tensor(q_lo[:, s], acc, q_hi[:, s].bitcast(F32), ALU.subtract).then_inc(emptied, 1)

            def top(dve, j, s):
                n = [0]

                def all_so_far():
                    dve.wait_ge(tops, j * NTOPS + (n[0] + 2 * NTOPS))
                    dve.sem_inc(held, 1)

                def done(ins):
                    ins.then_inc(tops, 1)
                    n[0] += 1
                dve.wait_ge(scored, j + 3)
                all_so_far()
                for b in range(TB):
                    done(dve.max(top_v[:, b, 0:8], score[s][:, b]))
                all_so_far()
                for b in range(TB):
                    done(dve.match_replace(work[:, b], top_v[:, b, 0:8], score[s][:, b], LOWEST))
                for b in range(TB):
                    done(dve.max_index(top_i[:, b, 0:8], top_v[:, b, 0:8], score[s][:, b]))
                all_so_far()
                for b in range(TB):
                    done(dve.max(top_v[:, b, 8:16], work[:, b]))
                all_so_far()
                for b in range(TB):
                    done(dve.max_index(top_i[:, b, 8:16], top_v[:, b, 8:16], work[:, b]))
                all_so_far()
                done(dve.tensor_copy(vals[:, :, bass.ds(j, 1)].rearrange("p b o k -> p b (o k)"), top_v[:]))
                done(dve.tensor_copy(idxs[:, :, bass.ds(j, 1)].rearrange("p b o k -> p b (o k)"), top_i[:]))
                assert n[0] == NTOPS

            def pe_after(pe, j, s, emptied):
                pe.wait_ge(emptied, j + 3)
                pe.wait_ge(tops, j * NTOPS + NTOPS)
                kh = k_hi[:, bass.ds(j, 1)].rearrange("d o n -> d (o n)")
                kl = k_lo[:, bass.ds(j, 1)].rearrange("d o n -> d (o n)")
                for b in range(TB):
                    q = slice(b * P, (b + 1) * P)
                    pe.matmul(score[s][:, b], q_hi[:, s, q], kh, start=True, stop=False)
                    pe.matmul(score[s][:, b], q_hi[:, s, q], kl, start=False, stop=False)
                    last = pe.matmul(score[s][:, b], q_lo[:, s, q], kh, start=False, stop=True)
                last.then_inc(scored, 1)
            with nc.Block() as block:
                @block.vector
                def _(dve):
                    dve.sem_inc(tops, 2 * NTOPS)
                    dve.sem_inc(scored, 2)
            self.projection("rq", a["w_peer"], 0, h2_hi, h2_lo, SIDES, act_out=act_out, dve_out=dve_out,
                            pe_after=pe_after, dve_after=top)

    def scatter_weights(self, vals, idxs):
        nc, ps = self.nc, self.psum
        SEL = HEADS * TOPK
        RING, QUAD = 8, 4
        QUADS = P // QUAD
        chain = self.sem("sc_chain")
        exp_in = self.sem("sc_exp_in")
        exp_out = self.sem("sc_exp_out")
        chosen = self.sem("sc_chosen")
        turned = self.sem("sc_turned")
        rows_ready = self.sem("sc_rows")
        onehots = self.sem("sc_onehots")
        matrices = self.sem("sc_matrices")
        staged = self.sem("sc_staged")
        stored = self.sem("sc_stored")
        iotas = self.sem("sc_iotas")
        held = self.sem("sc_held")
        with ExitStack() as c:
            vt = self.sb(c, "sc_vt", [P, HEADS, 2, TOPK])
            it_ = self.sb(c, "sc_it", [P, HEADS, 2, TOPK])
            cand = self.sb(c, "sc_cand", [P, HEADS, TOPK, TOPK])
            cand2 = self.sb(c, "sc_cand2", [P, HEADS, TOPK * TOPK])
            best = self.sb(c, "sc_best", [P, HEADS, TOPK])
            pos = self.sb(c, "sc_pos", [P, HEADS, TOPK], U32)
            pos_i = self.sb(c, "sc_pos_i", [P, 2, SEL], U32)
            pos_f = self.sb(c, "sc_pos_f", [P, 2, SEL])
            norm = self.sb(c, "sc_norm", [P, 2, HEADS])
            picks = self.sb(c, "sc_picks", [P, 3, SEL])
            rows = self.sb(c, "sc_rows_t", [SEL, 3, P])
            iota16 = self.sb(c, "sc_iota16", [P, TOPK])
            iota128 = self.sb(c, "sc_iota128", [P, KEYS])
            first = self.sb(c, "sc_first", [SEL, RING, KEYS])
            second = self.sb(c, "sc_second", [SEL, RING, KEYS])
            stage = self.sb(c, "sc_stage", [P, KEYS, P])
            with nc.Block() as block:
                @block.gpsimd
                def _(pool):
                    pool.iota(iota16[:], [[1, TOPK]], base=0, channel_multiplier=0, allow_small_or_imprecise_dtypes=True).then_inc(iotas, 1)
                    pool.iota(iota128[:], [[1, KEYS]], base=0, channel_multiplier=0, allow_small_or_imprecise_dtypes=True).then_inc(iotas, 1)

                @block.sync
                def _(sp):
                    dst = self.route_scr.rearrange("i j (b t) -> b j i t", t=P)
                    with sp.Fori(0, TB) as b:
                        at = sp.snap(b + 0)
                        ready = sp.snap(b * QUADS + (QUADS + 4))
                        sp.wait_ge(staged, ready)
                        sp.dma_start(dst[bass.ds(at, 1)].rearrange("o j i t -> (o j) i t"), stage[:]).then_inc(stored, 16)
                    sp.wait_ge(stored, 16 * (TB + 1))

                @block.vector
                def _(dve):
                    dve.sem_inc(stored, 16)
                    dve.sem_inc(chain, 1)
                    dve.wait_ge(iotas, 2)
                    LINKS = 54
                    with dve.Fori(0, TB) as b:
                        n = [0]

                        def do(ins):
                            n[0] += 1
                            ins.then_inc(chain, 1)

                        def all_so_far():
                            dve.wait_ge(chain, b * LINKS + (n[0] + 1))
                            dve.sem_inc(held, 1)
                        all_so_far()
                        do(dve.tensor_copy(vt[:].rearrange("p h s k -> p (h s k)"), vals[:, bass.ds(b, 1)].rearrange("p o s k -> p (o s k)")))
                        do(dve.tensor_copy(it_[:].rearrange("p h s k -> p (h s k)"), idxs[:, bass.ds(b, 1)].rearrange("p o s k -> p (o s k)")))
                        all_so_far()
                        shape = [P, HEADS, TOPK, TOPK]
                        do(dve.tensor_tensor(cand[:], vt[:, :, 0].unsqueeze(3).to_broadcast(shape), vt[:, :, 1].unsqueeze(2).to_broadcast(shape), ALU.add))
                        all_so_far()
                        flat = [cand[:, h].rearrange("p a b -> p (a b)") for h in range(HEADS)]
                        for h in range(HEADS):
                            do(dve.max(best[:, h, 0:8], flat[h]))
                        all_so_far()
                        for h in range(HEADS):
                            do(dve.match_replace(cand2[:, h], best[:, h, 0:8], flat[h], LOWEST))
                        for h in range(HEADS):
                            do(dve.max_index(pos[:, h, 0:8], best[:, h, 0:8], flat[h]))
                        all_so_far()
                        for h in range(HEADS):
                            do(dve.max(best[:, h, 8:16], cand2[:, h]))
                        all_so_far()
                        for h in range(HEADS):
                            do(dve.max_index(pos[:, h, 8:16], best[:, h, 8:16], cand2[:, h]))
                        weight = picks[:, 2].rearrange("p (h k) -> p h k", k=TOPK)
                        dve.tensor_tensor(weight, best[:], best[:, :, 0:1].to_broadcast([P, HEADS, TOPK]), ALU.subtract).then_inc(exp_in, 1)
                        all_so_far()
                        pflat = pos[:].rearrange("p h k -> p (h k)")
                        do(dve.tensor_single_scalar(pos_i[:, 0], pflat, 4, ALU.logical_shift_right))
                        do(dve.tensor_single_scalar(pos_i[:, 1], pflat, 15, ALU.bitwise_and))
                        all_so_far()
                        do(dve.tensor_copy(pos_f[:], pos_i[:]))
                        all_so_far()
                        eq = cand2[:].rearrange("p h (k a) -> p (h k) a", a=TOPK)
                        eq4 = cand2[:].rearrange("p h (k a) -> p h k a", a=TOPK)
                        for side in range(2):
                            do(dve.tensor_tensor(eq, pos_f[:, side].unsqueeze(2).to_broadcast([P, SEL, TOPK]),
                                                 iota16[:].unsqueeze(1).to_broadcast([P, SEL, TOPK]), ALU.is_equal))
                            all_so_far()
                            do(dve.tensor_tensor(cand[:], eq4, it_[:, :, side].unsqueeze(2).to_broadcast(shape), ALU.mult))
                            all_so_far()
                            do(dve.tensor_reduce(picks[:, side], cand[:].rearrange("p h k a -> p (h k) a"), AXX, ALU.add))
                        dve.wait_ge(exp_out, b + 1)
                        do(dve.tensor_reduce(norm[:, 0], weight, AXX, ALU.add))
                        all_so_far()
                        do(dve.reciprocal(norm[:, 1], norm[:, 0]))
                        all_so_far()
                        dve.tensor_tensor(weight, weight, norm[:, 1].unsqueeze(2).to_broadcast([P, HEADS, TOPK]), ALU.mult).then_inc(chosen, 1)
                        dve.wait_ge(turned, b + 1)
                        dve.tensor_copy(rows[:].rearrange("k a t -> k (a t)"), ps[:, 0, 0:3 * P]).then_inc(rows_ready, 1)
                        dve.wait_ge(rows_ready, b + 1)
                        for q in range(QUADS):
                            dve.wait_ge(matrices, b * QUADS + (q + 1))
                            for t in range(q * QUAD, (q + 1) * QUAD):
                                dve.tensor_scalar(first[:, t % RING], iota128[:], rows[:, 0, t:t + 1], rows[:, 2, t:t + 1], ALU.is_equal, ALU.mult)
                                last = dve.tensor_scalar(second[:, t % RING], iota128[:], rows[:, 1, t:t + 1], None, ALU.is_equal)
                            last.then_inc(onehots, 1)
                        assert n[0] == LINKS, n[0]

                @block.scalar
                def _(act):
                    with act.Fori(0, TB) as b:
                        weight = picks[:, 2]
                        act.wait_ge(exp_in, b + 1)
                        act.activation(weight, weight, ACT.Exp).then_inc(exp_out, 1)
                        act.wait_ge(stored, b * 16 + 16)
                        for q in range(QUADS):
                            act.wait_ge(matrices, b * QUADS + (q + 3))
                            act.activation(stage[:, :, q * QUAD:(q + 1) * QUAD].rearrange("j i t -> j t i"),
                                           ps[:, 4 + q % 4].rearrange("j (t i) -> j t i", i=KEYS), ACT.Copy).then_inc(staged, 1)

                @block.tensor
                def _(pe):
                    pe.sem_inc(matrices, 2)
                    pe.sem_inc(staged, 4)
                    with pe.Fori(0, TB) as b:
                        pe.wait_ge(chosen, b + 1)
                        for i in range(3):
                            last = pe.transpose(ps[:, 0, i * P:(i + 1) * P], picks[:, i], self.ident[:])
                        last.then_inc(turned, 1)
                        for q in range(QUADS):
                            pe.wait_ge(onehots, b * QUADS + (q + 1))
                            pe.wait_ge(staged, b * QUADS + (q + 1))
                            for t in range(QUAD):
                                slot = (q * QUAD + t) % RING
                                last = pe.matmul(ps[:, 4 + q % 4, t * KEYS:(t + 1) * KEYS], second[:, slot], first[:, slot], start=True, stop=True)
                            last.then_inc(matrices, 1)

    def experts(self, h2_hi, h2_lo, y):
        nc, a, ps = self.nc, self.a, self.psum
        C = KEYS
        u_loaded = [self.sem(f"ex_u_loaded{i}") for i in range(2)]
        v_loaded = [self.sem(f"ex_v_loaded{i}") for i in range(2)]
        g_loaded = [self.sem(f"ex_g_loaded{i}") for i in range(2)]
        u_hi_done = self.sem("ex_u_hi")
        u_split = self.sem("ex_u_split")
        v_hi_done = self.sem("ex_v_hi")
        v_split = self.sem("ex_v_split")
        hidden = self.sem("ex_hidden")
        gelu_done = self.sem("ex_gelu")
        weighted = self.sem("ex_weighted")
        a_hi_done = self.sem("ex_a_hi")
        a_split = self.sem("ex_a_split")
        summed = self.sem("ex_summed")
        added = self.sem("ex_added")
        zeroed = self.sem("ex_zeroed")
        TILES = 2 * KT
        hid = [ps[:, 2 * s:2 * s + 2].rearrange("p b t -> p (b t)") for s in range(2)]
        with ExitStack() as c:
            u_raw = self.sb(c, "u_raw", [P, 2, D])
            u_hi = self.sb(c, "u_hi", [P, 2, KT, P], F32R)
            u_lo = self.sb(c, "u_lo", [P, 2, KT, P], F32R)
            v_raw = self.sb(c, "v_raw", [P, 2, D])
            v_hi = self.sb(c, "v_hi", [P, 4, D], F32R)
            v_lo = self.sb(c, "v_lo", [P, 4, D], F32R)
            g = self.sb(c, "g", [P, 2, T])
            act_hi = self.sb(c, "act_hi", [P, 4, T], F32R)
            act_lo = self.sb(c, "act_lo", [P, 4, T], F32R)
            flat = lambda w, s: w[:, s].rearrange("p k n -> p (k n)")
            with nc.Block() as block:
                @block.sync
                def _(sp):
                    with sp.Fori(0, C // 2) as it:
                        at = [sp.snap(it * 2 + s) for s in range(2)]
                        free = [sp.snap(it * 2 + (s + 1)) for s in range(2)]
                        for s in range(2):
                            sp.wait_ge(u_split, free[s])
                            sp.dma_start(u_raw[:, s], a["peer_uT"][bass.ds(at[s], 1)].rearrange("o p n -> (o p) n")).then_inc(u_loaded[s], 16)
                            sp.wait_ge(a_split, free[s])
                            sp.dma_start(g[:, s], self.route_scr[bass.ds(at[s], 1)].rearrange("o p n -> (o p) n")).then_inc(g_loaded[s], 16)
                            sp.wait_ge(v_split, free[s])
                            sp.dma_start(v_raw[:, s], a["peer_v"][bass.ds(at[s], 1)].rearrange("o p n -> (o p) n")).then_inc(v_loaded[s], 16)

                @block.scalar
                def _(act):
                    def split_u(j, s):
                        act.wait_ge(u_loaded[s], j * 8 + (16 - 8 * s))
                        if not isinstance(j, int):
                            act.wait_ge(hidden, j - 1)
                        act.activation(flat(u_hi, s), u_raw[:, s], ACT.Copy).then_inc(u_hi_done, 1)

                    def chunk(j, ring, more=True):
                        s = ring % 2
                        act.wait_ge(hidden, j + 1)
                        act.activation(hid[s], hid[s], ACT.Gelu_apprx_tanh).then_inc(gelu_done, 1)
                        if more:
                            split_u(j + 2, s)
                        act.wait_ge(weighted, j + 3)
                        act.activation(act_hi[:, ring], g[:, s], ACT.Copy).then_inc(a_hi_done, 1)
                        act.wait_ge(v_loaded[s], j * 8 + (16 - 8 * s))
                        act.activation(v_hi[:, ring], v_raw[:, s], ACT.Copy).then_inc(v_hi_done, 1)
                    split_u(0, 0)
                    split_u(1, 1)
                    chunk(0, 0)
                    chunk(1, 1)
                    with act.Fori(0, C // 4 - 1) as it:
                        for i in range(2, 6):
                            chunk(it * 4 + i, i % 4)
                    chunk(C - 2, 2, more=False)
                    chunk(C - 1, 3, more=False)

                @block.vector
                def _(dve):
                    dve.memset(y[:], 0.0).then_inc(zeroed, 1)
                    dve.sem_inc(u_split, 2)
                    dve.sem_inc(v_split, 2)
                    dve.sem_inc(weighted, 2)
                    dve.sem_inc(a_split, 2)

                    def split_u(j, s):
                        dve.wait_ge(u_hi_done, j + 1)
                        dve.tensor_tensor(flat(u_lo, s), u_raw[:, s], flat(u_hi, s).bitcast(F32), ALU.subtract).then_inc(u_split, 1)

                    def chunk(j, ring, more=True):
                        s = ring % 2
                        dve.wait_ge(gelu_done, j + 1)
                        dve.wait_ge(g_loaded[s], j * 8 + (16 - 8 * s))
                        dve.tensor_tensor(g[:, s], hid[s], g[:, s], ALU.mult).then_inc(weighted, 1)
                        if more:
                            split_u(j + 2, s)
                        dve.wait_ge(a_hi_done, j + 1)
                        dve.tensor_tensor(act_lo[:, ring], g[:, s], act_hi[:, ring].bitcast(F32), ALU.subtract).then_inc(a_split, 1)
                        dve.wait_ge(v_hi_done, j + 1)
                        dve.tensor_tensor(v_lo[:, ring], v_raw[:, s], v_hi[:, ring].bitcast(F32), ALU.subtract).then_inc(v_split, 1)

                    def add(pair):
                        for n in range(TILES):
                            k, half = divmod(n, 2)
                            to = y[:, k, half * HALF:(half + 1) * HALF]
                            dve.wait_ge(summed, pair * TILES + (n + 1))
                            dve.tensor_tensor(to, to, ps[:, 4 + n % 4], ALU.add).then_inc(added, 1)
                    split_u(0, 0)
                    split_u(1, 1)
                    chunk(0, 0)
                    chunk(1, 1)
                    dve.wait_ge(zeroed, 1)
                    with dve.Fori(0, C // 4 - 1) as it:
                        chunk(it * 4 + 2, 2)
                        chunk(it * 4 + 3, 3)
                        add(it * 2)
                        chunk(it * 4 + 4, 0)
                        chunk(it * 4 + 5, 1)
                        add(it * 2 + 1)
                    chunk(C - 2, 2, more=False)
                    chunk(C - 1, 3, more=False)
                    add(C // 2 - 2)
                    add(C // 2 - 1)

                @block.tensor
                def _(pe):
                    pe.sem_inc(added, 4)

                    def up(j, ring):
                        s = ring % 2
                        pe.wait_ge(u_split, j + 3)
                        pe.wait_ge(weighted, j + 1)
                        for half in range(2):
                            t = slice(half * HALF, (half + 1) * HALF)
                            for k in range(KT):
                                last = self.product3(pe, ps[:, 2 * s + half], u_hi[:, s, k], u_lo[:, s, k],
                                                     h2_hi[:, k, t], h2_lo[:, k, t], k == 0, k == KT - 1)
                        last.then_inc(hidden, 1)

                    def down(pair, rings):
                        pe.wait_ge(a_split, pair * 2 + 4)
                        pe.wait_ge(v_split, pair * 2 + 4)
                        for n in range(TILES):
                            k, half = divmod(n, 2)
                            d = slice(k * P, (k + 1) * P)
                            t = slice(half * HALF, (half + 1) * HALF)
                            pe.wait_ge(added, pair * TILES + (n + 1))
                            for r in rings:
                                last = self.product3(pe, ps[:, 4 + n % 4], v_hi[:, r, d], v_lo[:, r, d],
                                                     act_hi[:, r, t], act_lo[:, r, t], r == rings[0], r == rings[1])
                            last.then_inc(summed, 1)
                    up(0, 0)
                    up(1, 1)
                    with pe.Fori(0, C // 4 - 1) as it:
                        up(it * 4 + 2, 2)
                        up(it * 4 + 3, 3)
                        down(it * 2, (0, 1))
                        up(it * 4 + 4, 0)
                        up(it * 4 + 5, 1)
                        down(it * 2 + 1, (2, 3))
                    up(C - 2, 2)
                    up(C - 1, 3)
                    down(C // 2 - 2, (0, 1))
                    down(C // 2 - 1, (2, 3))


def _tiles(w):
    n = w.shape[1] // P
    return np.ascontiguousarray(w.reshape(KT, P, n, P).transpose(2, 1, 0, 3)).reshape(n, P, KT * P)


def _columns(v):
    return np.asarray(v).reshape(-1, P).T


def kernel(**inputs):
    import concourse.bacc as bacc
    from concourse.bass_utils import run_bass_kernel_spmd

    x = {k: np.asarray(v) for k, v in inputs.items()}
    rot = np.zeros((P, P), np.float32)
    freq = np.zeros((P, 1), np.float32)
    half = ROPE_DIM // 2
    inv = np.float32(ROPE_THETA) ** (-np.arange(0, ROPE_DIM, 2, dtype=np.float32) / np.float32(ROPE_DIM))
    for m in range(2):
        for i in range(half):
            r1, r2 = m * MAP_DIM + i, m * MAP_DIM + half + i
            rot[r2, r1] = -1.0
            rot[r1, r2] = 1.0
            freq[r1, 0] = freq[r2, 0] = inv[i]
    arrays = {
        "xT": x["x"][0].T,
        "c": x["c"],
        "positions": x["positions"],
        "w_adaT": x["w_ada"][0].T.reshape(NMOD, P, D).transpose(1, 0, 2),
        "b_ada": _columns(x["b_ada"][0]),
        "vecs": np.concatenate([_columns(x[n][0]) for n in ("g_pre_mix", "g_post_mix", "g_pre_ffn", "g_post_ffn", "gmlp_ln_g", "gmlp_ln_b")], 1),
        "g_subln": x["g_subln"][0][:, None],
        "lams": np.concatenate([x[n][0] for n in ("lambda_q1", "lambda_k1", "lambda_q2", "lambda_k2")])[None],
        "ident": np.eye(P, dtype=np.float32),
        "rotate": rot,
        "freq": freq,
        "w_in": _tiles(x["w_in"][0]),
        "w_attn": _tiles(x["w_attn_branch"][0]),
        "w_gmlp": _tiles(x["w_gmlp_branch"][0]),
        "w_out": _tiles(x["w_out"][0]),
        "w_peer": _tiles(x["w_peer_q"][0]),
        "w_spatial": x["w_spatial"][0].transpose(2, 0, 1).reshape(P, -1),
        "b_spatial": x["b_spatial"][0].reshape(1, -1),
        "keysT": x["peer_sub_keys"][0].reshape(SIDES, KEYS, P).transpose(2, 0, 1).reshape(P, -1),
        "peer_uT": x["peer_u"][0].reshape(KEYS, P, KT, P).transpose(0, 3, 2, 1).reshape(KEYS, P, D),
        "peer_v": x["peer_v"][0].reshape(KEYS, P, D),
    }
    arrays = {f"{k}_dram": np.ascontiguousarray(v) for k, v in arrays.items()}
    nc = bacc.Bacc("TRN2", target_bir_lowering=False, num_devices=1)
    aps = {k.removesuffix("_dram"): nc.dram_tensor(k, v.shape, mybir.dt.from_np(v.dtype), kind="ExternalInput").ap() for k, v in arrays.items()}
    aps["out"] = nc.dram_tensor("out", (D, T), F32, kind="ExternalOutput").ap()
    Layer(nc, aps).build()
    got = run_bass_kernel_spmd(nc, [arrays], core_ids=[0])
    return got.results[0]["out"].T[None]
```

```python
import math
from contextlib import ExitStack

import numpy as np

import concourse.bass as bass
from concourse import mybir

F32 = mybir.dt.float32
F32R = mybir.dt.float32r
F16 = mybir.dt.float16
I32 = mybir.dt.int32
U32 = mybir.dt.uint32
ALU = mybir.AluOpType
ACT = mybir.ActivationFunctionType
AXX = mybir.AxisListType.X

P = 128
T = 1024
D = 1024
KT = D // P
TB = T // P
HALF = 512
HEADS = 8
MAP_DIM = 64
TOPK = 16
SIDES = 2 * HEADS
KEYS = 128
NMOD = 6 * KT
EPS = 1e-6
LAMBDA_INIT = 0.8 - 0.6 * math.exp(-0.3 * 0)
SCALE = MAP_DIM ** -0.5
ROPE_DIM = MAP_DIM // 4
ROPE_THETA = 500000.0
LOWEST = -3.0e38
WEIGHT_SCALE = 2.0 ** 14
EARLY = 5 * TB

Q0, K0, V0, ZU0, ZV0, GA0, GG0 = 0, 8, 16, 24, 32, 40, 48


class Layer:

    def __init__(self, nc, a):
        self.nc, self.a = nc, a
        self.ctx = ExitStack()
        self.stage_sems = []

    def sb(self, ctx, name, shape, dt=F32):
        return ctx.enter_context(self.nc.sbuf_tensor(name, shape, dt))

    def sem(self, name):
        self.stage_sems.append(self.nc.alloc_semaphore(name=name))
        return self.stage_sems[-1]

    def stage_end(self):
        self.nc.all_engine_barrier()
        self.nc.clear_and_free_semaphores(self.stage_sems)
        self.nc.all_engine_barrier()
        self.stage_sems = []

    def scratch(self, name, shape):
        return self.nc.dram_tensor(name, shape, F32, kind="Internal").ap()

    def build(self):
        nc = self.nc
        with self.ctx:
            c = self.ctx
            self.ident = self.sb(c, "ident", [P, P])
            self.ones_mean = self.sb(c, "ones_mean", [P, P])
            self.ones_head = self.sb(c, "ones_head", [P, P])
            self.vecs = self.sb(c, "vecs", [P, NMOD])
            self.subln_gain = self.sb(c, "subln_gain", [P, 1])
            self.mod = self.sb(c, "mod", [P, NMOD])
            self.coef = self.sb(c, "coef", [P, 4 * KT])
            self.lam = self.sb(c, "lam", [P, 1])
            self.psum = c.enter_context(nc.psum_tensor("psum", [P, 8, HALF], F32))
            self.gate_scr = self.scratch("gate_scratch", [2 * KT, P, T])
            self.u_scr = self.scratch("gelu_u_scratch", [KT, P, T])
            self.o_scr = self.scratch("attention_scratch", [HEADS, P, T])
            self.sg_scr = self.scratch("spatial_scratch", [KT, P, T])
            self.x1_scr = self.scratch("residual_scratch", [KT, P, T])
            self.h_scr = self.scratch("hidden_scratch", [EARLY, P, T])
            self.route_scr = self.scratch("route_scratch", [KEYS, P, T])

            with ExitStack() as rope_scope:
                self.cos = self.sb(rope_scope, "cos", [P, T])
                self.sin = self.sb(rope_scope, "sin", [P, T])
                self.rotate = self.sb(rope_scope, "rotate", [P, P])
                self.conditioning()
                self.stage_end()
                h_hi = self.sb(rope_scope, "h_hi", [P, KT, T], F32R)
                h_lo = self.sb(rope_scope, "h_lo", [P, KT, T], F32R)
                with ExitStack() as s:
                    x = self.sb(s, "x", [P, KT, T])
                    self.load(x, self.a["xT"].rearrange("(k p) t -> p k t", p=P), "x")
                    self.rms_modulate("pre_mix", x, self.coef[:, 0:KT], self.mod[:, 0:KT], h_hi, h_lo)
                    self.stage_end()
                self.attention(h_hi, h_lo)
                self.stage_end()
                self.gmlp(h_hi, h_lo)
                self.stage_end()
                self.gates(h_hi, h_lo)
                self.stage_end()
            with ExitStack() as mixing:
                wide = self.sb(mixing, "mixed", [P, KT, T])
                with ExitStack() as s:
                    m_hi = self.sb(s, "m_hi", [P, KT, T], F32R)
                    m_lo = self.sb(s, "m_lo", [P, KT, T], F32R)
                    self.branches(wide, m_hi, m_lo)
                    self.stage_end()
                    self.out_projection(wide, m_hi, m_lo)
                    self.stage_end()
                self.residual(wide, self.sb(mixing, "x1_made", [P, KT, T]))
                self.stage_end()
            h2_hi = self.sb(c, "h2_hi", [P, KT, T], F32R)
            h2_lo = self.sb(c, "h2_lo", [P, KT, T], F32R)
            with ExitStack() as s:
                x1 = self.sb(s, "x1", [P, KT, T])
                self.load(x1, self.x1_scr.rearrange("k p t -> p k t"), "x1")
                self.rms_modulate("pre_ffn", x1, self.coef[:, 2 * KT:3 * KT], self.mod[:, 3 * KT:4 * KT], h2_hi, h2_lo)
                self.stage_end()
            self.route(h2_hi, h2_lo)
            y = self.sb(c, "y", [P, KT, T])
            self.experts(h2_hi, h2_lo, y)
            self.stage_end()
            self.finish(y)
            self.stage_end()

    def load(self, tile, src, name):
        loaded = self.sem(f"{name}_loaded")
        with self.nc.Block() as block:
            @block.sync
            def _(sp):
                sp.dma_start(tile[:], src).then_inc(loaded, 16)
                sp.wait_ge(loaded, 16)

    def conditioning(self):
        nc, a = self.nc, self.a
        NBUF = 4
        small = self.sem("small_loaded")
        ada_loaded = [self.sem(f"ada_loaded{i}") for i in range(NBUF)]
        c_ready = self.sem("c_ready")
        mod_dot = self.sem("mod_dot")
        chain = self.sem("conditioning_chain")
        lam_dots = self.sem("lam_dots")
        lam_exp = self.sem("lam_exp")
        angles = self.sem("angles")
        tables = self.sem("rope_tables")
        with ExitStack() as s:
            ada = self.sb(s, "ada", [P, NBUF, 2, D])
            cb = self.sb(s, "cb", [P, D])
            junk = self.sb(s, "junk", [P, 2, D])
            b_ada = self.sb(s, "b_ada", [P, NMOD])
            lams = self.sb(s, "lams", [P, 4, MAP_DIM])
            lam2 = self.sb(s, "lam2", [P, 4])
            pos = self.sb(s, "pos", [P, T], I32)
            freq = self.sb(s, "freq", [P, 1])
            ang = self.sb(s, "ang", [P, T])
            turns = self.sb(s, "turns", [P, T])
            folded = self.sb(s, "folded", [P, T])
            NSMALL = 9
            with nc.Block() as block:
                @block.sync
                def _(sp):
                    sp.dma_start(cb[:], a["c"].to_broadcast([P, D])).then_inc(small, 16)
                    sp.dma_start(self.ident[:], a["ident"]).then_inc(small, 16)
                    sp.dma_start(self.rotate[:], a["rotate"]).then_inc(small, 16)
                    sp.dma_start(self.vecs[:], a["vecs"]).then_inc(small, 16)
                    sp.dma_start(self.subln_gain[:], a["g_subln"]).then_inc(small, 16)
                    sp.dma_start(b_ada[:], a["b_ada"]).then_inc(small, 16)
                    sp.dma_start(freq[:], a["freq"]).then_inc(small, 16)
                    sp.dma_start(lams[:].rearrange("p a d -> p (a d)"), a["lams"].to_broadcast([P, 4 * MAP_DIM])).then_inc(small, 16)
                    sp.dma_start(pos[:], a["positions"].to_broadcast([P, T])).then_inc(small, 16)
                    for g in range(NMOD // 2):
                        if g >= NBUF:
                            sp.wait_ge(mod_dot, 2 * (g - NBUF + 1))
                        sp.dma_start(ada[:, g % NBUF], a["w_adaT"][:, 2 * g:2 * g + 2, :]).then_inc(ada_loaded[g % NBUF], 16)

                @block.scalar
                def _(act):
                    act.wait_ge(small, 16 * NSMALL)
                    act.activation(cb[:], cb[:], ACT.Silu).then_inc(c_ready, 1)
                    act.wait_ge(lam_dots, 2)
                    act.activation(lam2[:, 2:4], lam2[:, 0:2], ACT.Exp).then_inc(lam_exp, 1)
                    act.wait_ge(angles, 1)
                    act.activation(self.sin[:], ang[:], ACT.Sin).then_inc(tables, 1)
                    act.activation(self.cos[:], folded[:], ACT.Sin).then_inc(tables, 1)

                @block.vector
                def _(dve):
                    n = [0]

                    def link(ins):
                        n[0] += 1
                        ins.then_inc(chain, 1)
                        dve.wait_ge(chain, n[0])

                    dve.memset(self.ones_mean[:], 1.0 / D)
                    link(dve.memset(self.ones_head[:], 1.0 / P))
                    dve.wait_ge(small, 16 * NSMALL)
                    for i in range(2):
                        dve.tensor_tensor_reduce(out=junk[:, i, 0:MAP_DIM], in0=lams[:, 2 * i], in1=lams[:, 2 * i + 1],
                                                 scale=1.0, scalar=0.0, op0=ALU.mult, op1=ALU.add,
                                                 accum_out=lam2[:, i:i + 1]).then_inc(lam_dots, 1)
                    link(dve.tensor_copy(ang[:], pos[:]))
                    link(dve.tensor_scalar(ang[:], ang[:], freq[:, 0:1], None, ALU.mult))
                    magic = 1.5 * 2.0 ** 23
                    link(dve.tensor_scalar(turns[:], ang[:], 1.0 / (2.0 * math.pi), None, ALU.mult))
                    link(dve.tensor_scalar(turns[:], turns[:], magic, None, ALU.add))
                    link(dve.tensor_scalar(turns[:], turns[:], magic, None, ALU.subtract))
                    c1 = 6.28125
                    c2 = float(np.float32(round((2 * math.pi - c1) * 2 ** 20) / 2 ** 20))
                    c3 = 2 * math.pi - c1 - c2
                    for part in (c1, c2, c3):
                        link(dve.scalar_tensor_tensor(ang[:], turns[:], -part, ang[:], ALU.mult, ALU.add))
                    limit = float(np.nextafter(np.float32(math.pi), np.float32(0)))
                    link(dve.tensor_scalar(ang[:], ang[:], limit, -limit, ALU.min, ALU.max))
                    link(dve.tensor_scalar(folded[:], ang[:], -1.0, None, ALU.mult))
                    link(dve.tensor_tensor(folded[:], folded[:], ang[:], ALU.max))
                    dve.tensor_scalar(folded[:], folded[:], -1.0, math.pi / 2, ALU.mult, ALU.add).then_inc(angles, 1)
                    dve.wait_ge(c_ready, 1)
                    for j in range(NMOD):
                        g = j // 2
                        dve.wait_ge(ada_loaded[g % NBUF], 16 * (g // NBUF + 1))
                        if j >= 2:
                            dve.wait_ge(mod_dot, j - 1)
                        elif j == 0:
                            dve.wait_ge(lam_dots, 2)
                        dve.tensor_tensor_reduce(out=junk[:, j % 2], in0=ada[:, g % NBUF, j % 2], in1=cb[:], scale=1.0,
                                                 scalar=0.0, op0=ALU.mult, op1=ALU.add,
                                                 accum_out=self.mod[:, j:j + 1]).then_inc(mod_dot, 1)
                    dve.wait_ge(mod_dot, NMOD)
                    link(dve.tensor_tensor(self.mod[:], self.mod[:], b_ada[:], ALU.add))
                    K = KT
                    sc1, gt1, sc2, gt2 = (self.mod[:, K * i:K * i + K] for i in (1, 2, 4, 5))
                    pre1, post1, pre2, post2 = (self.vecs[:, K * i:K * i + K] for i in range(4))
                    dve.scalar_tensor_tensor(self.coef[:, 0:K], sc1, 1.0, pre1, ALU.add, ALU.mult)
                    dve.tensor_tensor(self.coef[:, K:2 * K], gt1, post1, ALU.mult)
                    dve.scalar_tensor_tensor(self.coef[:, 2 * K:3 * K], sc2, 1.0, pre2, ALU.add, ALU.mult)
                    dve.tensor_tensor(self.coef[:, 3 * K:4 * K], gt2, post2, ALU.mult)
                    dve.tensor_scalar(self.subln_gain[:], self.subln_gain[:], 1.0 - LAMBDA_INIT, None, ALU.mult)
                    dve.wait_ge(lam_exp, 1)
                    link(dve.tensor_tensor(self.lam[:], lam2[:, 2:3], lam2[:, 3:4], ALU.subtract))
                    link(dve.tensor_scalar(self.lam[:], self.lam[:], LAMBDA_INIT, None, ALU.add))

    def mean_square(self, name, src, rstd, ones, sq, tiles=KT):
        nc = self.nc
        squared = self.sem(f"{name}_squared")
        summed = self.sem(f"{name}_summed")
        chain = self.sem(f"{name}_rstd")
        ms = self.psum[:, 0:2].rearrange("p b t -> p (b t)")
        with nc.Block() as block:
            @block.scalar
            def _(act):
                for k in range(tiles):
                    if k >= 2:
                        act.wait_ge(summed, k - 1)
                    act.activation(sq[:, k % 2], src[:, k], ACT.Square).then_inc(squared, 1)
                act.wait_ge(chain, 1)
                act.activation(rstd[:], rstd[:], ACT.Sqrt).then_inc(chain, 1)

            @block.tensor
            def _(pe):
                for k in range(tiles):
                    pe.wait_ge(squared, k + 1)
                    for half in range(2):
                        last = pe.matmul(self.psum[:, half], ones[:], sq[:, k % 2, half * HALF:(half + 1) * HALF],
                                         start=(k == 0), stop=(k == tiles - 1))
                    last.then_inc(summed, 1)

            @block.vector
            def _(dve):
                dve.wait_ge(summed, tiles)
                dve.tensor_scalar(rstd[:], ms, EPS, None, ALU.add).then_inc(chain, 1)
                dve.wait_ge(chain, 2)
                dve.reciprocal(rstd[:], rstd[:]).then_inc(chain, 1)

    def rms_modulate(self, name, x, gain, shift, hi, lo):
        nc = self.nc
        scaled = self.sem(f"{name}_scaled")
        full = self.sem(f"{name}_full")
        hi_done = self.sem(f"{name}_hi")
        lo_done = self.sem(f"{name}_lo")
        with ExitStack() as s:
            rstd = self.sb(s, f"{name}_rstd_t", [P, T])
            sq = self.sb(s, f"{name}_sq", [P, 2, T])
            self.mean_square(name, x, rstd, self.ones_mean, sq)
            with nc.Block() as block:
                @block.vector
                def _(dve):
                    for k in range(KT):
                        if k >= 2:
                            dve.wait_ge(lo_done, k - 1)
                        dve.tensor_tensor(sq[:, k % 2], x[:, k], rstd[:], ALU.mult).then_inc(scaled, 1)
                        dve.wait_ge(scaled, k + 1)
                        dve.tensor_scalar(sq[:, k % 2], sq[:, k % 2], gain[:, k:k + 1], shift[:, k:k + 1],
                                          ALU.mult, ALU.add).then_inc(full, 1)
                        dve.wait_ge(hi_done, k + 1)
                        dve.tensor_tensor(lo[:, k], sq[:, k % 2], hi[:, k].bitcast(F32), ALU.subtract).then_inc(lo_done, 1)

                @block.scalar
                def _(act):
                    for k in range(KT):
                        act.wait_ge(full, k + 1)
                        act.activation(hi[:, k], sq[:, k % 2], ACT.Copy).then_inc(hi_done, 1)

    def product3(self, pe, out, w_hi, w_lo, x_hi, x_lo, start, stop):
        pe.matmul(out, w_hi, x_hi, start=start, stop=False)
        pe.matmul(out, w_hi, x_lo, start=False, stop=False)
        return pe.matmul(out, w_lo, x_hi, start=False, stop=stop)

    def projection(self, name, wt, first, x_hi, x_lo, tiles, act_out=None, dve_out=None, pe_after=None, dve_after=None, pool_program=None):
        nc = self.nc
        loaded = [self.sem(f"{name}_w_loaded{i}") for i in range(2)]
        w_hi_done = self.sem(f"{name}_w_hi_done")
        w_split = self.sem(f"{name}_w_split")
        product = self.sem(f"{name}_product")
        emptied = self.sem(f"{name}_emptied")
        acc = [self.psum[:, 2 * s:2 * s + 2].rearrange("p b t -> p (b t)") for s in range(2)]
        turns = tiles // 2
        with ExitStack() as c:
            raw = self.sb(c, f"{name}_w_raw", [P, 2, D])
            w_hi = self.sb(c, f"{name}_w_hi_t", [P, 2, KT, P], F32R)
            w_lo = self.sb(c, f"{name}_w_lo_t", [P, 2, KT, P], F32R)
            flat = lambda w, s: w[:, s].rearrange("p k n -> p (k n)")
            with nc.Block() as block:
                @block.sync
                def _(sp):
                    def turn(j0):
                        at = [sp.snap(j0 + s) if not isinstance(j0, int) else j0 + s for s in range(2)]
                        free = [sp.snap(j0 + s + 1) if not isinstance(j0, int) else j0 + s + 1 for s in range(2)]
                        src = [sp.snap(j0 + s + first) if not isinstance(j0, int) else j0 + s + first for s in range(2)]
                        for s in range(2):
                            sp.wait_ge(w_split, free[s])
                            sp.dma_start(raw[:, s], wt[bass.ds(src[s], 1)].rearrange("o p n -> (o p) n")).then_inc(loaded[s], 16)
                    with sp.Fori(0, turns) as it:
                        turn(it * 2)

                @block.scalar
                def _(act):
                    def split(j, s):
                        act.wait_ge(loaded[s], j * 8 + (16 - 8 * s))
                        act.wait_ge(product, j + 1)
                        act.activation(flat(w_hi, s), raw[:, s], ACT.Copy).then_inc(w_hi_done, 1)

                    def empty(j, s):
                        if act_out:
                            act.wait_ge(product, j + 3)
                            act_out(act, j, s, acc[s], emptied)
                    for s in range(2):
                        split(s, s)
                    if turns > 1:
                        with act.Fori(0, turns - 1) as it:
                            for s in range(2):
                                empty(it * 2 + s, s)
                                split(it * 2 + (2 + s), s)
                    for s in range(2):
                        empty(tiles - 2 + s, s)

                @block.vector
                def _(dve):
                    dve.sem_inc(w_split, 2)

                    def split(j, s):
                        dve.wait_ge(w_hi_done, j + 1)
                        dve.tensor_tensor(flat(w_lo, s), raw[:, s], flat(w_hi, s).bitcast(F32), ALU.subtract).then_inc(w_split, 1)

                    def empty(j, s):
                        if dve_out:
                            dve.wait_ge(product, j + 3)
                            dve_out(dve, j, s, acc[s], emptied)
                    for s in range(2):
                        split(s, s)
                    if dve_after is None:
                        with dve.Fori(0, turns - 1) as it:
                            for s in range(2):
                                empty(it * 2 + s, s)
                                split(it * 2 + (2 + s), s)
                        for s in range(2):
                            empty(tiles - 2 + s, s)
                    else:
                        empty(0, 0)
                        split(2, 0)
                        with dve.Fori(0, turns - 2) as it:
                            for s in range(2):
                                empty(it * 2 + (1 + s), 1 - s)
                                split(it * 2 + (3 + s), 1 - s)
                                dve_after(dve, it * 2 + s, s)
                        empty(tiles - 3, 1)
                        split(tiles - 1, 1)
                        dve_after(dve, tiles - 4, 0)
                        empty(tiles - 2, 0)
                        dve_after(dve, tiles - 3, 1)
                        empty(tiles - 1, 1)
                        dve_after(dve, tiles - 2, 0)
                        dve_after(dve, tiles - 1, 1)

                @block.tensor
                def _(pe):
                    pe.sem_inc(product, 2)
                    pe.sem_inc(emptied, 2)

                    def tile(j, s):
                        pe.wait_ge(w_split, j + 3)
                        pe.wait_ge(emptied, j + 1)
                        for half in range(2):
                            t = slice(half * HALF, (half + 1) * HALF)
                            for k in range(KT):
                                last = self.product3(pe, self.psum[:, 2 * s + half], w_hi[:, s, k], w_lo[:, s, k],
                                                     x_hi[:, k, t], x_lo[:, k, t], k == 0, k == KT - 1)
                        last.then_inc(product, 1)
                    if pe_after is None:
                        with pe.Fori(0, turns) as it:
                            for s in range(2):
                                tile(it * 2 + s, s)
                    else:
                        tile(0, 0)
                        with pe.Fori(0, turns - 1) as it:
                            for s in range(2):
                                tile(it * 2 + (1 + s), 1 - s)
                                pe_after(pe, it * 2 + s, s, emptied)
                        tile(tiles - 1, 1)
                        pe_after(pe, tiles - 2, 0, emptied)
                        pe_after(pe, tiles - 1, 1, emptied)

                if pool_program:
                    @block.gpsimd
                    def _(pool):
                        pool_program(pool, emptied)

    def attention(self, h_hi, h_lo):
        nc, w = self.nc, self.a["w_in"]
        ps = self.psum
        acc = [ps[:, 2 * s:2 * s + 2].rearrange("p b t -> p (b t)") for s in range(2)]
        turned = ps[:, 4:6].rearrange("p b t -> p (b t)")
        o_acc = ps[:, 6]
        job = ps[:, 7]
        KK, QQ, VV = range(3)
        TILE0 = (K0, Q0, V0)
        HALVES = [(i, half) for i in (KK, QQ, VV) for half in range(2)]
        BPH = TB
        w_loaded = [self.sem(f"att_w_loaded{i}") for i in range(2)]
        w_hi_done = self.sem("att_w_hi_done")
        w_split = self.sem("att_w_split")
        projected = self.sem("att_projected")
        copied = self.sem("att_copied")
        prepared = self.sem("att_prepared")
        rope = self.sem("att_rope")
        x_hi_done = self.sem("att_x_hi_done")
        x_split = self.sem("att_x_split")
        scored = self.sem("att_scored")
        negmax = self.sem("att_negmax")
        exped = self.sem("att_exped")
        mixing = self.sem("att_mixing")
        mixed = self.sem("att_mixed")
        a_turned = self.sem("att_a_turned")
        a_hi_done = self.sem("att_a_hi")
        a_split = self.sem("att_a_split")
        out_summed = self.sem("att_out_summed")
        out_copied = self.sem("att_out_copied")
        stored = [self.sem(f"att_stored{i}") for i in range(2)]
        with ExitStack() as c:
            raw = self.sb(c, "att_raw", [P, 2, D])
            w_hi = self.sb(c, "att_w_hi_t", [P, 2, KT, P], F32R)
            w_lo = self.sb(c, "att_w_lo_t", [P, 2, KT, P], F32R)
            x_hi = self.sb(c, "att_x_hi", [P, 2, 3, T], F32R)
            x_lo = self.sb(c, "att_x_lo", [P, 2, 3, T], F32R)
            plain = self.sb(c, "att_plain", [P, 2, HALF])
            swung = self.sb(c, "att_swung", [P, HALF])
            prob = self.sb(c, "att_prob", [P, 2, T])
            amap = self.sb(c, "att_map", [P, 2, T])
            a_hi = self.sb(c, "att_a_hi_t", [P, KT, HALF], F32R)
            a_lo = self.sb(c, "att_a_lo_t", [P, KT, HALF], F32R)
            nmax = self.sb(c, "att_nmax", [P, 2])
            z = self.sb(c, "att_z", [P, 2])
            zr = self.sb(c, "att_zr", [P, 2])
            o = self.sb(c, "att_o", [P, 2, HALF])
            flat = lambda t, s: t[:, s].rearrange("p k n -> p (k n)")
            cols = lambda half: slice(half * HALF, (half + 1) * HALF)

            class Head:

                def __init__(self, it, c):
                    self.it, self.c, self.par = it, c, c % 2

                def at(self, per_head, more):
                    return self.it * (2 * per_head) + (self.c * per_head + more)

                def next(self):
                    return Head(self.it, self.c + 1)

                def ring(self, i):
                    return (3 * self.c + i) % 2

                def loads(self, i):
                    return self.it * 48 + 16 * ((3 * self.c + i) // 2 + 1)

            def all_heads(eng, body, first=None):
                with eng.Fori(0, HEADS // 2 - 1) as it:
                    for c2 in range(2):
                        body(Head(it, c2), Head(it, c2 + 1))
                last = HEADS // 2 - 1
                body(Head(last, 0), Head(last, 1))
                body(Head(last, 1), None)

            PROJECTS = {b: b for b in range(6)}
            PREPARES = {b: b - 1 for b in range(1, 7)}
            SPLITS = {0: (QQ, 0), 2: (VV, 0), 4: (KK, 1)}

            with nc.Block() as block:
                @block.sync
                def _(sp):
                    with sp.Fori(0, HEADS // 2) as it:
                        n0 = [sp.snap(it * 6 + (n + 1)) for n in range(6)]
                        src = [sp.snap(it * 2 + (c2 + TILE0[i])) for c2 in range(2) for i in range(3)]
                        to = [sp.snap(it * 2 + c2) for c2 in range(2)]
                        for n in range(6):
                            sp.wait_ge(w_split, n0[n])
                            sp.dma_start(raw[:, n % 2], w[bass.ds(src[n], 1)].rearrange("o p n -> (o p) n")).then_inc(w_loaded[n % 2], 16)

                @block.scalar
                def _(act):
                    def split_weights(g, i):
                        r = g.ring(i)
                        act.wait_ge(w_loaded[r], g.loads(i))
                        act.wait_ge(projected, g.at(6, 2 * i + 2))
                        act.activation(flat(w_hi, r), raw[:, r], ACT.Copy).then_inc(w_hi_done, 1)

                    def copy(g, e):
                        act.wait_ge(projected, g.at(6, e + 5))
                        act.wait_ge(x_split, g.at(6, e + 5))
                        act.activation(plain[:, e % 2], job, ACT.Copy).then_inc(copied, 1)

                    def high(g, e):
                        i, half = HALVES[e]
                        if i == VV:
                            act.wait_ge(prepared, g.at(6, e + 1))
                            act.activation(x_hi[:, g.par, i, cols(half)], job, ACT.Copy).then_inc(x_hi_done, 1)
                        else:
                            act.wait_ge(rope, g.at(12, 3 * e + 3))
                            act.activation(x_hi[:, g.par, i, cols(half)], plain[:, e % 2], ACT.Copy).then_inc(x_hi_done, 1)

                    def exps(h, b):
                        for m in range(2):
                            act.wait_ge(negmax, h.at(2 * BPH, 2 * b + m + 1))
                            act.wait_ge(mixed, h.at(BPH, b + 2))
                            act.activation(prob[:, m], acc[m], ACT.Exp, bias=nmax[:, m:m + 1], scale=1.0,
                                           accum_out=z[:, m:m + 1]).then_inc(exped, 1)

                    def turned_hi(h, b):
                        act.wait_ge(a_turned, h.at(BPH, b + 3))
                        if b % 4 == 0:
                            act.wait_ge(out_summed, h.at(2, b // 4 + 1))
                        act.activation(a_hi[:, :, (b % 4) * P:(b % 4 + 1) * P], turned.rearrange("p (k q) -> p k q", q=P),
                                       ACT.Copy).then_inc(a_hi_done, 1)

                    def out(h, half):
                        act.wait_ge(out_summed, h.at(2, half + 2))
                        act.wait_ge(stored[half], h.at(16, 16))
                        act.activation(o[:, half], o_acc, ACT.Copy).then_inc(out_copied, 1)
                        act.wait_ge(out_copied, h.at(2, half + 2))
                        act.dma_start(self.o_scr[bass.ds(h.at(1, 0), 1), :, cols(half)].rearrange("o p n -> (o p) n"),
                                      o[:, half]).then_inc(stored[half], 16)

                    def body(h, g):
                        for b in range(BPH):
                            e = PREPARES.get(b)
                            if g and e is not None and HALVES[e][0] == VV:
                                high(g, e)
                            turned_hi(h, b)
                            if b + 1 < BPH:
                                exps(h, b + 1)
                            elif g:
                                exps(g, 0)
                            if g and b in SPLITS:
                                i, after = SPLITS[b]
                                if not after:
                                    split_weights(g, i)
                                elif not (isinstance(g.it, int) and 2 * g.it + g.c == HEADS - 1):
                                    split_weights(g.next(), i)
                            if g and e is not None and HALVES[e][0] != VV:
                                high(g, e)
                            if b == 4:
                                out(h, 0)
                            if g and b in PROJECTS:
                                copy(g, PROJECTS[b])
                        out(h, 1)
                    first = Head(0, 0)
                    split_weights(first, KK)
                    split_weights(first, QQ)
                    for e, (i, half) in enumerate(HALVES):
                        copy(first, e)
                        if e == 1:
                            split_weights(first, VV)
                        if e == 3:
                            split_weights(first.next(), KK)
                        high(first, e)
                    exps(first, 0)
                    all_heads(act, body)

                @block.vector
                def _(dve):
                    dve.sem_inc(w_split, 2)
                    dve.sem_inc(x_split, 6)
                    dve.sem_inc(mixed, 2)
                    dve.sem_inc(a_split, 1)

                    def split_weights(g, i):
                        r = g.ring(i)
                        dve.wait_ge(w_hi_done, g.at(3, i + 1))
                        dve.tensor_tensor(flat(w_lo, r), raw[:, r], flat(w_hi, r).bitcast(F32), ALU.subtract).then_inc(w_split, 1)

                    def swing(g, e):
                        i, half = HALVES[e]
                        dve.wait_ge(prepared, g.at(6, e + 1))
                        dve.scalar_tensor_tensor(swung[:], job, SCALE if i == QQ else 1.0, self.sin[:, cols(half)],
                                                 ALU.mult, ALU.mult).then_inc(rope, 1)

                    def rope_sum(g, e):
                        i, half = HALVES[e]
                        x = plain[:, e % 2]
                        dve.scalar_tensor_tensor(x, x, SCALE if i == QQ else 1.0, self.cos[:, cols(half)],
                                                 ALU.mult, ALU.mult).then_inc(rope, 1)
                        dve.wait_ge(rope, g.at(12, 3 * e + 2))
                        dve.tensor_tensor(x, x, swung[:], ALU.add).then_inc(rope, 1)

                    def low(g, e):
                        i, half = HALVES[e]
                        src = job if i == VV else plain[:, e % 2]
                        dve.wait_ge(x_hi_done, g.at(6, e + 1))
                        dve.tensor_tensor(x_lo[:, g.par, i, cols(half)], src, x_hi[:, g.par, i, cols(half)].bitcast(F32),
                                          ALU.subtract).then_inc(x_split, 1)

                    def maxima(h, b):
                        for m in range(2):
                            dve.wait_ge(scored, h.at(2 * BPH, 2 * b + m + 1))
                            dve.wait_ge(exped, h.at(2 * BPH, 2 * b + m + 1))
                            dve.tensor_reduce(nmax[:, m:m + 1], acc[m], AXX, ALU.max, negate=True).then_inc(negmax, 1)

                    def combine(h, b):
                        dve.wait_ge(exped, h.at(2 * BPH, 2 * b + 4))
                        dve.reciprocal(zr[:], z[:]).then_inc(mixing, 1)
                        dve.wait_ge(mixing, h.at(3 * BPH, 3 * b + 1))
                        dve.tensor_scalar(zr[:, 1:2], zr[:, 1:2], self.lam[:, 0:1], None, ALU.mult).then_inc(mixing, 1)
                        dve.wait_ge(mixing, h.at(3 * BPH, 3 * b + 2))
                        dve.tensor_scalar(prob[:, 1], prob[:, 1], zr[:, 1:2], None, ALU.mult).then_inc(mixing, 1)
                        dve.wait_ge(mixing, h.at(3 * BPH, 3 * b + 3))
                        dve.wait_ge(a_turned, h.at(BPH, b + 1))
                        dve.scalar_tensor_tensor(amap[:, b % 2], prob[:, 0], zr[:, 0:1], prob[:, 1], ALU.mult, ALU.subtract)\
                           .then_inc(mixed, 1)

                    def turned_lo(h, b):
                        dve.wait_ge(a_hi_done, h.at(BPH, b + 1))
                        q = slice((b % 4) * P, (b % 4 + 1) * P)
                        dve.tensor_tensor(a_lo[:, :, q], turned.rearrange("p (k q) -> p k q", q=P),
                                          a_hi[:, :, q].bitcast(F32), ALU.subtract).then_inc(a_split, 1)

                    def body(h, g):
                        for b in range(BPH):
                            combine(h, b)
                            e = PREPARES.get(b) if g else None
                            if e is not None:
                                if HALVES[e][0] == VV:
                                    low(g, e)
                                else:
                                    swing(g, e)
                            if b + 1 < BPH:
                                maxima(h, b + 1)
                            elif g:
                                maxima(g, 0)
                            turned_lo(h, b)
                            if e is not None and HALVES[e][0] != VV:
                                rope_sum(g, e)
                            if g and b in SPLITS:
                                i, after = SPLITS[b]
                                if not after:
                                    split_weights(g, i)
                                elif not (isinstance(g.it, int) and 2 * g.it + g.c == HEADS - 1):
                                    split_weights(g.next(), i)
                            if e is not None and HALVES[e][0] != VV:
                                low(g, e)
                    first = Head(0, 0)
                    split_weights(first, KK)
                    split_weights(first, QQ)
                    for e, (i, half) in enumerate(HALVES):
                        if e == 1:
                            split_weights(first, VV)
                        if e == 3:
                            split_weights(first.next(), KK)
                        if i != VV:
                            swing(first, e)
                            rope_sum(first, e)
                        low(first, e)
                    maxima(first, 0)
                    all_heads(dve, body)

                @block.tensor
                def _(pe):
                    pe.sem_inc(projected, 4)
                    pe.sem_inc(exped, 2)
                    pe.sem_inc(a_turned, 2)
                    pe.sem_inc(out_summed, 1)
                    pe.sem_inc(out_copied, 1)
                    for half in range(2):
                        pe.sem_inc(stored[half], 16)

                    def project(g, e):
                        i, half = HALVES[e]
                        r = g.ring(i)
                        pe.wait_ge(w_split, g.at(3, i + 3))
                        if e in (0, 5):
                            pe.wait_ge(x_split, g.at(6, e + 6))
                        else:
                            pe.wait_ge(rope, g.at(12, 3 * (e - 1) + 1))
                        for k in range(KT):
                            last = self.product3(pe, job, w_hi[:, r, k], w_lo[:, r, k], h_hi[:, k, cols(half)], h_lo[:, k, cols(half)],
                                                 k == 0, k == KT - 1)
                        last.then_inc(projected, 1)

                    def prepare(g, e):
                        i, half = HALVES[e]
                        pe.wait_ge(copied, g.at(6, e + 1))
                        if i == VV:
                            for k in range(4):
                                last = pe.transpose(job[:, k * P:(k + 1) * P], plain[:, e % 2, k * P:(k + 1) * P], self.ident[:])
                        else:
                            last = pe.matmul(job, self.rotate[:], plain[:, e % 2], start=True, stop=True)
                        last.then_inc(prepared, 1)

                    def scores(h, b):
                        x, xl = x_hi[:, h.par], x_lo[:, h.par]
                        q = slice(b * P, (b + 1) * P)
                        if b == 0:
                            pe.wait_ge(x_split, h.at(6, 10))
                        for m in range(2):
                            rows = slice(m * MAP_DIM, (m + 1) * MAP_DIM)
                            pe.wait_ge(exped, h.at(2 * BPH, 2 * b + m + 1))
                            for half in range(2):
                                last = self.product3(pe, ps[:, 2 * m + half], x[rows, QQ, q], xl[rows, QQ, q],
                                                     x[rows, KK, cols(half)], xl[rows, KK, cols(half)], True, True)
                            last.then_inc(scored, 1)

                    def turn(h, b):
                        pe.wait_ge(mixed, h.at(BPH, b + 3))
                        pe.wait_ge(a_split, h.at(BPH, b + 1))
                        for k in range(TB):
                            last = pe.transpose(turned[:, k * P:(k + 1) * P], amap[:, b % 2, k * P:(k + 1) * P], self.ident[:])
                        last.then_inc(a_turned, 1)

                    def times_v(h, half):
                        pe.wait_ge(a_split, h.at(BPH, 4 * half + 5))
                        pe.wait_ge(x_split, h.at(6, 12))
                        pe.wait_ge(out_copied, h.at(2, half + 1))
                        for k in range(TB):
                            v = slice(k * P, (k + 1) * P)
                            last = self.product3(pe, o_acc, x_hi[:, h.par, VV, v], x_lo[:, h.par, VV, v],
                                                 a_hi[:, k], a_lo[:, k], k == 0, k == TB - 1)
                        last.then_inc(out_summed, 1)

                    def body(h, g):
                        for b in range(BPH):
                            if b + 1 < BPH:
                                scores(h, b + 1)
                            elif g:
                                scores(g, 0)
                            if g and b in PREPARES:
                                prepare(g, PREPARES[b])
                            turn(h, b)
                            if g and b in PROJECTS:
                                project(g, PROJECTS[b])
                            if b % 4 == 3:
                                times_v(h, b // 4)
                    first = Head(0, 0)
                    for e in range(6):
                        project(first, e)
                        prepare(first, e)
                    scores(first, 0)
                    all_heads(pe, body)

                @block.gpsimd
                def _(pool):
                    for half in range(2):
                        pool.wait_ge(stored[half], 16 * (HEADS + 1))

    def to_scratch(self, name, first, tiles, func, dst, h_hi, h_lo):
        stored = [self.sem(f"{name}_stored{i}") for i in range(2)]
        with ExitStack() as c:
            buf = self.sb(c, f"{name}_buf", [P, 2, T])

            def act_out(act, j, s, acc, emptied):
                act.wait_ge(stored[s], j * 8 + (16 - 8 * s))
                act.activation(buf[:, s], acc, func).then_inc(emptied, 1)
                act.wait_ge(emptied, j + 3)
                act.dma_start(dst[bass.ds(j, 1)].rearrange("o p t -> (o p) t"), buf[:, s]).then_inc(stored[s], 16)
            with self.nc.Block() as block:
                @block.tensor
                def _(pe):
                    for s in range(2):
                        pe.sem_inc(stored[s], 16)
            self.projection(name, self.a["w_in"], first, h_hi, h_lo, tiles, act_out=act_out)
            with self.nc.Block() as block:
                @block.sync
                def _(sp):
                    for s in range(2):
                        sp.wait_ge(stored[s], 16 * (tiles // 2 + 1))

    def gates(self, h_hi, h_lo):
        self.to_scratch("gates", GA0, 2 * KT, ACT.Sigmoid, self.gate_scr, h_hi, h_lo)

    def gmlp(self, h_hi, h_lo):
        nc, a, ps = self.nc, self.a, self.psum
        self.to_scratch("zu", ZU0, KT, ACT.Gelu_apprx_tanh, self.u_scr, h_hi, h_lo)
        with ExitStack() as c:
            zv = self.sb(c, "zv", [P, KT, T])

            def act_out(act, j, s, acc, emptied):
                act.activation(zv[:, bass.ds(j, 1)].rearrange("p o t -> p (o t)"), acc, ACT.Gelu_apprx_tanh).then_inc(emptied, 1)
            self.projection("zv", a["w_in"], ZV0, h_hi, h_lo, KT, act_out=act_out)
            rstd = self.sb(c, "zv_rstd_t", [P, T])
            mean_done = self.sem("zv_mean")
            centred = self.sem("zv_centred")
            with nc.Block() as block:
                @block.tensor
                def _(pe):
                    for k in range(KT):
                        for half in range(2):
                            last = pe.matmul(ps[:, half], self.ones_mean[:], zv[:, k, half * HALF:(half + 1) * HALF],
                                             start=(k == 0), stop=(k == KT - 1))
                    last.then_inc(mean_done, 1)

                @block.vector
                def _(dve):
                    dve.wait_ge(mean_done, 1)
                    for k in range(KT):
                        dve.tensor_tensor(zv[:, k], zv[:, k], ps[:, 0:2].rearrange("p b t -> p (b t)"), ALU.subtract).then_inc(centred, 1)
            with ExitStack() as s:
                self.mean_square("zv", zv, rstd, self.ones_mean, self.sb(s, "zv_sq", [P, 2, T]))
            self.spatial(zv, rstd)

    def spatial(self, zv, rstd):
        nc, a, ps = self.nc, self.a, self.psum
        G = KT
        turned = ps[:, 0:2].rearrange("p b t -> p (b t)")
        sv = ps[:, 2:4].rearrange("p b t -> p (b t)")
        tables = self.sem("spatial_tables")
        u_loaded = self.sem("spatial_u_loaded")
        w_hi_done = self.sem("spatial_w_hi")
        w_split = self.sem("spatial_w_split")
        normed = self.sem("spatial_normed")
        v_turned = self.sem("spatial_turned")
        v_hi_done = self.sem("spatial_v_hi")
        v_split = self.sem("spatial_v_split")
        mixed = self.sem("spatial_mixed")
        gated = self.sem("spatial_gated")
        stored = self.sem("spatial_stored")
        ln_g, ln_b = self.vecs[:, 4 * KT:5 * KT], self.vecs[:, 5 * KT:6 * KT]
        with ExitStack() as c:
            w = self.sb(c, "sp_w", [P, G, P])
            w_hi = self.sb(c, "sp_w_hi", [P, G, P], F32R)
            w_lo = self.sb(c, "sp_w_lo", [P, G, P], F32R)
            bias = self.sb(c, "sp_bias", [P, G, P])
            u = self.sb(c, "sp_u", [P, T])
            v = self.sb(c, "sp_v", [P, T])
            v_hi = self.sb(c, "sp_v_hi", [P, T], F32R)
            v_lo = self.sb(c, "sp_v_lo", [P, T], F32R)
            sg = self.sb(c, "sp_sg", [P, T])
            with nc.Block() as block:
                @block.sync
                def _(sp):
                    sp.dma_start(w[:].rearrange("q g p -> q (g p)"), a["w_spatial"]).then_inc(tables, 16)
                    sp.dma_start(bias[:].rearrange("q g p -> q (g p)"), a["b_spatial"].to_broadcast([P, G * P])).then_inc(tables, 16)
                    with sp.Fori(0, G) as g:
                        at = sp.snap(g + 0)
                        free = sp.snap(g * 2 + 1)
                        ready = sp.snap(g * 2 + 3)
                        sp.wait_ge(gated, free)
                        sp.dma_start(u[:], self.u_scr[bass.ds(at, 1)].rearrange("o p t -> (o p) t")).then_inc(u_loaded, 16)
                        sp.wait_ge(gated, ready)
                        sp.dma_start(self.sg_scr[bass.ds(at, 1)].rearrange("o p t -> (o p) t"), sg[:]).then_inc(stored, 16)
                    sp.wait_ge(stored, 16 * (G + 1))

                @block.scalar
                def _(act):
                    act.wait_ge(tables, 32)
                    act.activation(w_hi[:], w[:], ACT.Copy).then_inc(w_hi_done, 1)
                    with act.Fori(0, G) as g:
                        act.wait_ge(v_turned, g + 1)
                        act.wait_ge(mixed, g + 1)
                        act.activation(v_hi[:], turned, ACT.Copy).then_inc(v_hi_done, 1)

                @block.vector
                def _(dve):
                    dve.sem_inc(gated, 1)
                    dve.wait_ge(w_hi_done, 1)
                    dve.tensor_tensor(w_lo[:], w[:], w_hi[:].bitcast(F32), ALU.subtract).then_inc(w_split, 1)
                    with dve.Fori(0, G) as g:
                        dve.tensor_tensor(v[:], zv[:, bass.ds(g, 1)].rearrange("p o t -> p (o t)"), rstd[:], ALU.mult).then_inc(normed, 1)
                        dve.wait_ge(normed, g * 2 + 1)
                        dve.tensor_scalar(v[:], v[:], ln_g[:, bass.ds(g, 1)], ln_b[:, bass.ds(g, 1)], ALU.mult, ALU.add).then_inc(normed, 1)
                        dve.wait_ge(v_hi_done, g + 1)
                        dve.tensor_tensor(v_lo[:], turned, v_hi[:].bitcast(F32), ALU.subtract).then_inc(v_split, 1)
                        dve.wait_ge(mixed, g + 2)
                        dve.wait_ge(stored, g * 16 + 16)
                        dve.tensor_tensor(sg[:].rearrange("h (c p) -> h c p", p=P), sv.rearrange("h (c p) -> h c p", p=P),
                                          bias[:, bass.ds(g, 1)].to_broadcast([P, TB, P]), ALU.add).then_inc(gated, 1)
                        dve.wait_ge(gated, g * 2 + 2)
                        dve.wait_ge(u_loaded, g * 16 + 16)
                        dve.tensor_tensor(sg[:], sg[:], u[:], ALU.mult).then_inc(gated, 1)

                @block.tensor
                def _(pe):
                    pe.sem_inc(mixed, 1)
                    pe.sem_inc(stored, 16)
                    pe.wait_ge(w_split, 1)
                    with pe.Fori(0, G) as g:
                        pe.wait_ge(normed, g * 2 + 2)
                        for k in range(TB):
                            last = pe.transpose(turned[:, k * P:(k + 1) * P], v[:, k * P:(k + 1) * P], self.ident[:])
                        last.then_inc(v_turned, 1)
                        pe.wait_ge(v_split, g + 1)
                        for k in range(TB):
                            cols = slice(k * P, (k + 1) * P)
                            wh = w_hi[:, bass.ds(g, 1)].rearrange("q o p -> q (o p)")
                            wl = w_lo[:, bass.ds(g, 1)].rearrange("q o p -> q (o p)")
                            pe.matmul(sv[:, cols], v_hi[:, cols], wh, start=True, stop=False)
                            pe.matmul(sv[:, cols], v_hi[:, cols], wl, start=False, stop=False)
                            last = pe.matmul(sv[:, cols], v_lo[:, cols], wh, start=False, stop=True)
                        last.then_inc(mixed, 1)

    def split(self, name, src, hi, lo):
        hi_done = self.sem(f"{name}_split_hi")
        lo_done = self.sem(f"{name}_split_lo")
        with self.nc.Block() as block:
            @block.scalar
            def _(act):
                for k in range(KT):
                    act.activation(hi[:, k], src[:, k], ACT.Copy).then_inc(hi_done, 1)

            @block.vector
            def _(dve):
                for k in range(KT):
                    dve.wait_ge(hi_done, k + 1)
                    dve.tensor_tensor(lo[:, k], src[:, k], hi[:, k].bitcast(F32), ALU.subtract).then_inc(lo_done, 1)

    def branches(self, wide, m_hi, m_lo):
        with ExitStack() as c:
            with ExitStack() as s:
                o = self.sb(s, "o_all", [P, HEADS, T])
                self.load(o, self.o_scr.rearrange("h p t -> p h t"), "o")
                self.head_norm(o)
                self.split("o", o, m_hi, m_lo)
            self.branch("attn", "w_attn", 0, wide, m_hi, m_lo)
            sg = self.sb(c, "sg_all", [P, KT, T])
            self.load(sg, self.sg_scr.rearrange("h p t -> p h t"), "sg")
            self.split("sg", sg, m_hi, m_lo)
            self.branch("spat", "w_gmlp", KT, wide, m_hi, m_lo)
            self.split("mix", wide, m_hi, m_lo)

    def head_norm(self, o):
        nc, ps = self.nc, self.psum
        squared = self.sem("head_squared")
        summed = self.sem("head_summed")
        eps_added = self.sem("head_eps")
        rooted = self.sem("head_rooted")
        inverse = self.sem("head_inverse")
        normed = self.sem("head_normed")
        with ExitStack() as c:
            sq = self.sb(c, "head_sq", [P, 2, T])
            rstd = self.sb(c, "head_rstd", [P, 2, T])
            with nc.Block() as block:
                @block.scalar
                def _(act):
                    def square(h):
                        if h >= 2:
                            act.wait_ge(summed, h - 1)
                        act.activation(sq[:, h % 2], o[:, h], ACT.Square).then_inc(squared, 1)
                    square(0)
                    for h in range(HEADS):
                        if h + 1 < HEADS:
                            square(h + 1)
                        act.wait_ge(eps_added, h + 1)
                        act.activation(rstd[:, h % 2], rstd[:, h % 2], ACT.Sqrt).then_inc(rooted, 1)

                @block.tensor
                def _(pe):
                    for h in range(HEADS):
                        pe.wait_ge(squared, h + 1)
                        if h >= 2:
                            pe.wait_ge(eps_added, h - 1)
                        for half in range(2):
                            last = pe.matmul(ps[:, 2 * (h % 2) + half], self.ones_head[:], sq[:, h % 2, half * HALF:(half + 1) * HALF],
                                             start=True, stop=True)
                        last.then_inc(summed, 1)

                @block.vector
                def _(dve):
                    def add_eps(h):
                        dve.wait_ge(summed, h + 1)
                        if h >= 2:
                            dve.wait_ge(normed, 2 * (h - 1))
                        dve.tensor_scalar(rstd[:, h % 2], ps[:, 2 * (h % 2):2 * (h % 2) + 2].rearrange("p b t -> p (b t)"),
                                          EPS, None, ALU.add).then_inc(eps_added, 1)
                    add_eps(0)
                    for h in range(HEADS):
                        if h + 1 < HEADS:
                            add_eps(h + 1)
                        dve.wait_ge(rooted, h + 1)
                        dve.reciprocal(rstd[:, h % 2], rstd[:, h % 2]).then_inc(inverse, 1)
                        dve.wait_ge(inverse, h + 1)
                        dve.tensor_tensor(o[:, h], o[:, h], rstd[:, h % 2], ALU.mult).then_inc(normed, 1)
                        dve.wait_ge(normed, 2 * h + 1)
                        dve.tensor_scalar(o[:, h], o[:, h], self.subln_gain[:, 0:1], None, ALU.mult).then_inc(normed, 1)

    def branch(self, name, weights, gate0, wide, x_hi, x_lo):
        g_loaded = [self.sem(f"{name}_gate_loaded{i}") for i in range(2)]
        gated = self.sem(f"{name}_gated")
        with ExitStack() as c:
            gate = self.sb(c, f"{name}_gate", [P, 2, T])
            term = self.sb(c, f"{name}_term", [P, 2, T])

            def dve_out(dve, j, s, acc, emptied):
                dve.wait_ge(g_loaded[s], j * 8 + (16 - 8 * s))
                to = wide[:, bass.ds(j, 1)].rearrange("p o t -> p (o t)")
                if gate0 == 0:
                    dve.tensor_tensor(to, acc, gate[:, s], ALU.mult).then_inc(emptied, 1)
                else:
                    dve.tensor_tensor(term[:, s], acc, gate[:, s], ALU.mult).then_inc(emptied, 1)
                    dve.wait_ge(emptied, j + 3)
                    dve.tensor_tensor(to, to, term[:, s], ALU.add).then_inc(gated, 1)

            def pool_program(pool, emptied):
                with pool.Fori(0, KT // 2) as it:
                    at = [pool.snap(it * 2 + (s + gate0)) for s in range(2)]
                    for s in range(2):
                        pool.wait_ge(emptied, it * 2 + (s + 1))
                        pool.dma_start(gate[:, s], self.gate_scr[bass.ds(at[s], 1)].rearrange("o p t -> (o p) t")).then_inc(g_loaded[s], 16)
            self.projection(name, self.a[weights], 0, x_hi, x_lo, KT, dve_out=dve_out, pool_program=pool_program)

    def out_projection(self, wide, m_hi, m_lo):
        def act_out(act, j, s, acc, emptied):
            act.activation(wide[:, bass.ds(j, 1)].rearrange("p o t -> p (o t)"), acc, ACT.Copy).then_inc(emptied, 1)
        self.projection("out", self.a["w_out"], 0, m_hi, m_lo, KT, act_out=act_out)

    def add_normed(self, name, y, coef, base_dram, x1, dst_dram):
        nc = self.nc
        loaded = self.sem(f"{name}_base_loaded")
        scaled = self.sem(f"{name}_scaled")
        added = self.sem(f"{name}_added")
        stored = self.sem(f"{name}_stored")
        with ExitStack() as c:
            rstd = self.sb(c, f"{name}_rstd_t", [P, T])
            sq = self.sb(c, f"{name}_sq", [P, 2, T])
            self.mean_square(name, y, rstd, self.ones_mean, sq)
            with nc.Block() as block:
                @block.sync
                def _(sp):
                    sp.dma_start(x1[:], base_dram).then_inc(loaded, 16)
                    for k in range(KT):
                        sp.wait_ge(added, k + 1)
                        sp.dma_start(dst_dram[:, k], x1[:, k]).then_inc(stored, 16)
                    sp.wait_ge(stored, 16 * KT)

                @block.vector
                def _(dve):
                    for k in range(KT):
                        dve.tensor_tensor(y[:, k], y[:, k], rstd[:], ALU.mult).then_inc(scaled, 1)
                    dve.wait_ge(loaded, 16)
                    for k in range(KT):
                        dve.wait_ge(scaled, k + 1)
                        dve.scalar_tensor_tensor(x1[:, k], y[:, k], coef[:, k:k + 1], x1[:, k], ALU.mult, ALU.add).then_inc(added, 1)

    def residual(self, wide, x1):
        self.add_normed("mix", wide, self.coef[:, KT:2 * KT], self.a["xT"].rearrange("(k p) t -> p k t", p=P), x1,
                        self.x1_scr.rearrange("k p t -> p k t"))

    def finish(self, wide):
        with ExitStack() as c:
            x1 = self.sb(c, "x_out", [P, KT, T])
            self.add_normed("final", wide, self.coef[:, 3 * KT:4 * KT], self.x1_scr.rearrange("k p t -> p k t"), x1,
                            self.a["out"].rearrange("(k p) t -> p k t", p=P))

    def route(self, h2_hi, h2_lo):
        with ExitStack() as c:
            vals = self.sb(c, "top_vals", [P, TB, SIDES, TOPK])
            idxs = self.sb(c, "top_idxs", [P, TB, SIDES, TOPK], F16)
            self.side_tops(h2_hi, h2_lo, vals, idxs)
            self.stage_end()
            self.scatter_weights(vals, idxs, h2_hi, h2_lo)
            self.stage_end()

    def side_tops(self, h2_hi, h2_lo, vals, idxs):
        nc, a, ps = self.nc, self.a, self.psum
        keys_loaded = self.sem("keys_loaded")
        keys_hi_done = self.sem("keys_hi")
        keys_split = self.sem("keys_split")
        q_hi_done = self.sem("rq_hi")
        q_split = self.sem("rq_emptied_too")
        scored = self.sem("rq_scored")
        tops = self.sem("rq_tops")
        held = self.sem("rq_held")
        NTOPS = 5 * TB + 2
        with ExitStack() as c:
            k_raw = self.sb(c, "k_raw", [P, SIDES, KEYS])
            k_hi = self.sb(c, "k_hi", [P, SIDES, KEYS], F32R)
            k_lo = self.sb(c, "k_lo", [P, SIDES, KEYS], F32R)
            with nc.Block() as block:
                @block.sync
                def _(sp):
                    sp.dma_start(k_raw[:].rearrange("d s n -> d (s n)"), a["keysT"]).then_inc(keys_loaded, 16)

                @block.scalar
                def _(act):
                    act.wait_ge(keys_loaded, 16)
                    act.activation(k_hi[:], k_raw[:], ACT.Copy).then_inc(keys_hi_done, 1)

                @block.vector
                def _(dve):
                    dve.wait_ge(keys_hi_done, 1)
                    dve.tensor_tensor(k_lo[:], k_raw[:], k_hi[:].bitcast(F32), ALU.subtract).then_inc(keys_split, 1)
            q_hi = self.sb(c, "rq_hi_t", [P, 2, T], F32R)
            q_lo = self.sb(c, "rq_lo_t", [P, 2, T], F32R)
            work = self.sb(c, "rq_work", [P, TB, KEYS])
            top_v = self.sb(c, "rq_top_v", [P, TB, TOPK])
            top_i = self.sb(c, "rq_top_i", [P, TB, TOPK], U32)
            score = [ps[:, 4 + 2 * s:6 + 2 * s].rearrange("p b (c n) -> p (b c) n", n=KEYS) for s in range(2)]

            def act_out(act, j, s, acc, emptied):
                act.wait_ge(scored, j + 1)
                act.activation(q_hi[:, s], acc, ACT.Copy).then_inc(q_hi_done, 1)

            def dve_out(dve, j, s, acc, emptied):
                dve.wait_ge(q_hi_done, j + 1)
                dve.tensor_tensor(q_lo[:, s], acc, q_hi[:, s].bitcast(F32), ALU.subtract).then_inc(emptied, 1)

            def top(dve, j, s):
                n = [0]

                def all_so_far():
                    dve.wait_ge(tops, j * NTOPS + (n[0] + 2 * NTOPS))
                    dve.sem_inc(held, 1)

                def done(ins):
                    ins.then_inc(tops, 1)
                    n[0] += 1
                dve.wait_ge(scored, j + 3)
                all_so_far()
                for b in range(TB):
                    done(dve.max(top_v[:, b, 0:8], score[s][:, b]))
                all_so_far()
                for b in range(TB):
                    done(dve.match_replace(work[:, b], top_v[:, b, 0:8], score[s][:, b], LOWEST))
                for b in range(TB):
                    done(dve.max_index(top_i[:, b, 0:8], top_v[:, b, 0:8], score[s][:, b]))
                all_so_far()
                for b in range(TB):
                    done(dve.max(top_v[:, b, 8:16], work[:, b]))
                all_so_far()
                for b in range(TB):
                    done(dve.max_index(top_i[:, b, 8:16], top_v[:, b, 8:16], work[:, b]))
                all_so_far()
                done(dve.tensor_copy(vals[:, :, bass.ds(j, 1)].rearrange("p b o k -> p b (o k)"), top_v[:]))
                done(dve.tensor_copy(idxs[:, :, bass.ds(j, 1)].rearrange("p b o k -> p b (o k)"), top_i[:]))
                assert n[0] == NTOPS

            def pe_after(pe, j, s, emptied):
                pe.wait_ge(emptied, j + 3)
                pe.wait_ge(tops, j * NTOPS + NTOPS)
                kh = k_hi[:, bass.ds(j, 1)].rearrange("d o n -> d (o n)")
                kl = k_lo[:, bass.ds(j, 1)].rearrange("d o n -> d (o n)")
                for b in range(TB):
                    q = slice(b * P, (b + 1) * P)
                    pe.matmul(score[s][:, b], q_hi[:, s, q], kh, start=True, stop=False)
                    pe.matmul(score[s][:, b], q_hi[:, s, q], kl, start=False, stop=False)
                    last = pe.matmul(score[s][:, b], q_lo[:, s, q], kh, start=False, stop=True)
                last.then_inc(scored, 1)
            with nc.Block() as block:
                @block.vector
                def _(dve):
                    dve.sem_inc(tops, 2 * NTOPS)
                    dve.sem_inc(scored, 2)
            self.projection("rq", a["w_peer"], 0, h2_hi, h2_lo, SIDES, act_out=act_out, dve_out=dve_out,
                            pe_after=pe_after, dve_after=top)

    def scatter_weights(self, vals, idxs, h2_hi, h2_lo):
        nc, a, ps = self.nc, self.a, self.psum
        SEL = HEADS * TOPK
        GROUP, QUAD = 8, 4
        PIECES = 4
        GROUPS = P // GROUP
        QUADS = P // QUAD
        PER_BLOCK = EARLY // TB
        chain = self.sem("sc_chain")
        held = self.sem("sc_held")
        exp_in = self.sem("sc_exp_in")
        exp_out = self.sem("sc_exp_out")
        chosen = self.sem("sc_chosen")
        turned = self.sem("sc_turned")
        first_hot = self.sem("sc_first_hot")
        onehots = self.sem("sc_onehots")
        matrices = self.sem("sc_matrices")
        staged = self.sem("sc_staged")
        stored = self.sem("sc_stored")
        iotas = self.sem("sc_iotas")
        u_loaded = self.sem("sc_u_loaded")
        u_hi_done = self.sem("sc_u_hi")
        u_split = self.sem("sc_u_split")
        hidden = self.sem("sc_hidden")
        gelu_done = self.sem("sc_gelu")
        h_stored = self.sem("sc_h_stored")
        hid = [ps[:, 2 * s:2 * s + 2].rearrange("p b t -> p (b t)") for s in range(2)]
        with ExitStack() as c:
            cand = self.sb(c, "sc_cand", [P, HEADS, TOPK, TOPK])
            cand2 = self.sb(c, "sc_cand2", [P, HEADS, TOPK * TOPK])
            best = self.sb(c, "sc_best", [P, HEADS, TOPK])
            pos = self.sb(c, "sc_pos", [P, HEADS, TOPK], U32)
            pos_i = self.sb(c, "sc_pos_i", [P, 2, SEL], U32)
            pos_h = self.sb(c, "sc_pos_h", [P, 2, SEL], F16)
            norm = self.sb(c, "sc_norm", [P, 2, HEADS])
            picks = self.sb(c, "sc_picks", [P, 3, SEL])
            scaled = self.sb(c, "sc_scaled", [SEL, P])
            rows = self.sb(c, "sc_rows_t", [SEL, 4, P], F16)
            iota16 = self.sb(c, "sc_iota16", [P, TOPK], F16)
            key_of = self.sb(c, "sc_key_of", [SEL, KEYS, GROUP], F16)
            first = self.sb(c, "sc_first", [SEL, 2, KEYS, GROUP], F16)
            second = self.sb(c, "sc_second", [SEL, 2, KEYS, GROUP], F16)
            w_hi = self.sb(c, "sc_w_hi", [SEL, 2, KEYS, GROUP], F16)
            w_lo = self.sb(c, "sc_w_lo", [SEL, 2, KEYS, GROUP], F16)
            stage = self.sb(c, "sc_stage", [P, KEYS, P])
            u_raw = self.sb(c, "sc_u_raw", [P, D])
            u_hi = self.sb(c, "sc_u_hi_t", [P, 2, KT, P], F32R)
            u_lo = self.sb(c, "sc_u_lo_t", [P, 2, KT, P], F32R)
            gelu = self.sb(c, "sc_gelu_t", [P, T])
            flat = lambda w, s: w[:, s].rearrange("p k n -> p (k n)")
            with nc.Block() as block:
                @block.sync
                def _(sp):
                    dst = self.route_scr.rearrange("i j (b t) -> b j i t", t=P)

                    def load(at):
                        sp.dma_start(u_raw[:], a["peer_uT"][bass.ds(at, 1)].rearrange("o p n -> (o p) n")).then_inc(u_loaded, 16)
                    def blocks_loads(b):
                        snap = sp.snap if not isinstance(b, int) else (lambda value: value)
                        chunk = [snap(b * PER_BLOCK + i) for i in (4, 5, 6)]
                        free = [snap(b * PER_BLOCK + (i + 1)) for i in (4, 5, 6)]
                        for i in range(3):
                            sp.wait_ge(u_split, free[i])
                            load(chunk[i])

                    def store(at, piece):
                        k = slice(piece * KEYS // PIECES, (piece + 1) * KEYS // PIECES)
                        sp.dma_start(dst[bass.ds(at, 1), :, k].rearrange("o j i t -> (o j) i t"), stage[:, k]).then_inc(stored, 16)
                    load(0)
                    for j in range(1, 4):
                        sp.wait_ge(u_split, j + 1)
                        load(j)
                    with sp.Fori(0, TB - 1) as b:
                        at = sp.snap(b + 0)
                        blocks_loads(b)
                        ready = sp.snap(b * QUADS + (QUADS + 4))
                        next_chunk = [sp.snap(b * PER_BLOCK + i) for i in (7, 8)]
                        next_free = [sp.snap(b * PER_BLOCK + (i + 1)) for i in (7, 8)]
                        piece_stored = [sp.snap(b * 16 * PIECES + 16 * (i + 2)) for i in range(PIECES)]
                        sp.wait_ge(staged, ready)
                        store(at, 0)
                        sp.wait_ge(u_split, next_free[0])
                        load(next_chunk[0])
                        sp.wait_ge(stored, piece_stored[0])
                        store(at, 1)
                        sp.wait_ge(stored, piece_stored[1])
                        store(at, 2)
                        sp.wait_ge(u_split, next_free[1])
                        load(next_chunk[1])
                        sp.wait_ge(stored, piece_stored[2])
                        store(at, 3)
                    blocks_loads(TB - 1)
                    sp.wait_ge(staged, QUADS * TB + 4)
                    for piece in range(PIECES):
                        store(TB - 1, piece)
                    sp.wait_ge(stored, 16 * (PIECES * TB + 1))
                    sp.wait_ge(h_stored, 16 * (EARLY + 1))

                @block.gpsimd
                def _(pool):
                    pool.iota(iota16[:], [[1, TOPK]], base=0, channel_multiplier=0, allow_small_or_imprecise_dtypes=True).then_inc(iotas, 1)
                    pool.iota(key_of[:], [[1, KEYS], [0, GROUP]], base=0, channel_multiplier=0, allow_small_or_imprecise_dtypes=True).then_inc(iotas, 1)
                    pool.sem_inc(u_split, 1)

                    def split(j, s):
                        pool.wait_ge(u_hi_done, j + 1)
                        pool.tensor_tensor(flat(u_lo, s), u_raw[:], flat(u_hi, s).bitcast(F32), ALU.subtract).then_inc(u_split, 1)
                    split(0, 0)
                    split(1, 1)
                    with pool.Fori(0, TB // 2) as two:
                        for i in range(2 * PER_BLOCK):
                            split(two * (2 * PER_BLOCK) + (i + 2), i % 2)

                @block.vector
                def _(dve):
                    dve.sem_inc(stored, 16)
                    dve.sem_inc(h_stored, 16)
                    dve.sem_inc(chain, 1)
                    dve.sem_inc(onehots, 2)
                    dve.wait_ge(iotas, 2)
                    LINKS = 56
                    with dve.Fori(0, TB) as b:
                        n = [0]

                        def do(ins):
                            n[0] += 1
                            ins.then_inc(chain, 1)

                        def all_so_far():
                            dve.wait_ge(chain, b * LINKS + (n[0] + 1))
                            dve.sem_inc(held, 1)
                        shape = [P, HEADS, TOPK, TOPK]
                        val = vals[:, bass.ds(b, 1)].rearrange("p o (h s) k -> p (o h) s k", s=2)
                        all_so_far()
                        do(dve.tensor_tensor(cand[:], val[:, :, 0].unsqueeze(3).to_broadcast(shape), val[:, :, 1].unsqueeze(2).to_broadcast(shape), ALU.add))
                        all_so_far()
                        cflat = [cand[:, h].rearrange("p a b -> p (a b)") for h in range(HEADS)]
                        for h in range(HEADS):
                            do(dve.max(best[:, h, 0:8], cflat[h]))
                        all_so_far()
                        for h in range(HEADS):
                            do(dve.match_replace(cand2[:, h], best[:, h, 0:8], cflat[h], LOWEST))
                        for h in range(HEADS):
                            do(dve.max_index(pos[:, h, 0:8], best[:, h, 0:8], cflat[h]))
                        all_so_far()
                        for h in range(HEADS):
                            do(dve.max(best[:, h, 8:16], cand2[:, h]))
                        all_so_far()
                        weight = picks[:, 2].rearrange("p (h k) -> p h k", k=TOPK)
                        dve.tensor_tensor(weight, best[:], best[:, :, 0:1].to_broadcast([P, HEADS, TOPK]), ALU.subtract).then_inc(exp_in, 1)
                        for h in range(HEADS):
                            do(dve.max_index(pos[:, h, 8:16], best[:, h, 8:16], cand2[:, h]))
                        all_so_far()
                        pflat = pos[:].rearrange("p h k -> p (h k)")
                        do(dve.tensor_single_scalar(pos_i[:, 0], pflat, 4, ALU.logical_shift_right))
                        do(dve.tensor_single_scalar(pos_i[:, 1], pflat, 15, ALU.bitwise_and))
                        all_so_far()
                        do(dve.tensor_copy(pos_h[:], pos_i[:]))
                        all_so_far()
                        half = lambda w: w.bitcast(F16)[:, 0:SEL * TOPK]
                        eq_flat = half(cand2[:].rearrange("p h c -> p (h c)"))
                        prod_flat = half(cand[:].rearrange("p h k a -> p (h k a)"))
                        eq = eq_flat.rearrange("p (k a) -> p k a", a=TOPK)
                        eq4 = eq_flat.rearrange("p (h k a) -> p h k a", h=HEADS, a=TOPK)
                        prod = prod_flat.rearrange("p (k a) -> p k a", a=TOPK)
                        prod4 = prod_flat.rearrange("p (h k a) -> p h k a", h=HEADS, a=TOPK)
                        idx = idxs[:, bass.ds(b, 1)].rearrange("p o (h s) k -> p (o h) s k", s=2)
                        for side in range(2):
                            do(dve.tensor_tensor(eq, pos_h[:, side].unsqueeze(2).to_broadcast([P, SEL, TOPK]),
                                                 iota16[:].unsqueeze(1).to_broadcast([P, SEL, TOPK]), ALU.is_equal))
                            all_so_far()
                            do(dve.tensor_tensor(prod4, eq4, idx[:, :, side].unsqueeze(2).to_broadcast(shape), ALU.mult))
                            all_so_far()
                            do(dve.tensor_reduce(picks[:, side], prod, AXX, ALU.add))
                        dve.wait_ge(exp_out, b + 1)
                        do(dve.tensor_reduce(norm[:, 0], weight, AXX, ALU.add))
                        all_so_far()
                        do(dve.reciprocal(norm[:, 1], norm[:, 0]))
                        all_so_far()
                        dve.tensor_tensor(weight, weight, norm[:, 1].unsqueeze(2).to_broadcast([P, HEADS, TOPK]), ALU.mult).then_inc(chosen, 1)
                        dve.wait_ge(turned, b + 1)
                        do(dve.tensor_copy(rows[:, 0:2].rearrange("k a t -> k (a t)"), ps[:, 4, 0:2 * P]))
                        do(dve.tensor_scalar(scaled[:], ps[:, 4, 2 * P:3 * P], WEIGHT_SCALE, None, ALU.mult))
                        all_so_far()
                        do(dve.tensor_copy(rows[:, 2], scaled[:]))
                        all_so_far()
                        do(dve.tensor_tensor(rows[:, 3], scaled[:], rows[:, 2], ALU.subtract))
                        all_so_far()
                        for q in range(GROUPS):
                            s = q % 2
                            row = lambda r: rows[:, r, q * GROUP:(q + 1) * GROUP].unsqueeze(1).to_broadcast([SEL, KEYS, GROUP])
                            dve.wait_ge(onehots, b * GROUPS + (q + 1))
                            dve.wait_ge(matrices, b * QUADS + (2 * q + 2))
                            dve.tensor_tensor(first[:, s], key_of[:], row(0), ALU.is_equal).then_inc(first_hot, 1)
                            dve.tensor_tensor(second[:, s], key_of[:], row(1), ALU.is_equal)
                            dve.wait_ge(first_hot, b * GROUPS + (q + 1))
                            dve.tensor_tensor(w_hi[:, s], first[:, s], row(2), ALU.mult)
                            dve.tensor_tensor(w_lo[:, s], first[:, s], row(3), ALU.mult).then_inc(onehots, 1)
                        dve.wait_ge(onehots, b * GROUPS + (GROUPS + 2))
                        assert n[0] == LINKS, n[0]

                @block.scalar
                def _(act):
                    def split(j, s):
                        act.wait_ge(u_loaded, j * 16 + 16)
                        act.activation(flat(u_hi, s), u_raw[:], ACT.Copy).then_inc(u_hi_done, 1)

                    def chunk(j, s):
                        act.wait_ge(hidden, j + 1)
                        act.wait_ge(h_stored, j * 16 + 16)
                        act.activation(gelu[:], hid[s], ACT.Gelu_apprx_tanh).then_inc(gelu_done, 1)
                        act.wait_ge(gelu_done, j + 3)
                        act.dma_start(self.h_scr[bass.ds(j, 1)].rearrange("o p t -> (o p) t"), gelu[:]).then_inc(h_stored, 16)
                        split(j + 2, s)
                    split(0, 0)
                    split(1, 1)
                    weight = picks[:, 2]

                    def block_of_tokens(b, j, odd):
                        chunk(j, odd)
                        act.wait_ge(exp_in, b + 1)
                        act.activation(weight, weight, ACT.Exp).then_inc(exp_out, 1)
                        chunk(j + 1, 1 - odd)
                        chunk(j + 2, odd)
                        act.wait_ge(stored, b * (16 * PIECES) + 16)
                        for q in range(QUADS):
                            act.wait_ge(matrices, b * QUADS + (q + 5))
                            act.activation(stage[:, :, q * QUAD:(q + 1) * QUAD].rearrange("j i t -> j t i"),
                                           ps[:, 4 + q % 4].rearrange("j (t i) -> j t i", i=KEYS), ACT.Copy).then_inc(staged, 1)
                            if q == QUADS // 2:
                                chunk(j + 3, 1 - odd)
                        chunk(j + 4, odd)
                    with act.Fori(0, TB // 2) as two:
                        for odd in range(2):
                            block_of_tokens(two * 2 + odd, two * (2 * PER_BLOCK) + odd * PER_BLOCK, odd)

                @block.tensor
                def _(pe):
                    pe.sem_inc(matrices, 4)
                    pe.sem_inc(staged, 4)
                    pe.sem_inc(gelu_done, 2)

                    def up_piece(s, k, half):
                        t = slice(half * HALF, (half + 1) * HALF)
                        return self.product3(pe, ps[:, 2 * s + half], u_hi[:, s, k], u_lo[:, s, k], h2_hi[:, k, t], h2_lo[:, k, t],
                                             k == 0, k == KT - 1)

                    def up_ready(j):
                        pe.wait_ge(u_split, j + 2)
                        pe.wait_ge(gelu_done, j + 1)
                    def block_of_tokens(b, j, odd):
                        for i in range(3):
                            up_ready(j + i)
                            for half in range(2):
                                for k in range(KT):
                                    last = up_piece((odd + i) % 2, k, half)
                            last.then_inc(hidden, 1)
                        pe.wait_ge(chosen, b + 1)
                        pe.wait_ge(staged, b * QUADS + 4)
                        for i in range(3):
                            last = pe.transpose(ps[:, 4, i * P:(i + 1) * P], picks[:, i], self.ident[:])
                        last.then_inc(turned, 1)
                        for q in range(GROUPS):
                            i, at = divmod(q, GROUPS // 2)
                            if at == 0:
                                up_ready(j + (3 + i))
                            for piece in (2 * at, 2 * at + 1):
                                last = up_piece((odd + 3 + i) % 2, piece % KT, piece // KT)
                            if at == GROUPS // 2 - 1:
                                last.then_inc(hidden, 1)
                            pe.wait_ge(onehots, b * GROUPS + (q + 3))
                            s = q % 2
                            for half in range(2):
                                quad = 2 * q + half
                                pe.wait_ge(staged, b * QUADS + (quad + 1))
                                for t in range(QUAD):
                                    to = ps[:, 4 + quad % 4, t * KEYS:(t + 1) * KEYS]
                                    tok = half * QUAD + t
                                    pe.matmul(to, second[:, s, :, tok], w_hi[:, s, :, tok], start=True, stop=False)
                                    last = pe.matmul(to, second[:, s, :, tok], w_lo[:, s, :, tok], start=False, stop=True)
                                last.then_inc(matrices, 1)
                    with pe.Fori(0, TB // 2) as two:
                        for odd in range(2):
                            block_of_tokens(two * 2 + odd, two * (2 * PER_BLOCK) + odd * PER_BLOCK, odd)

    def experts(self, h2_hi, h2_lo, y):
        nc, a, ps = self.nc, self.a, self.psum
        C = KEYS
        E = EARLY
        u_loaded = [self.sem(f"ex_u_loaded{i}") for i in range(2)]
        v_loaded = [self.sem(f"ex_v_loaded{i}") for i in range(2)]
        g_loaded = [self.sem(f"ex_g_loaded{i}") for i in range(2)]
        u_hi_done = self.sem("ex_u_hi")
        u_split = self.sem("ex_u_split")
        v_hi_done = self.sem("ex_v_hi")
        v_split = self.sem("ex_v_split")
        hidden = self.sem("ex_hidden")
        gelu_done = self.sem("ex_gelu")
        weighted = self.sem("ex_weighted")
        a_hi_done = self.sem("ex_a_hi")
        a_split = self.sem("ex_a_split")
        summed = self.sem("ex_summed")
        added = self.sem("ex_added")
        zeroed = self.sem("ex_zeroed")
        TILES = 2 * KT
        hid = [ps[:, 2 * s:2 * s + 2].rearrange("p b t -> p (b t)") for s in range(2)]
        with ExitStack() as c:
            u_raw = self.sb(c, "u_raw", [P, 2, D])
            u_hi = self.sb(c, "u_hi", [P, 2, KT, P], F32R)
            u_lo = self.sb(c, "u_lo", [P, 2, KT, P], F32R)
            v_raw = self.sb(c, "v_raw", [P, 2, D])
            v_hi = self.sb(c, "v_hi", [P, 4, D], F32R)
            v_lo = self.sb(c, "v_lo", [P, 4, D], F32R)
            g = self.sb(c, "g", [P, 2, T])
            act_hi = self.sb(c, "act_hi", [P, 4, T], F32R)
            act_lo = self.sb(c, "act_lo", [P, 4, T], F32R)
            flat = lambda w, s: w[:, s].rearrange("p k n -> p (k n)")

            def arrivals(j, s):
                return j * 8 + (16 - 8 * s)
            with nc.Block() as block:
                @block.sync
                def _(sp):
                    def fetch(src, at, to, arrived):
                        sp.dma_start(to, src[bass.ds(at, 1)].rearrange("o p n -> (o p) n")).then_inc(arrived, 16)

                    with sp.Fori(0, E // 2) as it:
                        at = [sp.snap(it * 2 + s) for s in range(2)]
                        free = [sp.snap(it * 2 + (s + 1)) for s in range(2)]
                        for s in range(2):
                            sp.wait_ge(a_split, free[s])
                            fetch(self.route_scr, at[s], g[:, s], g_loaded[s])
                            fetch(self.h_scr, at[s], u_raw[:, s], u_loaded[s])
                            sp.wait_ge(v_split, free[s])
                            fetch(a["peer_v"], at[s], v_raw[:, s], v_loaded[s])
                    for s in range(2):
                        sp.wait_ge(a_split, E + s + 1)
                        fetch(a["peer_uT"], E + s, u_raw[:, s], u_loaded[s])
                        fetch(self.route_scr, E + s, g[:, s], g_loaded[s])
                        sp.wait_ge(v_split, E + s + 1)
                        fetch(a["peer_v"], E + s, v_raw[:, s], v_loaded[s])
                    with sp.Fori(E // 2 + 1, C // 2) as it:
                        at = [sp.snap(it * 2 + s) for s in range(2)]
                        free = [sp.snap(it * 2 + (s + 1)) for s in range(2)]
                        u_free = [sp.snap(it * 2 + (s + 1 - E)) for s in range(2)]
                        for s in range(2):
                            sp.wait_ge(u_split, u_free[s])
                            fetch(a["peer_uT"], at[s], u_raw[:, s], u_loaded[s])
                            sp.wait_ge(a_split, free[s])
                            fetch(self.route_scr, at[s], g[:, s], g_loaded[s])
                            sp.wait_ge(v_split, free[s])
                            fetch(a["peer_v"], at[s], v_raw[:, s], v_loaded[s])

                @block.scalar
                def _(act):
                    def split_u(j, s):
                        act.wait_ge(u_loaded[s], arrivals(j, s))
                        act.activation(flat(u_hi, s), u_raw[:, s], ACT.Copy).then_inc(u_hi_done, 1)

                    def parts(j, ring):
                        s = ring % 2
                        act.wait_ge(weighted, j + 3)
                        act.activation(act_hi[:, ring], g[:, s], ACT.Copy).then_inc(a_hi_done, 1)
                        act.wait_ge(v_loaded[s], arrivals(j, s))
                        act.activation(v_hi[:, ring], v_raw[:, s], ACT.Copy).then_inc(v_hi_done, 1)

                    def late(j, ring, more=True):
                        s = ring % 2
                        act.wait_ge(hidden, j + (1 - E))
                        act.activation(hid[s], hid[s], ACT.Gelu_apprx_tanh).then_inc(gelu_done, 1)
                        if more:
                            split_u(j + 2, s)
                        parts(j, ring)
                    for i in range(4):
                        parts(i, i)
                    with act.Fori(0, E // 4 - 1) as it:
                        for i in range(4, 8):
                            act.wait_ge(summed, it * 2 * TILES + TILES * (i // 2 - 1))
                            parts(it * 4 + i, i % 4)
                    split_u(E, 0)
                    split_u(E + 1, 1)
                    late(E, 0)
                    late(E + 1, 1)
                    with act.Fori(0, (C - E) // 4 - 1) as it:
                        for i in range(2, 6):
                            late(it * 4 + (E + i), i % 4)
                    late(C - 2, 2, more=False)
                    late(C - 1, 3, more=False)

                @block.vector
                def _(dve):
                    dve.memset(y[:], 0.0).then_inc(zeroed, 1)
                    dve.sem_inc(u_split, 2)
                    dve.sem_inc(v_split, 2)
                    dve.sem_inc(weighted, 2)
                    dve.sem_inc(a_split, 2)

                    def split_u(j, s):
                        dve.wait_ge(u_hi_done, j + (1 - E))
                        dve.tensor_tensor(flat(u_lo, s), u_raw[:, s], flat(u_hi, s).bitcast(F32), ALU.subtract).then_inc(u_split, 1)

                    def weigh(j, s, values):
                        dve.wait_ge(g_loaded[s], arrivals(j, s))
                        dve.scalar_tensor_tensor(g[:, s], g[:, s], 1.0 / WEIGHT_SCALE, values, ALU.mult, ALU.mult).then_inc(weighted, 1)

                    def parts(j, ring):
                        s = ring % 2
                        dve.wait_ge(a_hi_done, j + 1)
                        dve.tensor_tensor(act_lo[:, ring], g[:, s], act_hi[:, ring].bitcast(F32), ALU.subtract).then_inc(a_split, 1)
                        dve.wait_ge(v_hi_done, j + 1)
                        dve.tensor_tensor(v_lo[:, ring], v_raw[:, s], v_hi[:, ring].bitcast(F32), ALU.subtract).then_inc(v_split, 1)

                    def early(j, ring, between=lambda: None):
                        s = ring % 2
                        dve.wait_ge(u_loaded[s], arrivals(j, s))
                        weigh(j, s, u_raw[:, s])
                        between()
                        parts(j, ring)

                    def late(j, ring, more=True, between=lambda: None):
                        s = ring % 2
                        dve.wait_ge(gelu_done, j + (1 - E))
                        weigh(j, s, hid[s])
                        if more:
                            split_u(j + 2, s)
                        between()
                        parts(j, ring)

                    def add(pair, tiles=range(TILES)):
                        for n in tiles:
                            k, half = divmod(n, 2)
                            to = y[:, k, half * HALF:(half + 1) * HALF]
                            dve.wait_ge(summed, pair * TILES + (n + 1))
                            dve.tensor_tensor(to, to, ps[:, 4 + n % 4], ALU.add).then_inc(added, 1)

                    def late_pair(first, ring, pair):
                        late(first, ring)
                        late(first + 1, ring + 1, between=lambda: add(pair, range(2)))
                        add(pair, range(2, TILES))
                    for i in range(4):
                        early(i, i)
                    dve.wait_ge(zeroed, 1)
                    add(0)
                    with dve.Fori(0, E // 4 - 1) as it:
                        for p2 in range(2):
                            pair = it * 2 + (1 + p2)
                            early(it * 4 + (4 + 2 * p2), 2 * p2, between=lambda: add(pair, range(3)))
                            add(pair, range(3, 8))
                            early(it * 4 + (5 + 2 * p2), 2 * p2 + 1, between=lambda: add(pair, range(8, 11)))
                            add(pair, range(11, TILES))
                    split_u(E, 0)
                    split_u(E + 1, 1)
                    late(E, 0)
                    late(E + 1, 1, between=lambda: add(E // 2 - 1, range(2)))
                    add(E // 2 - 1, range(2, TILES))
                    with dve.Fori(0, (C - E) // 4 - 1) as it:
                        late_pair(it * 4 + (E + 2), 2, it * 2 + E // 2)
                        late_pair(it * 4 + (E + 4), 0, it * 2 + (E // 2 + 1))
                    late(C - 2, 2, more=False)
                    late(C - 1, 3, more=False, between=lambda: add(C // 2 - 2, range(2)))
                    add(C // 2 - 2, range(2, TILES))
                    add(C // 2 - 1)

                @block.tensor
                def _(pe):
                    pe.sem_inc(added, 4)

                    def up(j, ring):
                        s = ring % 2
                        pe.wait_ge(u_split, j + (3 - E))
                        pe.wait_ge(weighted, j + 1)
                        for half in range(2):
                            t = slice(half * HALF, (half + 1) * HALF)
                            for k in range(KT):
                                last = self.product3(pe, ps[:, 2 * s + half], u_hi[:, s, k], u_lo[:, s, k],
                                                     h2_hi[:, k, t], h2_lo[:, k, t], k == 0, k == KT - 1)
                        last.then_inc(hidden, 1)

                    def down(pair, rings):
                        pe.wait_ge(a_split, pair * 2 + 4)
                        pe.wait_ge(v_split, pair * 2 + 4)
                        for n in range(TILES):
                            k, half = divmod(n, 2)
                            d = slice(k * P, (k + 1) * P)
                            t = slice(half * HALF, (half + 1) * HALF)
                            pe.wait_ge(added, pair * TILES + (n + 1))
                            for r in rings:
                                last = self.product3(pe, ps[:, 4 + n % 4], v_hi[:, r, d], v_lo[:, r, d],
                                                     act_hi[:, r, t], act_lo[:, r, t], r == rings[0], r == rings[1])
                            last.then_inc(summed, 1)
                    with pe.Fori(0, E // 4 - 1) as it:
                        down(it * 2, (0, 1))
                        down(it * 2 + 1, (2, 3))
                    down(E // 2 - 2, (0, 1))
                    up(E, 0)
                    up(E + 1, 1)
                    down(E // 2 - 1, (2, 3))
                    with pe.Fori(0, (C - E) // 4 - 1) as it:
                        up(it * 4 + (E + 2), 2)
                        up(it * 4 + (E + 3), 3)
                        down(it * 2 + E // 2, (0, 1))
                        up(it * 4 + (E + 4), 0)
                        up(it * 4 + (E + 5), 1)
                        down(it * 2 + (E // 2 + 1), (2, 3))
                    up(C - 2, 2)
                    up(C - 1, 3)
                    down(C // 2 - 2, (0, 1))
                    down(C // 2 - 1, (2, 3))


def _tiles(w):
    n = w.shape[1] // P
    return np.ascontiguousarray(w.reshape(KT, P, n, P).transpose(2, 1, 0, 3)).reshape(n, P, KT * P)


def _columns(v):
    return np.asarray(v).reshape(-1, P).T


def kernel(**inputs):
    import concourse.bacc as bacc
    from concourse.bass_utils import run_bass_kernel_spmd

    x = {k: np.asarray(v) for k, v in inputs.items()}
    rot = np.zeros((P, P), np.float32)
    freq = np.zeros((P, 1), np.float32)
    half = ROPE_DIM // 2
    inv = np.float32(ROPE_THETA) ** (-np.arange(0, ROPE_DIM, 2, dtype=np.float32) / np.float32(ROPE_DIM))
    for m in range(2):
        for i in range(half):
            r1, r2 = m * MAP_DIM + i, m * MAP_DIM + half + i
            rot[r2, r1] = -1.0
            rot[r1, r2] = 1.0
            freq[r1, 0] = freq[r2, 0] = inv[i]
    arrays = {
        "xT": x["x"][0].T,
        "c": x["c"],
        "positions": x["positions"],
        "w_adaT": x["w_ada"][0].T.reshape(NMOD, P, D).transpose(1, 0, 2),
        "b_ada": _columns(x["b_ada"][0]),
        "vecs": np.concatenate([_columns(x[n][0]) for n in ("g_pre_mix", "g_post_mix", "g_pre_ffn", "g_post_ffn", "gmlp_ln_g", "gmlp_ln_b")], 1),
        "g_subln": x["g_subln"][0][:, None],
        "lams": np.concatenate([x[n][0] for n in ("lambda_q1", "lambda_k1", "lambda_q2", "lambda_k2")])[None],
        "ident": np.eye(P, dtype=np.float32),
        "rotate": rot,
        "freq": freq,
        "w_in": _tiles(x["w_in"][0]),
        "w_attn": _tiles(x["w_attn_branch"][0]),
        "w_gmlp": _tiles(x["w_gmlp_branch"][0]),
        "w_out": _tiles(x["w_out"][0]),
        "w_peer": _tiles(x["w_peer_q"][0]),
        "w_spatial": x["w_spatial"][0].transpose(2, 0, 1).reshape(P, -1),
        "b_spatial": x["b_spatial"][0].reshape(1, -1),
        "keysT": x["peer_sub_keys"][0].reshape(SIDES, KEYS, P).transpose(2, 0, 1).reshape(P, -1),
        "peer_uT": x["peer_u"][0].reshape(KEYS, P, KT, P).transpose(0, 3, 2, 1).reshape(KEYS, P, D),
        "peer_v": x["peer_v"][0].reshape(KEYS, P, D),
    }
    arrays = {f"{k}_dram": np.ascontiguousarray(v) for k, v in arrays.items()}
    nc = bacc.Bacc("TRN2", target_bir_lowering=False, num_devices=1)
    aps = {k.removesuffix("_dram"): nc.dram_tensor(k, v.shape, mybir.dt.from_np(v.dtype), kind="ExternalInput").ap() for k, v in arrays.items()}
    aps["out"] = nc.dram_tensor("out", (D, T), F32, kind="ExternalOutput").ap()
    Layer(nc, aps).build()
    got = run_bass_kernel_spmd(nc, [arrays], core_ids=[0])
    return got.results[0]["out"].T[None]
```

```python
import math
from contextlib import ExitStack

import numpy as np

import concourse.bass as bass
from concourse import mybir

F32 = mybir.dt.float32
F32R = mybir.dt.float32r
F16 = mybir.dt.float16
I32 = mybir.dt.int32
U32 = mybir.dt.uint32
ALU = mybir.AluOpType
ACT = mybir.ActivationFunctionType
AXX = mybir.AxisListType.X

P = 128
T = 1024
D = 1024
KT = D // P
TB = T // P
HALF = 512
HEADS = 8
MAP_DIM = 64
TOPK = 16
SIDES = 2 * HEADS
KEYS = 128
NMOD = 6 * KT
EPS = 1e-6
LAMBDA_INIT = 0.8 - 0.6 * math.exp(-0.3 * 0)
SCALE = MAP_DIM ** -0.5
ROPE_DIM = MAP_DIM // 4
ROPE_THETA = 500000.0
LOWEST = -3.0e38
WEIGHT_SCALE = 2.0 ** 14
EARLY = 5 * TB

Q0, K0, V0, ZU0, ZV0, GA0, GG0 = 0, 8, 16, 24, 32, 40, 48


class Layer:

    def __init__(self, nc, a):
        self.nc, self.a = nc, a
        self.ctx = ExitStack()
        self.stage_sems = []

    def sb(self, ctx, name, shape, dt=F32):
        return ctx.enter_context(self.nc.sbuf_tensor(name, shape, dt))

    def sem(self, name):
        self.stage_sems.append(self.nc.alloc_semaphore(name=name))
        return self.stage_sems[-1]

    def stage_end(self):
        self.nc.all_engine_barrier()
        self.nc.clear_and_free_semaphores(self.stage_sems)
        self.nc.all_engine_barrier()
        self.stage_sems = []

    def scratch(self, name, shape):
        return self.nc.dram_tensor(name, shape, F32, kind="Internal").ap()

    def build(self):
        nc = self.nc
        with self.ctx:
            c = self.ctx
            self.ident = self.sb(c, "ident", [P, P])
            self.ones_mean = self.sb(c, "ones_mean", [P, P])
            self.ones_head = self.sb(c, "ones_head", [P, P])
            self.vecs = self.sb(c, "vecs", [P, NMOD])
            self.subln_gain = self.sb(c, "subln_gain", [P, 1])
            self.mod = self.sb(c, "mod", [P, NMOD])
            self.coef = self.sb(c, "coef", [P, 4 * KT])
            self.lam = self.sb(c, "lam", [P, 1])
            self.psum = c.enter_context(nc.psum_tensor("psum", [P, 8, HALF], F32))
            self.gate_scr = self.scratch("gate_scratch", [2 * KT, P, T])
            self.u_scr = self.scratch("gelu_u_scratch", [KT, P, T])
            self.o_scr = self.scratch("attention_scratch", [HEADS, P, T])
            self.sg_scr = self.scratch("spatial_scratch", [KT, P, T])
            self.x1_scr = self.scratch("residual_scratch", [KT, P, T])
            self.h_scr = self.scratch("hidden_scratch", [EARLY, P, T])
            self.route_scr = self.scratch("route_scratch", [KEYS, P, T])

            self.b_ada = self.sb(c, "b_ada", [P, NMOD])
            hi = self.sb(c, "in_hi", [P, KT, T], F32R)
            lo = self.sb(c, "in_lo", [P, KT, T], F32R)
            with ExitStack() as rope_scope:
                self.cos = self.sb(rope_scope, "cos", [P, T])
                self.sin = self.sb(rope_scope, "sin", [P, T])
                self.rotate = self.sb(rope_scope, "rotate", [P, P])
                with ExitStack() as s:
                    x = self.sb(s, "x", [P, KT, T])
                    self.conditioning(x)
                    self.rms_modulate("pre_mix", x, self.coef[:, 0:KT], self.mod[:, 0:KT], hi, lo)
                    self.stage_end()
                self.attention(hi, lo)
                self.stage_end()
            self.gmlp(hi, lo)
            self.stage_end()
            self.gates(hi, lo)
            self.stage_end()
            with ExitStack() as mixing:
                wide = self.sb(mixing, "mixed", [P, KT, T])
                self.branches(wide, hi, lo)
                self.stage_end()
                total = self.sb(mixing, "out_total", [P, T])
                self.out_projection(wide, hi, lo, total)
                self.stage_end()
                x1 = self.sb(mixing, "x1", [P, KT, T])
                self.add_normed("mix", wide, self.coef[:, KT:2 * KT], self.a["xT"].rearrange("(k p) t -> p k t", p=P), x1,
                                self.x1_scr.rearrange("k p t -> p k t"), total=total, squares_too=True)
                self.rms_modulate("pre_ffn", x1, self.coef[:, 2 * KT:3 * KT], self.mod[:, 3 * KT:4 * KT], hi, lo, summed_before=True)
                self.stage_end()
            self.route(hi, lo)
            y = self.sb(c, "y", [P, KT, T])
            self.experts(hi, lo, y)
            self.stage_end()
            self.finish(y)
            self.stage_end()

    def conditioning(self, x):
        nc, a = self.nc, self.a
        NBUF = 4
        NOW = 2 * KT
        x_loaded = self.sem("x_loaded")
        small = self.sem("small_loaded")
        ada_loaded = [self.sem(f"ada_loaded{i}") for i in range(NBUF)]
        c_ready = self.sem("c_ready")
        mod_dot = self.sem("mod_dot")
        chain = self.sem("conditioning_chain")
        lam_dots = self.sem("lam_dots")
        lam_exp = self.sem("lam_exp")
        angles = self.sem("angles")
        tables = self.sem("rope_tables")
        with ExitStack() as s:
            ada = self.sb(s, "ada", [P, NBUF, 2, D])
            cb = self.sb(s, "cb", [P, D])
            junk = self.sb(s, "junk", [P, 2, D])
            lams = self.sb(s, "lams", [P, 4, MAP_DIM])
            lam2 = self.sb(s, "lam2", [P, 4])
            pos = self.sb(s, "pos", [P, T], I32)
            freq = self.sb(s, "freq", [P, 1])
            ang = self.sb(s, "ang", [P, T])
            turns = self.sb(s, "turns", [P, T])
            folded = self.sb(s, "folded", [P, T])
            NSMALL = 9
            with nc.Block() as block:
                @block.sync
                def _(sp):
                    sp.dma_start(cb[:], a["c"].to_broadcast([P, D])).then_inc(small, 16)
                    sp.dma_start(self.ident[:], a["ident"]).then_inc(small, 16)
                    sp.dma_start(self.rotate[:], a["rotate"]).then_inc(small, 16)
                    sp.dma_start(self.vecs[:], a["vecs"]).then_inc(small, 16)
                    sp.dma_start(self.subln_gain[:], a["g_subln"]).then_inc(small, 16)
                    sp.dma_start(self.b_ada[:], a["b_ada"]).then_inc(small, 16)
                    sp.dma_start(freq[:], a["freq"]).then_inc(small, 16)
                    sp.dma_start(lams[:].rearrange("p a d -> p (a d)"), a["lams"].to_broadcast([P, 4 * MAP_DIM])).then_inc(small, 16)
                    sp.dma_start(pos[:], a["positions"].to_broadcast([P, T])).then_inc(small, 16)
                    for g in range(NOW // 2):
                        if g >= NBUF:
                            sp.wait_ge(mod_dot, 2 * (g - NBUF + 1))
                        sp.dma_start(ada[:, g % NBUF], a["w_adaT"][:, 2 * g:2 * g + 2, :]).then_inc(ada_loaded[g % NBUF], 16)
                    sp.dma_start(x[:], a["xT"].rearrange("(k p) t -> p k t", p=P)).then_inc(x_loaded, 16)
                    sp.wait_ge(x_loaded, 16)

                @block.scalar
                def _(act):
                    act.wait_ge(small, 16 * NSMALL)
                    act.activation(cb[:], cb[:], ACT.Silu).then_inc(c_ready, 1)
                    act.wait_ge(lam_dots, 2)
                    act.activation(lam2[:, 2:4], lam2[:, 0:2], ACT.Exp).then_inc(lam_exp, 1)
                    act.wait_ge(angles, 1)
                    act.activation(self.sin[:], ang[:], ACT.Sin).then_inc(tables, 1)
                    act.activation(self.cos[:], folded[:], ACT.Sin).then_inc(tables, 1)

                @block.vector
                def _(dve):
                    n = [0]

                    def link(ins):
                        n[0] += 1
                        ins.then_inc(chain, 1)
                        dve.wait_ge(chain, n[0])

                    dve.memset(self.ones_mean[:], 1.0 / D)
                    link(dve.memset(self.ones_head[:], 1.0 / P))
                    dve.wait_ge(small, 16 * NSMALL)
                    for i in range(2):
                        dve.tensor_tensor_reduce(out=junk[:, i, 0:MAP_DIM], in0=lams[:, 2 * i], in1=lams[:, 2 * i + 1],
                                                 scale=1.0, scalar=0.0, op0=ALU.mult, op1=ALU.add,
                                                 accum_out=lam2[:, i:i + 1]).then_inc(lam_dots, 1)
                    link(dve.tensor_copy(ang[:], pos[:]))
                    link(dve.tensor_scalar(ang[:], ang[:], freq[:, 0:1], None, ALU.mult))
                    magic = 1.5 * 2.0 ** 23
                    link(dve.tensor_scalar(turns[:], ang[:], 1.0 / (2.0 * math.pi), None, ALU.mult))
                    link(dve.tensor_scalar(turns[:], turns[:], magic, None, ALU.add))
                    link(dve.tensor_scalar(turns[:], turns[:], magic, None, ALU.subtract))
                    c1 = 6.28125
                    c2 = float(np.float32(round((2 * math.pi - c1) * 2 ** 20) / 2 ** 20))
                    c3 = 2 * math.pi - c1 - c2
                    for part in (c1, c2, c3):
                        link(dve.scalar_tensor_tensor(ang[:], turns[:], -part, ang[:], ALU.mult, ALU.add))
                    limit = float(np.nextafter(np.float32(math.pi), np.float32(0)))
                    link(dve.tensor_scalar(ang[:], ang[:], limit, -limit, ALU.min, ALU.max))
                    link(dve.tensor_scalar(folded[:], ang[:], -1.0, None, ALU.mult))
                    link(dve.tensor_tensor(folded[:], folded[:], ang[:], ALU.max))
                    dve.tensor_scalar(folded[:], folded[:], -1.0, math.pi / 2, ALU.mult, ALU.add).then_inc(angles, 1)
                    dve.wait_ge(c_ready, 1)
                    for j in range(NOW):
                        g = j // 2
                        dve.wait_ge(ada_loaded[g % NBUF], 16 * (g // NBUF + 1))
                        if j >= 2:
                            dve.wait_ge(mod_dot, j - 1)
                        elif j == 0:
                            dve.wait_ge(lam_dots, 2)
                        dve.tensor_tensor_reduce(out=junk[:, j % 2], in0=ada[:, g % NBUF, j % 2], in1=cb[:], scale=1.0,
                                                 scalar=0.0, op0=ALU.mult, op1=ALU.add,
                                                 accum_out=self.mod[:, j:j + 1]).then_inc(mod_dot, 1)
                    dve.wait_ge(mod_dot, NOW)
                    link(dve.tensor_tensor(self.mod[:, 0:NOW], self.mod[:, 0:NOW], self.b_ada[:, 0:NOW], ALU.add))
                    dve.scalar_tensor_tensor(self.coef[:, 0:KT], self.mod[:, KT:2 * KT], 1.0, self.vecs[:, 0:KT], ALU.add, ALU.mult)
                    dve.tensor_scalar(self.subln_gain[:], self.subln_gain[:], 1.0 - LAMBDA_INIT, None, ALU.mult)
                    dve.wait_ge(lam_exp, 1)
                    link(dve.tensor_tensor(self.lam[:], lam2[:, 2:3], lam2[:, 3:4], ALU.subtract))
                    link(dve.tensor_scalar(self.lam[:], self.lam[:], LAMBDA_INIT, None, ALU.add))

    def broadcast_rows(self, pe, to, diag):
        for half in range(2):
            last = pe.matmul(to[half], self.ones_head[:], diag[:, half * HALF:(half + 1) * HALF], start=True, stop=True)
        return last

    def mean_square(self, name, src, rstd, sq, total=None, summed_before=False):
        nc, ps = self.nc, self.psum
        squared = self.sem(f"{name}_squared")
        summed = self.sem(f"{name}_summed")
        meaned = self.sem(f"{name}_meaned")
        eps_added = self.sem(f"{name}_eps")
        rooted = self.sem(f"{name}_rooted")
        inverse = self.sem(f"{name}_inverse")
        on_diag = self.sem(f"{name}_diag")
        spread = self.sem(f"{name}_spread")
        copied = self.sem(f"{name}_copied")
        make_total = total is None and not summed_before
        with ExitStack() as c:
            if make_total:
                total = self.sb(c, f"{name}_total", [P, T])
            token = self.sb(c, f"{name}_token", [P, TB])
            diag = sq[:, 0]
            with nc.Block() as block:
                @block.scalar
                def _(act):
                    if make_total:
                        for k in range(KT):
                            if k >= 2:
                                act.wait_ge(summed, k - 1)
                            act.activation(sq[:, k % 2], src[:, k], ACT.Square).then_inc(squared, 1)
                    act.wait_ge(eps_added, 1)
                    act.activation(token[:], token[:], ACT.Sqrt).then_inc(rooted, 1)
                    act.wait_ge(spread, 1)
                    act.activation(rstd[:], ps[:, 2:4].rearrange("p b t -> p (b t)"), ACT.Copy).then_inc(copied, 1)

                @block.vector
                def _(dve):
                    if make_total:
                        dve.wait_ge(squared, 2)
                        dve.tensor_tensor(total[:], sq[:, 0], sq[:, 1], ALU.add).then_inc(summed, 2)
                        for k in range(2, KT):
                            dve.wait_ge(squared, k + 1)
                            dve.wait_ge(summed, k)
                            dve.tensor_tensor(total[:], total[:], sq[:, k % 2], ALU.add).then_inc(summed, 1)
                    if summed_before:
                        parts = ps[:, 0, 0:KT * TB].rearrange("p (k b) -> p b k", b=TB)
                        dve.tensor_reduce(token[:], parts, AXX, ALU.add).then_inc(meaned, 1)
                        dve.wait_ge(meaned, 1)
                        dve.tensor_scalar(token[:], token[:], EPS, None, ALU.add).then_inc(eps_added, 1)
                    else:
                        dve.wait_ge(meaned, 1)
                        dve.tensor_scalar(token[:], ps[:, 0, 0:TB], EPS, None, ALU.add).then_inc(eps_added, 1)
                    dve.wait_ge(rooted, 1)
                    dve.reciprocal(token[:], token[:]).then_inc(inverse, 1)
                    dve.wait_ge(inverse, 1)
                    self.to_diagonals(dve, diag, token[:]).then_inc(on_diag, 1)

                @block.tensor
                def _(pe):
                    if make_total:
                        pe.wait_ge(summed, KT)
                    if not summed_before:
                        self.square_means(pe, ps[:, 0], total, self.ones_mean).then_inc(meaned, 1)
                    pe.wait_ge(on_diag, 1)
                    self.broadcast_rows(pe, [ps[:, 2], ps[:, 3]], diag).then_inc(spread, 1)

    def square_means(self, pe, bank, squares, ones, first=0):
        for b in range(TB):
            last = pe.matmul(bank[:, first + b:first + b + 1], squares[:, b * P:(b + 1) * P], ones[:, 0:1], start=True, stop=True)
        return last

    def to_diagonals(self, dve, diag, token):
        return dve.scalar_tensor_tensor(diag.rearrange("p (b t) -> p b t", t=P), self.ident[:].unsqueeze(1).to_broadcast([P, TB, P]),
                                        float(P), token.unsqueeze(2).to_broadcast([P, TB, P]), ALU.mult, ALU.mult)

    def rms_modulate(self, name, x, gain, shift, hi, lo, summed_before=False):
        nc = self.nc
        scaled = self.sem(f"{name}_scaled")
        full = self.sem(f"{name}_full")
        hi_done = self.sem(f"{name}_hi")
        lo_done = self.sem(f"{name}_lo")
        with ExitStack() as s:
            rstd = self.sb(s, f"{name}_rstd_t", [P, T])
            sq = self.sb(s, f"{name}_sq", [P, 2, T])
            self.mean_square(name, x, rstd, sq, summed_before=summed_before)
            with nc.Block() as block:
                @block.vector
                def _(dve):
                    def scale(k):
                        if k >= 2:
                            dve.wait_ge(lo_done, k - 1)
                        dve.tensor_tensor(sq[:, k % 2], x[:, k], rstd[:], ALU.mult).then_inc(scaled, 1)
                    scale(0)
                    for k in range(KT):
                        if k + 1 < KT:
                            scale(k + 1)
                        dve.wait_ge(hi_done, k + 1)
                        dve.tensor_tensor(lo[:, k], sq[:, k % 2], hi[:, k].bitcast(F32), ALU.subtract).then_inc(lo_done, 1)

                @block.scalar
                def _(act):
                    for k in range(KT):
                        act.wait_ge(scaled, k + 1)
                        act.activation(sq[:, k % 2], sq[:, k % 2], ACT.Identity, bias=shift[:, k:k + 1], scale=gain[:, k:k + 1]).then_inc(full, 1)
                        act.wait_ge(full, k + 1)
                        act.activation(hi[:, k], sq[:, k % 2], ACT.Copy).then_inc(hi_done, 1)

    def product3(self, pe, out, w_hi, w_lo, x_hi, x_lo, start, stop):
        pe.matmul(out, w_hi, x_hi, start=start, stop=False)
        pe.matmul(out, w_hi, x_lo, start=False, stop=False)
        return pe.matmul(out, w_lo, x_hi, start=False, stop=stop)

    def projection(self, name, wt, first, x_hi, x_lo, tiles, act_out=None, dve_out=None, pe_after=None, dve_after=None, pool_program=None):
        nc = self.nc
        loaded = [self.sem(f"{name}_w_loaded{i}") for i in range(2)]
        w_hi_done = self.sem(f"{name}_w_hi_done")
        w_split = self.sem(f"{name}_w_split")
        product = self.sem(f"{name}_product")
        emptied = self.sem(f"{name}_emptied")
        acc = [self.psum[:, 2 * s:2 * s + 2].rearrange("p b t -> p (b t)") for s in range(2)]
        turns = tiles // 2
        with ExitStack() as c:
            raw = self.sb(c, f"{name}_w_raw", [P, 2, D])
            w_hi = self.sb(c, f"{name}_w_hi_t", [P, 2, KT, P], F32R)
            w_lo = self.sb(c, f"{name}_w_lo_t", [P, 2, KT, P], F32R)
            flat = lambda w, s: w[:, s].rearrange("p k n -> p (k n)")
            with nc.Block() as block:
                @block.sync
                def _(sp):
                    def turn(j0):
                        at = [sp.snap(j0 + s) if not isinstance(j0, int) else j0 + s for s in range(2)]
                        free = [sp.snap(j0 + s + 1) if not isinstance(j0, int) else j0 + s + 1 for s in range(2)]
                        src = [sp.snap(j0 + s + first) if not isinstance(j0, int) else j0 + s + first for s in range(2)]
                        for s in range(2):
                            sp.wait_ge(w_split, free[s])
                            sp.dma_start(raw[:, s], wt[bass.ds(src[s], 1)].rearrange("o p n -> (o p) n")).then_inc(loaded[s], 16)
                    with sp.Fori(0, turns) as it:
                        turn(it * 2)

                @block.scalar
                def _(act):
                    def split(j, s):
                        act.wait_ge(loaded[s], j * 8 + (16 - 8 * s))
                        act.wait_ge(product, j + 1)
                        act.activation(flat(w_hi, s), raw[:, s], ACT.Copy).then_inc(w_hi_done, 1)

                    def empty(j, s):
                        if act_out:
                            act.wait_ge(product, j + 3)
                            act_out(act, j, s, acc[s], emptied)
                    for s in range(2):
                        split(s, s)
                    if turns > 1:
                        with act.Fori(0, turns - 1) as it:
                            for s in range(2):
                                empty(it * 2 + s, s)
                                split(it * 2 + (2 + s), s)
                    for s in range(2):
                        empty(tiles - 2 + s, s)

                @block.vector
                def _(dve):
                    dve.sem_inc(w_split, 2)

                    def split(j, s):
                        dve.wait_ge(w_hi_done, j + 1)
                        dve.tensor_tensor(flat(w_lo, s), raw[:, s], flat(w_hi, s).bitcast(F32), ALU.subtract).then_inc(w_split, 1)

                    def empty(j, s):
                        if dve_out:
                            dve.wait_ge(product, j + 3)
                            dve_out(dve, j, s, acc[s], emptied)
                    for s in range(2):
                        split(s, s)
                    if dve_after is None:
                        with dve.Fori(0, turns - 1) as it:
                            for s in range(2):
                                empty(it * 2 + s, s)
                                split(it * 2 + (2 + s), s)
                        for s in range(2):
                            empty(tiles - 2 + s, s)
                    else:
                        empty(0, 0)
                        split(2, 0)
                        with dve.Fori(0, turns - 2) as it:
                            for s in range(2):
                                empty(it * 2 + (1 + s), 1 - s)
                                split(it * 2 + (3 + s), 1 - s)
                                dve_after(dve, it * 2 + s, s)
                        empty(tiles - 3, 1)
                        split(tiles - 1, 1)
                        dve_after(dve, tiles - 4, 0)
                        empty(tiles - 2, 0)
                        dve_after(dve, tiles - 3, 1)
                        empty(tiles - 1, 1)
                        dve_after(dve, tiles - 2, 0)
                        dve_after(dve, tiles - 1, 1)

                @block.tensor
                def _(pe):
                    pe.sem_inc(product, 2)
                    pe.sem_inc(emptied, 2)

                    def tile(j, s):
                        pe.wait_ge(w_split, j + 3)
                        pe.wait_ge(emptied, j + 1)
                        for half in range(2):
                            t = slice(half * HALF, (half + 1) * HALF)
                            for k in range(KT):
                                last = self.product3(pe, self.psum[:, 2 * s + half], w_hi[:, s, k], w_lo[:, s, k],
                                                     x_hi[:, k, t], x_lo[:, k, t], k == 0, k == KT - 1)
                        last.then_inc(product, 1)
                    if pe_after is None:
                        with pe.Fori(0, turns) as it:
                            for s in range(2):
                                tile(it * 2 + s, s)
                    else:
                        tile(0, 0)
                        with pe.Fori(0, turns - 1) as it:
                            for s in range(2):
                                tile(it * 2 + (1 + s), 1 - s)
                                pe_after(pe, it * 2 + s, s, emptied)
                        tile(tiles - 1, 1)
                        pe_after(pe, tiles - 2, 0, emptied)
                        pe_after(pe, tiles - 1, 1, emptied)

                if pool_program:
                    @block.gpsimd
                    def _(pool):
                        pool_program(pool, emptied)

    def attention(self, h_hi, h_lo):
        nc, w = self.nc, self.a["w_in"]
        ps = self.psum
        acc = [ps[:, 2 * s:2 * s + 2].rearrange("p b t -> p (b t)") for s in range(2)]
        turned = ps[:, 4:6].rearrange("p b t -> p (b t)")
        o_acc = ps[:, 6]
        job = ps[:, 7]
        KK, QQ, VV = range(3)
        TILE0 = (K0, Q0, V0)
        HALVES = [(i, half) for i in (KK, QQ, VV) for half in range(2)]
        BPH = TB
        w_loaded = [self.sem(f"att_w_loaded{i}") for i in range(2)]
        w_hi_done = self.sem("att_w_hi_done")
        w_split = self.sem("att_w_split")
        projected = self.sem("att_projected")
        copied = self.sem("att_copied")
        prepared = self.sem("att_prepared")
        rope = self.sem("att_rope")
        x_hi_done = self.sem("att_x_hi_done")
        x_split = self.sem("att_x_split")
        scored = self.sem("att_scored")
        negmax = self.sem("att_negmax")
        exped = self.sem("att_exped")
        mixing = self.sem("att_mixing")
        mixed = self.sem("att_mixed")
        a_turned = self.sem("att_a_turned")
        a_hi_done = self.sem("att_a_hi")
        a_split = self.sem("att_a_split")
        out_summed = self.sem("att_out_summed")
        out_copied = self.sem("att_out_copied")
        stored = [self.sem(f"att_stored{i}") for i in range(2)]
        with ExitStack() as c:
            raw = self.sb(c, "att_raw", [P, D])
            w_hi = self.sb(c, "att_w_hi_t", [P, 2, KT, P], F32R)
            w_lo = self.sb(c, "att_w_lo_t", [P, 2, KT, P], F32R)
            k_both = self.sb(c, "att_k_both", [P, 2, 2, T], F32R)
            q_twice = self.sb(c, "att_q_twice", [P, 2, 2, T], F32R)
            q_lo = self.sb(c, "att_q_lo", [P, 2, T], F32R)
            v_hi = self.sb(c, "att_v_hi", [P, 2, T], F32R)
            v_lo = self.sb(c, "att_v_lo", [P, 2, T], F32R)
            map_rows = [slice(m * MAP_DIM, (m + 1) * MAP_DIM) for m in range(2)]
            plain = self.sb(c, "att_plain", [P, 2, HALF])
            swung = self.sb(c, "att_swung", [P, HALF])
            prob = self.sb(c, "att_prob", [P, 2, T])
            amap = self.sb(c, "att_map", [P, 2, T])
            a_hi = self.sb(c, "att_a_hi_t", [P, KT, HALF], F32R)
            a_lo = self.sb(c, "att_a_lo_t", [P, KT, HALF], F32R)
            nmax = self.sb(c, "att_nmax", [P, 2])
            z = self.sb(c, "att_z", [P, 2])
            zr = self.sb(c, "att_zr", [P, 2])
            o = self.sb(c, "att_o", [P, HALF])
            flat = lambda t, s: t[:, s].rearrange("p k n -> p (k n)")
            cols = lambda half: slice(half * HALF, (half + 1) * HALF)

            class Head:

                def __init__(self, it, c):
                    self.it, self.c, self.par = it, c, c % 2

                def at(self, per_head, more):
                    return self.it * (2 * per_head) + (self.c * per_head + more)

                def next(self):
                    return Head(self.it, self.c + 1)

                def ring(self, i):
                    return (3 * self.c + i) % 2

                def loads(self, i):
                    return self.it * 48 + 16 * ((3 * self.c + i) // 2 + 1)

            def all_heads(eng, body, first=None):
                with eng.Fori(0, HEADS // 2 - 1) as it:
                    for c2 in range(2):
                        body(Head(it, c2), Head(it, c2 + 1))
                last = HEADS // 2 - 1
                body(Head(last, 0), Head(last, 1))
                body(Head(last, 1), None)

            PROJECTS = {b: b for b in range(6)}
            PREPARES = {b: b - 1 for b in range(1, 7)}
            SPLITS = {0: (QQ, 0), 2: (VV, 0), 4: (KK, 1)}

            with nc.Block() as block:
                @block.sync
                def _(sp):
                    with sp.Fori(0, HEADS // 2) as it:
                        n0 = [sp.snap(it * 6 + (n + 2)) for n in range(6)]
                        src = [sp.snap(it * 2 + (c2 + TILE0[i])) for c2 in range(2) for i in range(3)]
                        to = [sp.snap(it * 2 + c2) for c2 in range(2)]
                        for n in range(6):
                            sp.wait_ge(w_split, n0[n])
                            sp.dma_start(raw[:], w[bass.ds(src[n], 1)].rearrange("o p n -> (o p) n")).then_inc(w_loaded[n % 2], 16)

                @block.scalar
                def _(act):
                    def split_weights(g, i):
                        r = g.ring(i)
                        act.wait_ge(w_loaded[r], g.loads(i))
                        act.wait_ge(projected, g.at(6, 2 * i + 2))
                        act.activation(flat(w_hi, r), raw[:], ACT.Copy).then_inc(w_hi_done, 1)

                    def copy(g, e):
                        act.wait_ge(projected, g.at(6, e + 5))
                        act.wait_ge(x_split, g.at(6, e + 5))
                        act.activation(plain[:, e % 2], job, ACT.Copy).then_inc(copied, 1)

                    def high(g, e):
                        i, half = HALVES[e]
                        if i == VV:
                            act.wait_ge(prepared, g.at(6, e + 1))
                            act.activation(v_hi[:, g.par, cols(half)], job, ACT.Copy).then_inc(x_hi_done, 1)
                        else:
                            act.wait_ge(rope, g.at(12, 3 * e + 3))
                            for m in range(2):
                                own = map_rows[m]
                                if i == KK:
                                    last = act.activation(k_both[own, g.par, m, cols(half)], plain[own, e % 2], ACT.Copy)
                                else:
                                    for rows in map_rows:
                                        last = act.activation(q_twice[rows, g.par, m, cols(half)], plain[own, e % 2], ACT.Copy)
                            last.then_inc(x_hi_done, 1)

                    def exps(h, b):
                        for m in range(2):
                            act.wait_ge(negmax, h.at(2 * BPH, 2 * b + m + 1))
                            act.wait_ge(mixed, h.at(BPH, b + 2))
                            act.activation(prob[:, m], acc[m], ACT.Exp, bias=nmax[:, m:m + 1], scale=1.0,
                                           accum_out=z[:, m:m + 1]).then_inc(exped, 1)

                    def turned_hi(h, b):
                        act.wait_ge(a_turned, h.at(BPH, b + 3))
                        if b % 4 == 0:
                            act.wait_ge(out_summed, h.at(2, b // 4 + 1))
                        act.activation(a_hi[:, :, (b % 4) * P:(b % 4 + 1) * P], turned.rearrange("p (k q) -> p k q", q=P),
                                       ACT.Copy).then_inc(a_hi_done, 1)

                    def out(h, half):
                        act.wait_ge(out_summed, h.at(2, half + 2))
                        act.wait_ge(stored[1 - half], h.at(16, 16 + 16 * half))
                        act.activation(o[:], o_acc, ACT.Copy).then_inc(out_copied, 1)
                        act.wait_ge(out_copied, h.at(2, half + 2))
                        act.dma_start(self.o_scr[bass.ds(h.at(1, 0), 1), :, cols(half)].rearrange("o p n -> (o p) n"),
                                      o[:]).then_inc(stored[half], 16)

                    def body(h, g):
                        for b in range(BPH):
                            e = PREPARES.get(b)
                            if g and e is not None and HALVES[e][0] == VV:
                                high(g, e)
                            turned_hi(h, b)
                            if b + 1 < BPH:
                                exps(h, b + 1)
                            elif g:
                                exps(g, 0)
                            if g and b in SPLITS:
                                i, after = SPLITS[b]
                                if not after:
                                    split_weights(g, i)
                                elif not (isinstance(g.it, int) and 2 * g.it + g.c == HEADS - 1):
                                    split_weights(g.next(), i)
                            if g and e is not None and HALVES[e][0] != VV:
                                high(g, e)
                            if b == 4:
                                out(h, 0)
                            if g and b in PROJECTS:
                                copy(g, PROJECTS[b])
                        out(h, 1)
                    first = Head(0, 0)
                    split_weights(first, KK)
                    split_weights(first, QQ)
                    for e, (i, half) in enumerate(HALVES):
                        copy(first, e)
                        if e == 1:
                            split_weights(first, VV)
                        if e == 3:
                            split_weights(first.next(), KK)
                        high(first, e)
                    exps(first, 0)
                    all_heads(act, body)

                @block.vector
                def _(dve):
                    dve.sem_inc(w_split, 2)
                    dve.sem_inc(x_split, 6)
                    dve.sem_inc(mixed, 2)
                    dve.sem_inc(a_split, 1)

                    def split_weights(g, i):
                        r = g.ring(i)
                        dve.wait_ge(w_hi_done, g.at(3, i + 1))
                        dve.tensor_tensor(flat(w_lo, r), raw[:], flat(w_hi, r).bitcast(F32), ALU.subtract).then_inc(w_split, 1)

                    def swing(g, e):
                        i, half = HALVES[e]
                        dve.wait_ge(prepared, g.at(6, e + 1))
                        dve.scalar_tensor_tensor(swung[:], job, SCALE if i == QQ else 1.0, self.sin[:, cols(half)],
                                                 ALU.mult, ALU.mult).then_inc(rope, 1)

                    def rope_sum(g, e):
                        i, half = HALVES[e]
                        x = plain[:, e % 2]
                        dve.scalar_tensor_tensor(x, x, SCALE if i == QQ else 1.0, self.cos[:, cols(half)],
                                                 ALU.mult, ALU.mult).then_inc(rope, 1)
                        dve.wait_ge(rope, g.at(12, 3 * e + 2))
                        dve.tensor_tensor(x, x, swung[:], ALU.add).then_inc(rope, 1)

                    def low(g, e):
                        i, half = HALVES[e]
                        dve.wait_ge(x_hi_done, g.at(6, e + 1))
                        if i == VV:
                            last = dve.tensor_tensor(v_lo[:, g.par, cols(half)], job, v_hi[:, g.par, cols(half)].bitcast(F32), ALU.subtract)
                        else:
                            for m in range(2):
                                own = map_rows[m]
                                high = (k_both if i == KK else q_twice)[own, g.par, m, cols(half)].bitcast(F32)
                                to = k_both[map_rows[1 - m], g.par, m, cols(half)] if i == KK else q_lo[own, g.par, cols(half)]
                                last = dve.tensor_tensor(to, plain[own, e % 2], high, ALU.subtract)
                        last.then_inc(x_split, 1)

                    def maxima(h, b):
                        for m in range(2):
                            dve.wait_ge(scored, h.at(2 * BPH, 2 * b + m + 1))
                            dve.wait_ge(exped, h.at(2 * BPH, 2 * b + m + 1))
                            dve.tensor_reduce(nmax[:, m:m + 1], acc[m], AXX, ALU.max, negate=True).then_inc(negmax, 1)

                    def combine(h, b):
                        dve.wait_ge(exped, h.at(2 * BPH, 2 * b + 4))
                        dve.reciprocal(zr[:], z[:]).then_inc(mixing, 1)
                        dve.wait_ge(mixing, h.at(3 * BPH, 3 * b + 1))
                        dve.tensor_scalar(zr[:, 1:2], zr[:, 1:2], self.lam[:, 0:1], None, ALU.mult).then_inc(mixing, 1)
                        dve.wait_ge(mixing, h.at(3 * BPH, 3 * b + 2))
                        dve.tensor_scalar(prob[:, 1], prob[:, 1], zr[:, 1:2], None, ALU.mult).then_inc(mixing, 1)
                        dve.wait_ge(mixing, h.at(3 * BPH, 3 * b + 3))
                        dve.wait_ge(a_turned, h.at(BPH, b + 1))
                        dve.scalar_tensor_tensor(amap[:, b % 2], prob[:, 0], zr[:, 0:1], prob[:, 1], ALU.mult, ALU.subtract)\
                           .then_inc(mixed, 1)

                    def turned_lo(h, b):
                        dve.wait_ge(a_hi_done, h.at(BPH, b + 1))
                        q = slice((b % 4) * P, (b % 4 + 1) * P)
                        dve.tensor_tensor(a_lo[:, :, q], turned.rearrange("p (k q) -> p k q", q=P),
                                          a_hi[:, :, q].bitcast(F32), ALU.subtract).then_inc(a_split, 1)

                    def body(h, g):
                        for b in range(BPH):
                            combine(h, b)
                            e = PREPARES.get(b) if g else None
                            if e is not None:
                                if HALVES[e][0] == VV:
                                    low(g, e)
                                else:
                                    swing(g, e)
                            if b + 1 < BPH:
                                maxima(h, b + 1)
                            elif g:
                                maxima(g, 0)
                            turned_lo(h, b)
                            if e is not None and HALVES[e][0] != VV:
                                rope_sum(g, e)
                            if g and b in SPLITS:
                                i, after = SPLITS[b]
                                if not after:
                                    split_weights(g, i)
                                elif not (isinstance(g.it, int) and 2 * g.it + g.c == HEADS - 1):
                                    split_weights(g.next(), i)
                            if e is not None and HALVES[e][0] != VV:
                                low(g, e)
                    first = Head(0, 0)
                    split_weights(first, KK)
                    split_weights(first, QQ)
                    for e, (i, half) in enumerate(HALVES):
                        if e == 1:
                            split_weights(first, VV)
                        if e == 3:
                            split_weights(first.next(), KK)
                        if i != VV:
                            swing(first, e)
                            rope_sum(first, e)
                        low(first, e)
                    maxima(first, 0)
                    all_heads(dve, body)

                @block.tensor
                def _(pe):
                    pe.sem_inc(projected, 4)
                    pe.sem_inc(exped, 2)
                    pe.sem_inc(a_turned, 2)
                    pe.sem_inc(out_summed, 1)
                    pe.sem_inc(out_copied, 1)
                    for half in range(2):
                        pe.sem_inc(stored[half], 16)

                    def project(g, e):
                        i, half = HALVES[e]
                        r = g.ring(i)
                        pe.wait_ge(w_split, g.at(3, i + 3))
                        if e in (0, 5):
                            pe.wait_ge(x_split, g.at(6, e + 6))
                        else:
                            pe.wait_ge(rope, g.at(12, 3 * (e - 1) + 1))
                        for k in range(KT):
                            last = self.product3(pe, job, w_hi[:, r, k], w_lo[:, r, k], h_hi[:, k, cols(half)], h_lo[:, k, cols(half)],
                                                 k == 0, k == KT - 1)
                        last.then_inc(projected, 1)

                    def prepare(g, e):
                        i, half = HALVES[e]
                        pe.wait_ge(copied, g.at(6, e + 1))
                        if i == VV:
                            for k in range(4):
                                last = pe.transpose(job[:, k * P:(k + 1) * P], plain[:, e % 2, k * P:(k + 1) * P], self.ident[:])
                        else:
                            last = pe.matmul(job, self.rotate[:], plain[:, e % 2], start=True, stop=True)
                        last.then_inc(prepared, 1)

                    def scores(h, b):
                        q = slice(b * P, (b + 1) * P)
                        if b == 0:
                            pe.wait_ge(x_split, h.at(6, 10))
                        for m in range(2):
                            own = map_rows[m]
                            pe.wait_ge(exped, h.at(2 * BPH, 2 * b + m + 1))
                            for half in range(2):
                                to = ps[:, 2 * m + half]
                                pe.matmul(to, q_twice[:, h.par, m, q], k_both[:, h.par, m, cols(half)], start=True, stop=False)
                                last = pe.matmul(to, q_lo[own, h.par, q], k_both[own, h.par, m, cols(half)], start=False, stop=True)
                            last.then_inc(scored, 1)

                    def turn(h, b):
                        pe.wait_ge(mixed, h.at(BPH, b + 3))
                        pe.wait_ge(a_split, h.at(BPH, b + 1))
                        for k in range(TB):
                            last = pe.transpose(turned[:, k * P:(k + 1) * P], amap[:, b % 2, k * P:(k + 1) * P], self.ident[:])
                        last.then_inc(a_turned, 1)

                    def times_v(h, half):
                        pe.wait_ge(a_split, h.at(BPH, 4 * half + 5))
                        pe.wait_ge(x_split, h.at(6, 12))
                        pe.wait_ge(out_copied, h.at(2, half + 1))
                        for k in range(TB):
                            v = slice(k * P, (k + 1) * P)
                            last = self.product3(pe, o_acc, v_hi[:, h.par, v], v_lo[:, h.par, v],
                                                 a_hi[:, k], a_lo[:, k], k == 0, k == TB - 1)
                        last.then_inc(out_summed, 1)

                    def body(h, g):
                        for b in range(BPH):
                            if b + 1 < BPH:
                                scores(h, b + 1)
                            elif g:
                                scores(g, 0)
                            if g and b in PREPARES:
                                prepare(g, PREPARES[b])
                            if b == 4:
                                times_v(h, 0)
                            turn(h, b)
                            if g and b in PROJECTS:
                                project(g, PROJECTS[b])
                            if b == BPH - 1:
                                times_v(h, 1)
                    first = Head(0, 0)
                    for e in range(6):
                        project(first, e)
                        prepare(first, e)
                    scores(first, 0)
                    all_heads(pe, body)

                @block.gpsimd
                def _(pool):
                    for half in range(2):
                        pool.wait_ge(stored[half], 16 * (HEADS + 1))

    def to_scratch(self, name, first, tiles, func, dst, h_hi, h_lo, **others):
        stored = [self.sem(f"{name}_stored{i}") for i in range(2)]
        with ExitStack() as c:
            buf = self.sb(c, f"{name}_buf", [P, 2, T])

            def act_out(act, j, s, acc, emptied):
                act.wait_ge(stored[s], j * 8 + (16 - 8 * s))
                act.activation(buf[:, s], acc, func).then_inc(emptied, 1)
                act.wait_ge(emptied, j + 3)
                act.dma_start(dst[bass.ds(j, 1)].rearrange("o p t -> (o p) t"), buf[:, s]).then_inc(stored[s], 16)
            with self.nc.Block() as block:
                @block.tensor
                def _(pe):
                    for s in range(2):
                        pe.sem_inc(stored[s], 16)
            self.projection(name, self.a["w_in"], first, h_hi, h_lo, tiles, act_out=act_out, **others)
            with self.nc.Block() as block:
                @block.sync
                def _(sp):
                    for s in range(2):
                        sp.wait_ge(stored[s], 16 * (tiles // 2 + 1))

    def gates(self, h_hi, h_lo):
        nc, a = self.nc, self.a
        TILES = 2 * KT
        MADE = NMOD - 2 * TILES
        c_loaded = self.sem("gates_c_loaded")
        ada_loaded = [self.sem(f"gates_ada_loaded{s}") for s in range(2)]
        multiplied = self.sem("gates_multiplied")
        dotted = self.sem("gates_dotted")
        chain = self.sem("gates_chain")
        with ExitStack() as c:
            ada = self.sb(c, "gates_ada", [P, 2, 2, D])
            products = self.sb(c, "gates_products", [P, 2, 2, D])
            cb = self.sb(c, "gates_cb", [P, D])

            def dve_out(dve, j, s, acc, emptied):
                dve.wait_ge(ada_loaded[s], j * 8 + (16 - 8 * s))
                dve.wait_ge(dotted, j + 1)
                dve.tensor_tensor(products[:, s], ada[:, s], cb[:].unsqueeze(1).to_broadcast([P, 2, D]), ALU.mult).then_inc(multiplied, 1)
                dve.wait_ge(multiplied, j + 3)
                dve.tensor_reduce(self.mod[:, bass.ds(j * 2 + MADE, 2)], products[:, s], AXX, ALU.add).then_inc(dotted, 1)

            def pool_program(pool, emptied):
                with pool.Fori(0, TILES // 2) as it:
                    at = [pool.snap(it * 4 + (2 * s + MADE)) for s in range(2)]
                    for s in range(2):
                        pool.wait_ge(multiplied, it * 2 + (s + 1))
                        pool.dma_start(ada[:, s], a["w_adaT"][:, bass.ds(at[s], 2), :]).then_inc(ada_loaded[s], 16)
            with nc.Block() as block:
                @block.sync
                def _(sp):
                    sp.dma_start(cb[:], a["c"].to_broadcast([P, D])).then_inc(c_loaded, 16)

                @block.scalar
                def _(act):
                    act.wait_ge(c_loaded, 16)
                    act.activation(cb[:], cb[:], ACT.Silu).then_inc(chain, 1)

                @block.vector
                def _(dve):
                    dve.sem_inc(multiplied, 2)
                    dve.sem_inc(dotted, 2)
            self.to_scratch("gates", GA0, TILES, ACT.Sigmoid, self.gate_scr, h_hi, h_lo, dve_out=dve_out, pool_program=pool_program)
            with nc.Block() as block:
                @block.vector
                def _(dve):
                    dve.wait_ge(dotted, TILES + 2)
                    dve.tensor_tensor(self.mod[:, MADE:NMOD], self.mod[:, MADE:NMOD], self.b_ada[:, MADE:NMOD], ALU.add).then_inc(chain, 1)
                    dve.wait_ge(chain, 2)
                    K = KT
                    gt1, sc2, gt2 = (self.mod[:, K * i:K * i + K] for i in (2, 4, 5))
                    post1, pre2, post2 = (self.vecs[:, K * i:K * i + K] for i in range(1, 4))
                    dve.tensor_tensor(self.coef[:, K:2 * K], gt1, post1, ALU.mult)
                    dve.scalar_tensor_tensor(self.coef[:, 2 * K:3 * K], sc2, 1.0, pre2, ALU.add, ALU.mult)
                    dve.tensor_tensor(self.coef[:, 3 * K:4 * K], gt2, post2, ALU.mult)

    def gmlp(self, h_hi, h_lo):
        nc, a, ps = self.nc, self.a, self.psum
        self.to_scratch("zu", ZU0, KT, ACT.Gelu_apprx_tanh, self.u_scr, h_hi, h_lo)
        with ExitStack() as c:
            w = self.sb(c, "sp_w", [P, KT, P])
            bias = self.sb(c, "sp_bias", [P, KT, P])
            zv = self.sb(c, "zv", [P, KT, T])
            tables = self.sem("spatial_tables")

            def act_out(act, j, s, acc, emptied):
                act.activation(zv[:, bass.ds(j, 1)].rearrange("p o t -> p (o t)"), acc, ACT.Gelu_apprx_tanh).then_inc(emptied, 1)
            total = self.sb(c, "zv_total_t", [P, T])
            summed = self.sem("zv_so_far")

            def dve_out(dve, j, s, acc, emptied):
                dve.wait_ge(emptied, j + 3)
                dve.wait_ge(summed, j + 1)
                dve.tensor_tensor(total[:], total[:], zv[:, bass.ds(j, 1)].rearrange("p o t -> p (o t)"), ALU.add).then_inc(summed, 1)
            with nc.Block() as block:
                @block.sync
                def _(sp):
                    sp.dma_start(w[:].rearrange("q g p -> q (g p)"), a["w_spatial"]).then_inc(tables, 16)
                    sp.dma_start(bias[:].rearrange("q g p -> q (g p)"), a["b_spatial"].to_broadcast([P, KT * P])).then_inc(tables, 16)

                @block.vector
                def _(dve):
                    dve.memset(total[:], 0.0).then_inc(summed, 1)
            self.projection("zv", a["w_in"], ZV0, h_hi, h_lo, KT, act_out=act_out, dve_out=dve_out)
            rstd = self.sb(c, "zv_rstd_t", [P, T])
            mean_done = self.sem("zv_mean")
            centred = self.sem("zv_centred")
            with nc.Block() as block:
                @block.tensor
                def _(pe):
                    for half in range(2):
                        last = pe.matmul(ps[:, half], self.ones_mean[:], total[:, half * HALF:(half + 1) * HALF], start=True, stop=True)
                    last.then_inc(mean_done, 1)

                @block.vector
                def _(dve):
                    dve.wait_ge(mean_done, 1)
                    for k in range(KT):
                        dve.tensor_tensor(zv[:, k], zv[:, k], ps[:, 0:2].rearrange("p b t -> p (b t)"), ALU.subtract).then_inc(centred, 1)
            with ExitStack() as s:
                self.mean_square("zv", zv, rstd, self.sb(s, "zv_sq", [P, 2, T]))
            self.spatial(zv, rstd, w, bias, tables)

    def spatial(self, zv, rstd, w, bias, tables):
        nc, a, ps = self.nc, self.a, self.psum
        G = KT
        turned = [ps[:, 2 * s:2 * s + 2].rearrange("p b t -> p (b t)") for s in range(2)]
        sv = [ps[:, 4 + 2 * s:6 + 2 * s].rearrange("p b t -> p (b t)") for s in range(2)]
        w_hi_done = self.sem("spatial_w_hi")
        w_split = self.sem("spatial_w_split")
        normed = self.sem("spatial_normed")
        affined = self.sem("spatial_affined")
        v_turned = self.sem("spatial_turned")
        v_hi_done = self.sem("spatial_v_hi")
        v_split = self.sem("spatial_v_split")
        mixed = self.sem("spatial_mixed")
        biased = self.sem("spatial_biased")
        gated = self.sem("spatial_gated")
        u_loaded = [self.sem(f"spatial_u_loaded{s}") for s in range(2)]
        stored = [self.sem(f"spatial_stored{s}") for s in range(2)]
        ln_g, ln_b = self.vecs[:, 4 * KT:5 * KT], self.vecs[:, 5 * KT:6 * KT]

        def arrivals(j, s):
            return j * 8 + (16 - 8 * s)
        with ExitStack() as c:
            w_hi = self.sb(c, "sp_w_hi", [P, G, P], F32R)
            w_lo = self.sb(c, "sp_w_lo", [P, G, P], F32R)
            u = self.sb(c, "sp_u", [P, 2, T])
            v = self.sb(c, "sp_v", [P, 2, T])
            v_hi = self.sb(c, "sp_v_hi", [P, 2, T], F32R)
            v_lo = self.sb(c, "sp_v_lo", [P, 2, T], F32R)
            sg = self.sb(c, "sp_sg", [P, 2, T])
            with nc.Block() as block:
                @block.sync
                def _(sp):
                    with sp.Fori(0, G // 2) as it:
                        at = [sp.snap(it * 2 + s) for s in range(2)]
                        ready = [sp.snap(it * 2 + (s + 3)) for s in range(2)]
                        free = [sp.snap(it * 2 + (s + 1)) for s in range(2)]
                        for s in range(2):
                            sp.wait_ge(gated, free[s])
                            sp.dma_start(u[:, s], self.u_scr[bass.ds(at[s], 1)].rearrange("o p t -> (o p) t")).then_inc(u_loaded[s], 16)
                        for s in range(2):
                            sp.wait_ge(gated, ready[s])
                            sp.dma_start(self.sg_scr[bass.ds(at[s], 1)].rearrange("o p t -> (o p) t"), sg[:, s]).then_inc(stored[s], 16)
                    for s in range(2):
                        sp.wait_ge(stored[s], 16 * (G // 2 + 1))

                @block.gpsimd
                def _(pool):
                    with pool.Fori(0, G // 2) as it:
                        for s in range(2):
                            pool.wait_ge(u_loaded[s], arrivals(it * 2 + s, s))
                            pool.wait_ge(biased, it * 2 + (s + 3))
                            pool.tensor_tensor(sg[:, s], sg[:, s], u[:, s], ALU.mult).then_inc(gated, 1)

                @block.scalar
                def _(act):
                    act.wait_ge(tables, 32)
                    act.activation(w_hi[:], w[:], ACT.Copy).then_inc(w_hi_done, 1)

                    def affine(j, s):
                        act.wait_ge(normed, j + 1)
                        act.activation(v[:, s], v[:, s], ACT.Identity, bias=ln_b[:, bass.ds(j, 1)], scale=ln_g[:, bass.ds(j, 1)]).then_inc(affined, 1)

                    def high(j, s):
                        act.wait_ge(v_turned, j + 1)
                        act.wait_ge(mixed, j + 1)
                        act.activation(v_hi[:, s], turned[s], ACT.Copy).then_inc(v_hi_done, 1)
                    affine(0, 0)
                    affine(1, 1)
                    high(0, 0)
                    with act.Fori(0, G // 2 - 1) as it:
                        for s in range(2):
                            high(it * 2 + (s + 1), 1 - s)
                            affine(it * 2 + (s + 2), s)
                    high(G - 1, 1)

                @block.vector
                def _(dve):
                    dve.sem_inc(gated, 2)
                    dve.sem_inc(biased, 2)
                    dve.wait_ge(w_hi_done, 1)
                    dve.tensor_tensor(w_lo[:], w[:], w_hi[:].bitcast(F32), ALU.subtract).then_inc(w_split, 1)

                    def norm(j, s):
                        dve.tensor_tensor(v[:, s], zv[:, bass.ds(j, 1)].rearrange("p o t -> p (o t)"), rstd[:], ALU.mult).then_inc(normed, 1)

                    def low(j, s):
                        dve.wait_ge(v_hi_done, j + 1)
                        dve.tensor_tensor(v_lo[:, s], turned[s], v_hi[:, s].bitcast(F32), ALU.subtract).then_inc(v_split, 1)

                    def finish(j, s):
                        dve.wait_ge(mixed, j + 3)
                        dve.wait_ge(stored[s], arrivals(j, s))
                        dve.tensor_tensor(sg[:, s].rearrange("h (c p) -> h c p", p=P), sv[s].rearrange("h (c p) -> h c p", p=P),
                                          bias[:, bass.ds(j, 1)].to_broadcast([P, TB, P]), ALU.add).then_inc(biased, 1)
                    norm(0, 0)
                    norm(1, 1)
                    low(0, 0)
                    with dve.Fori(0, G // 2 - 1) as it:
                        for s in range(2):
                            dve.wait_ge(v_turned, it * 2 + (s + 1))
                            norm(it * 2 + (s + 2), s)
                            low(it * 2 + (s + 1), 1 - s)
                            finish(it * 2 + s, s)
                    low(G - 1, 1)
                    finish(G - 2, 0)
                    finish(G - 1, 1)

                @block.tensor
                def _(pe):
                    pe.sem_inc(mixed, 2)
                    for s in range(2):
                        pe.sem_inc(stored[s], 16)
                    pe.wait_ge(w_split, 1)

                    def turn(j, s):
                        pe.wait_ge(affined, j + 1)
                        for k in range(TB):
                            last = pe.transpose(turned[s][:, k * P:(k + 1) * P], v[:, s, k * P:(k + 1) * P], self.ident[:])
                        last.then_inc(v_turned, 1)

                    def mix(j, s):
                        pe.wait_ge(v_split, j + 1)
                        pe.wait_ge(biased, j + 1)
                        for k in range(TB):
                            cols = slice(k * P, (k + 1) * P)
                            wh = w_hi[:, bass.ds(j, 1)].rearrange("q o p -> q (o p)")
                            wl = w_lo[:, bass.ds(j, 1)].rearrange("q o p -> q (o p)")
                            pe.matmul(sv[s][:, cols], v_hi[:, s, cols], wh, start=True, stop=False)
                            pe.matmul(sv[s][:, cols], v_hi[:, s, cols], wl, start=False, stop=False)
                            last = pe.matmul(sv[s][:, cols], v_lo[:, s, cols], wh, start=False, stop=True)
                        last.then_inc(mixed, 1)
                    turn(0, 0)
                    turn(1, 1)
                    with pe.Fori(0, G // 2 - 1) as it:
                        for s in range(2):
                            mix(it * 2 + s, s)
                            turn(it * 2 + (s + 2), s)
                    mix(G - 2, 0)
                    mix(G - 1, 1)

    def branches(self, wide, m_hi, m_lo):
        with ExitStack() as c:
            with ExitStack() as s:
                self.head_norm(self.sb(s, "o_all", [P, HEADS, T]), m_hi, m_lo)
            sg_hi = self.sb(c, "sg_hi", [P, KT, T], F32R)
            sg_lo = self.sb(c, "sg_lo", [P, KT, T], F32R)
            self.attention_branch(wide, m_hi, m_lo, sg_hi, sg_lo)
            self.spatial_branch(wide, sg_hi, sg_lo, m_hi, m_lo)

    def head_norm(self, o, hi, lo):
        nc, ps = self.nc, self.psum
        loaded = [self.sem(f"head_loaded{h}") for h in range(HEADS)]
        squared = self.sem("head_squared")
        meaned = self.sem("head_meaned")
        eps_added = self.sem("head_eps")
        rooted = self.sem("head_rooted")
        inverse = self.sem("head_inverse")
        on_diag = self.sem("head_diag")
        spread = self.sem("head_spread")
        normed = self.sem("head_normed")
        hi_done = self.sem("head_hi")
        lo_done = self.sem("head_lo")
        with ExitStack() as c:
            sq = self.sb(c, "head_sq", [P, 2, T])
            token = self.sb(c, "head_token", [P, HEADS * TB])
            with nc.Block() as block:
                @block.sync
                def _(sp):
                    for h in range(HEADS):
                        sp.dma_start(o[:, h], self.o_scr[h]).then_inc(loaded[h], 16)

                @block.scalar
                def _(act):
                    for h in range(HEADS):
                        act.wait_ge(loaded[h], 16)
                        if h >= 2:
                            act.wait_ge(meaned, h - 1)
                        act.activation(sq[:, h % 2], o[:, h], ACT.Square).then_inc(squared, 1)
                    act.wait_ge(eps_added, 1)
                    act.activation(token[:], token[:], ACT.Sqrt).then_inc(rooted, 1)
                    for h in range(HEADS):
                        act.wait_ge(normed, h + 1)
                        act.activation(hi[:, h], o[:, h], ACT.Copy).then_inc(hi_done, 1)

                @block.tensor
                def _(pe):
                    for h in range(HEADS):
                        pe.wait_ge(squared, h + 1)
                        self.square_means(pe, ps[:, 4], sq[:, h % 2], self.ones_head, h * TB).then_inc(meaned, 1)
                    for h in range(HEADS):
                        pe.wait_ge(on_diag, h + 1)
                        if h >= 2:
                            pe.wait_ge(normed, h - 1)
                        self.broadcast_rows(pe, [ps[:, 2 * (h % 2)], ps[:, 2 * (h % 2) + 1]], sq[:, h % 2]).then_inc(spread, 1)

                @block.vector
                def _(dve):
                    def diagonals(h):
                        if h >= 2:
                            dve.wait_ge(spread, h - 1)
                        self.to_diagonals(dve, sq[:, h % 2], token[:, h * TB:(h + 1) * TB]).then_inc(on_diag, 1)
                    dve.wait_ge(meaned, HEADS)
                    dve.tensor_scalar(token[:], ps[:, 4, 0:HEADS * TB], EPS, None, ALU.add).then_inc(eps_added, 1)
                    dve.wait_ge(rooted, 1)
                    dve.reciprocal(token[:], token[:]).then_inc(inverse, 1)
                    dve.wait_ge(inverse, 1)
                    diagonals(0)
                    diagonals(1)
                    for h in range(HEADS):
                        dve.wait_ge(spread, h + 1)
                        dve.scalar_tensor_tensor(o[:, h], o[:, h], self.subln_gain[:, 0:1],
                                                 ps[:, 2 * (h % 2):2 * (h % 2) + 2].rearrange("p b t -> p (b t)"),
                                                 ALU.mult, ALU.mult).then_inc(normed, 1)
                        if h + 2 < HEADS:
                            diagonals(h + 2)
                        dve.wait_ge(hi_done, h + 1)
                        dve.tensor_tensor(lo[:, h], o[:, h], hi[:, h].bitcast(F32), ALU.subtract).then_inc(lo_done, 1)

    def load_gates(self, gate, first, g_loaded, also=lambda pool, it, s: None):
        def program(pool, emptied):
            with pool.Fori(0, KT // 2) as it:
                at = [pool.snap(it * 2 + (s + first)) for s in range(2)]
                for s in range(2):
                    pool.wait_ge(emptied, it * 2 + (s + 1))
                    pool.dma_start(gate[:, s], self.gate_scr[bass.ds(at[s], 1)].rearrange("o p t -> (o p) t")).then_inc(g_loaded[s], 16)
                    also(pool, it, s)
        return program

    def attention_branch(self, wide, x_hi, x_lo, sg_hi, sg_lo):
        g_loaded = [self.sem(f"attn_gate_loaded{i}") for i in range(2)]
        sg_loaded = [self.sem(f"attn_sg_loaded{i}") for i in range(2)]
        held = self.sem("attn_held")
        sg_hi_done = self.sem("attn_sg_hi")
        sg_split = self.sem("attn_sg_split")
        column = lambda w, j: w[:, bass.ds(j, 1)].rearrange("p o t -> p (o t)")
        with ExitStack() as c:
            gate = self.sb(c, "attn_gate", [P, 2, T])
            raw = self.sb(c, "attn_sg_raw", [P, 2, T])

            def act_out(act, j, s, acc, emptied):
                act.wait_ge(sg_loaded[s], j * 8 + (16 - 8 * s))
                act.activation(column(sg_hi, j), raw[:, s], ACT.Copy).then_inc(sg_hi_done, 1)

            def dve_out(dve, j, s, acc, emptied):
                dve.wait_ge(g_loaded[s], j * 8 + (16 - 8 * s))
                dve.tensor_tensor(column(wide, j), acc, gate[:, s], ALU.mult).then_inc(emptied, 1)
                dve.wait_ge(sg_hi_done, j + 1)
                dve.tensor_tensor(column(sg_lo, j), raw[:, s], column(sg_hi, j).bitcast(F32), ALU.subtract).then_inc(sg_split, 1)

            def load_sg(pool, it, s):
                pool.wait_ge(sg_split, it * 2 + (s + 1))
                pool.sem_inc(held, 1)
                pool.dma_start(raw[:, s], self.sg_scr[bass.ds(it * 2 + s, 1)].rearrange("o p t -> (o p) t")).then_inc(sg_loaded[s], 16)
            with self.nc.Block() as block:
                @block.vector
                def _(dve):
                    dve.sem_inc(sg_split, 2)
            self.projection("attn", self.a["w_attn"], 0, x_hi, x_lo, KT, act_out=act_out, dve_out=dve_out,
                            pool_program=self.load_gates(gate, 0, g_loaded, load_sg))

    def spatial_branch(self, wide, x_hi, x_lo, m_hi, m_lo):
        g_loaded = [self.sem(f"spat_gate_loaded{i}") for i in range(2)]
        added = self.sem("spat_added")
        m_hi_done = self.sem("spat_m_hi")
        m_split = self.sem("spat_m_split")
        column = lambda w, j: w[:, bass.ds(j, 1)].rearrange("p o t -> p (o t)")
        with ExitStack() as c:
            gate = self.sb(c, "spat_gate", [P, 2, T])
            term = self.sb(c, "spat_term", [P, 2, T])

            def act_out(act, j, s, acc, emptied):
                act.wait_ge(added, j + 1)
                act.activation(column(m_hi, j), column(wide, j), ACT.Copy).then_inc(m_hi_done, 1)

            def dve_out(dve, j, s, acc, emptied):
                dve.wait_ge(g_loaded[s], j * 8 + (16 - 8 * s))
                dve.tensor_tensor(term[:, s], acc, gate[:, s], ALU.mult).then_inc(emptied, 1)
                dve.wait_ge(emptied, j + 3)
                dve.tensor_tensor(column(wide, j), column(wide, j), term[:, s], ALU.add).then_inc(added, 1)
                dve.wait_ge(m_hi_done, j + 1)
                dve.tensor_tensor(column(m_lo, j), column(wide, j), column(m_hi, j).bitcast(F32), ALU.subtract).then_inc(m_split, 1)
            self.projection("spat", self.a["w_gmlp"], 0, x_hi, x_lo, KT, act_out=act_out, dve_out=dve_out,
                            pool_program=self.load_gates(gate, KT, g_loaded))

    def out_projection(self, wide, m_hi, m_lo, total):
        squared = self.sem("out_squared")
        summed = self.sem("out_summed")
        with ExitStack() as c:
            sq = self.sb(c, "out_sq", [P, 2, T])

            def act_out(act, j, s, acc, emptied):
                act.wait_ge(summed, j + 1)
                act.activation(sq[:, s], acc, ACT.Square).then_inc(squared, 1)
                act.activation(wide[:, bass.ds(j, 1)].rearrange("p o t -> p (o t)"), acc, ACT.Copy).then_inc(emptied, 1)

            def dve_out(dve, j, s, acc, emptied):
                dve.wait_ge(squared, j + 1)
                dve.wait_ge(summed, j + 2)
                dve.tensor_tensor(total[:], total[:], sq[:, s], ALU.add).then_inc(summed, 1)
            with self.nc.Block() as block:
                @block.vector
                def _(dve):
                    dve.memset(total[:], 0.0).then_inc(summed, 1)
                    dve.sem_inc(summed, 1)
            self.projection("out", self.a["w_out"], 0, m_hi, m_lo, KT, act_out=act_out, dve_out=dve_out)

    def add_normed(self, name, y, coef, base_dram, x1, dst_dram, total=None, squares_too=False):
        nc, ps = self.nc, self.psum
        loaded = self.sem(f"{name}_base_loaded")
        scaled = self.sem(f"{name}_scaled")
        added = self.sem(f"{name}_added")
        stored = self.sem(f"{name}_stored")
        squared = self.sem(f"{name}_x1_squared")
        meaned = self.sem(f"{name}_x1_meaned")
        with ExitStack() as c:
            rstd = self.sb(c, f"{name}_rstd_t", [P, T])
            sq = self.sb(c, f"{name}_sq", [P, 2, T])
            with nc.Block() as block:
                @block.sync
                def _(sp):
                    sp.dma_start(x1[:], base_dram).then_inc(loaded, 16)
            self.mean_square(name, y, rstd, sq, total=total)
            with nc.Block() as block:
                @block.sync
                def _(sp):
                    for k in range(KT):
                        sp.wait_ge(added, k + 1)
                        sp.dma_start(dst_dram[:, k], x1[:, k]).then_inc(stored, 16)
                    sp.wait_ge(stored, 16 * KT)

                @block.vector
                def _(dve):
                    def scale(k):
                        dve.tensor_tensor(y[:, k], y[:, k], rstd[:], ALU.mult).then_inc(scaled, 1)
                    scale(0)
                    dve.wait_ge(loaded, 16)
                    for k in range(KT):
                        if k + 1 < KT:
                            scale(k + 1)
                        dve.wait_ge(scaled, k + 1)
                        dve.scalar_tensor_tensor(x1[:, k], y[:, k], coef[:, k:k + 1], x1[:, k], ALU.mult, ALU.add).then_inc(added, 1)

                if squares_too:
                    @block.scalar
                    def _(act):
                        for k in range(KT):
                            act.wait_ge(added, k + 1)
                            if k >= 2:
                                act.wait_ge(meaned, k - 1)
                            act.activation(sq[:, k % 2], x1[:, k], ACT.Square).then_inc(squared, 1)

                    @block.tensor
                    def _(pe):
                        for k in range(KT):
                            pe.wait_ge(squared, k + 1)
                            self.square_means(pe, ps[:, 0], sq[:, k % 2], self.ones_mean, k * TB).then_inc(meaned, 1)

    def finish(self, wide):
        with ExitStack() as c:
            x1 = self.sb(c, "x_out", [P, KT, T])
            self.add_normed("final", wide, self.coef[:, 3 * KT:4 * KT], self.x1_scr.rearrange("k p t -> p k t"), x1,
                            self.a["out"].rearrange("(k p) t -> p k t", p=P))

    def route(self, h2_hi, h2_lo):
        with ExitStack() as c:
            vals = self.sb(c, "top_vals", [P, TB, SIDES, TOPK])
            idxs = self.sb(c, "top_idxs", [P, TB, SIDES, TOPK], F16)
            self.side_tops(h2_hi, h2_lo, vals, idxs)
            self.stage_end()
            self.scatter_weights(vals, idxs, h2_hi, h2_lo)
            self.stage_end()

    def side_tops(self, h2_hi, h2_lo, vals, idxs):
        nc, a, ps = self.nc, self.a, self.psum
        keys_loaded = self.sem("keys_loaded")
        keys_hi_done = self.sem("keys_hi")
        keys_split = self.sem("keys_split")
        q_hi_done = self.sem("rq_hi")
        q_split = self.sem("rq_emptied_too")
        scored = self.sem("rq_scored")
        tops = self.sem("rq_tops")
        held = self.sem("rq_held")
        NTOPS = 5 * TB + 2
        with ExitStack() as c:
            k_raw = self.sb(c, "k_raw", [P, SIDES, KEYS])
            k_hi = self.sb(c, "k_hi", [P, SIDES, KEYS], F32R)
            k_lo = self.sb(c, "k_lo", [P, SIDES, KEYS], F32R)
            with nc.Block() as block:
                @block.sync
                def _(sp):
                    sp.dma_start(k_raw[:].rearrange("d s n -> d (s n)"), a["keysT"]).then_inc(keys_loaded, 16)

                @block.scalar
                def _(act):
                    act.wait_ge(keys_loaded, 16)
                    act.activation(k_hi[:], k_raw[:], ACT.Copy).then_inc(keys_hi_done, 1)

                @block.vector
                def _(dve):
                    dve.wait_ge(keys_hi_done, 1)
                    dve.tensor_tensor(k_lo[:], k_raw[:], k_hi[:].bitcast(F32), ALU.subtract).then_inc(keys_split, 1)
            q_hi = self.sb(c, "rq_hi_t", [P, 2, T], F32R)
            q_lo = self.sb(c, "rq_lo_t", [P, 2, T], F32R)
            work = self.sb(c, "rq_work", [P, TB, KEYS])
            top_v = self.sb(c, "rq_top_v", [P, TB, TOPK])
            top_i = self.sb(c, "rq_top_i", [P, TB, TOPK], U32)
            score = [ps[:, 4 + 2 * s:6 + 2 * s].rearrange("p b (c n) -> p (b c) n", n=KEYS) for s in range(2)]

            def act_out(act, j, s, acc, emptied):
                act.wait_ge(scored, j + 1)
                act.activation(q_hi[:, s], acc, ACT.Copy).then_inc(q_hi_done, 1)

            def dve_out(dve, j, s, acc, emptied):
                dve.wait_ge(q_hi_done, j + 1)
                dve.tensor_tensor(q_lo[:, s], acc, q_hi[:, s].bitcast(F32), ALU.subtract).then_inc(emptied, 1)

            def top(dve, j, s):
                n = [0]

                def all_so_far():
                    dve.wait_ge(tops, j * NTOPS + (n[0] + 2 * NTOPS))
                    dve.sem_inc(held, 1)

                def done(ins):
                    ins.then_inc(tops, 1)
                    n[0] += 1
                dve.wait_ge(scored, j + 3)
                all_so_far()
                for b in range(TB):
                    done(dve.max(top_v[:, b, 0:8], score[s][:, b]))
                all_so_far()
                for b in range(TB):
                    done(dve.match_replace(work[:, b], top_v[:, b, 0:8], score[s][:, b], LOWEST))
                for b in range(TB):
                    done(dve.max_index(top_i[:, b, 0:8], top_v[:, b, 0:8], score[s][:, b]))
                all_so_far()
                for b in range(TB):
                    done(dve.max(top_v[:, b, 8:16], work[:, b]))
                all_so_far()
                for b in range(TB):
                    done(dve.max_index(top_i[:, b, 8:16], top_v[:, b, 8:16], work[:, b]))
                all_so_far()
                done(dve.tensor_copy(vals[:, :, bass.ds(j, 1)].rearrange("p b o k -> p b (o k)"), top_v[:]))
                done(dve.tensor_copy(idxs[:, :, bass.ds(j, 1)].rearrange("p b o k -> p b (o k)"), top_i[:]))
                assert n[0] == NTOPS

            def pe_after(pe, j, s, emptied):
                pe.wait_ge(emptied, j + 3)
                pe.wait_ge(tops, j * NTOPS + NTOPS)
                kh = k_hi[:, bass.ds(j, 1)].rearrange("d o n -> d (o n)")
                kl = k_lo[:, bass.ds(j, 1)].rearrange("d o n -> d (o n)")
                for b in range(TB):
                    q = slice(b * P, (b + 1) * P)
                    pe.matmul(score[s][:, b], q_hi[:, s, q], kh, start=True, stop=False)
                    pe.matmul(score[s][:, b], q_hi[:, s, q], kl, start=False, stop=False)
                    last = pe.matmul(score[s][:, b], q_lo[:, s, q], kh, start=False, stop=True)
                last.then_inc(scored, 1)
            with nc.Block() as block:
                @block.vector
                def _(dve):
                    dve.sem_inc(tops, 2 * NTOPS)
                    dve.sem_inc(scored, 2)
            self.projection("rq", a["w_peer"], 0, h2_hi, h2_lo, SIDES, act_out=act_out, dve_out=dve_out,
                            pe_after=pe_after, dve_after=top)

    def scatter_weights(self, vals, idxs, h2_hi, h2_lo):
        nc, a, ps = self.nc, self.a, self.psum
        SEL = HEADS * TOPK
        GROUP, QUAD = 8, 4
        PIECES = 4
        GROUPS = P // GROUP
        QUADS = P // QUAD
        PER_BLOCK = EARLY // TB
        chain = self.sem("sc_chain")
        held = self.sem("sc_held")
        exp_in = self.sem("sc_exp_in")
        exp_out = self.sem("sc_exp_out")
        chosen = self.sem("sc_chosen")
        turned = self.sem("sc_turned")
        first_hot = self.sem("sc_first_hot")
        onehots = self.sem("sc_onehots")
        matrices = self.sem("sc_matrices")
        staged = self.sem("sc_staged")
        stored = self.sem("sc_stored")
        iotas = self.sem("sc_iotas")
        u_loaded = self.sem("sc_u_loaded")
        u_hi_done = self.sem("sc_u_hi")
        u_split = self.sem("sc_u_split")
        hidden = self.sem("sc_hidden")
        gelu_done = self.sem("sc_gelu")
        h_stored = self.sem("sc_h_stored")
        hid = [ps[:, 2 * s:2 * s + 2].rearrange("p b t -> p (b t)") for s in range(2)]
        with ExitStack() as c:
            cand = self.sb(c, "sc_cand", [P, HEADS, TOPK, TOPK])
            cand2 = self.sb(c, "sc_cand2", [P, HEADS, TOPK * TOPK])
            best = self.sb(c, "sc_best", [P, HEADS, TOPK])
            pos = self.sb(c, "sc_pos", [P, HEADS, TOPK], U32)
            pos_i = self.sb(c, "sc_pos_i", [P, 2, SEL], U32)
            pos_h = self.sb(c, "sc_pos_h", [P, 2, SEL], F16)
            norm = self.sb(c, "sc_norm", [P, 2, HEADS])
            picks = self.sb(c, "sc_picks", [P, 3, SEL])
            scaled = self.sb(c, "sc_scaled", [SEL, P])
            rows = self.sb(c, "sc_rows_t", [SEL, 4, P], F16)
            iota16 = self.sb(c, "sc_iota16", [P, TOPK], F16)
            key_of = self.sb(c, "sc_key_of", [SEL, KEYS, GROUP], F16)
            first = self.sb(c, "sc_first", [SEL, 2, KEYS, GROUP], F16)
            second = self.sb(c, "sc_second", [SEL, 2, KEYS, GROUP], F16)
            w_hi = self.sb(c, "sc_w_hi", [SEL, 2, KEYS, GROUP], F16)
            w_lo = self.sb(c, "sc_w_lo", [SEL, 2, KEYS, GROUP], F16)
            stage = self.sb(c, "sc_stage", [P, KEYS, P])
            u_raw = self.sb(c, "sc_u_raw", [P, D])
            u_hi = self.sb(c, "sc_u_hi_t", [P, 2, KT, P], F32R)
            u_lo = self.sb(c, "sc_u_lo_t", [P, 2, KT, P], F32R)
            gelu = self.sb(c, "sc_gelu_t", [P, T])
            flat = lambda w, s: w[:, s].rearrange("p k n -> p (k n)")
            with nc.Block() as block:
                @block.sync
                def _(sp):
                    dst = self.route_scr.rearrange("i j (b t) -> b j i t", t=P)

                    def load(at):
                        sp.dma_start(u_raw[:], a["peer_uT"][bass.ds(at, 1)].rearrange("o p n -> (o p) n")).then_inc(u_loaded, 16)
                    def blocks_loads(b):
                        snap = sp.snap if not isinstance(b, int) else (lambda value: value)
                        chunk = [snap(b * PER_BLOCK + i) for i in (4, 5, 6)]
                        free = [snap(b * PER_BLOCK + (i + 1)) for i in (4, 5, 6)]
                        for i in range(3):
                            sp.wait_ge(u_split, free[i])
                            load(chunk[i])

                    def store(at, piece):
                        k = slice(piece * KEYS // PIECES, (piece + 1) * KEYS // PIECES)
                        sp.dma_start(dst[bass.ds(at, 1), :, k].rearrange("o j i t -> (o j) i t"), stage[:, k]).then_inc(stored, 16)
                    load(0)
                    for j in range(1, 4):
                        sp.wait_ge(u_split, j + 1)
                        load(j)
                    with sp.Fori(0, TB - 1) as b:
                        at = sp.snap(b + 0)
                        blocks_loads(b)
                        ready = sp.snap(b * QUADS + (QUADS + 4))
                        next_chunk = [sp.snap(b * PER_BLOCK + i) for i in (7, 8)]
                        next_free = [sp.snap(b * PER_BLOCK + (i + 1)) for i in (7, 8)]
                        piece_stored = [sp.snap(b * 16 * PIECES + 16 * (i + 2)) for i in range(PIECES)]
                        sp.wait_ge(staged, ready)
                        store(at, 0)
                        sp.wait_ge(u_split, next_free[0])
                        load(next_chunk[0])
                        sp.wait_ge(stored, piece_stored[0])
                        store(at, 1)
                        sp.wait_ge(stored, piece_stored[1])
                        store(at, 2)
                        sp.wait_ge(u_split, next_free[1])
                        load(next_chunk[1])
                        sp.wait_ge(stored, piece_stored[2])
                        store(at, 3)
                    blocks_loads(TB - 1)
                    sp.wait_ge(staged, QUADS * TB + 4)
                    for piece in range(PIECES):
                        store(TB - 1, piece)
                    sp.wait_ge(stored, 16 * (PIECES * TB + 1))
                    sp.wait_ge(h_stored, 16 * (EARLY + 1))

                @block.gpsimd
                def _(pool):
                    pool.iota(iota16[:], [[1, TOPK]], base=0, channel_multiplier=0, allow_small_or_imprecise_dtypes=True).then_inc(iotas, 1)
                    pool.iota(key_of[:], [[1, KEYS], [0, GROUP]], base=0, channel_multiplier=0, allow_small_or_imprecise_dtypes=True).then_inc(iotas, 1)
                    pool.sem_inc(u_split, 1)

                    def split(j, s):
                        pool.wait_ge(u_hi_done, j + 1)
                        pool.tensor_tensor(flat(u_lo, s), u_raw[:], flat(u_hi, s).bitcast(F32), ALU.subtract).then_inc(u_split, 1)
                    split(0, 0)
                    split(1, 1)
                    with pool.Fori(0, TB // 2) as two:
                        for i in range(2 * PER_BLOCK):
                            split(two * (2 * PER_BLOCK) + (i + 2), i % 2)

                @block.vector
                def _(dve):
                    dve.sem_inc(stored, 16)
                    dve.sem_inc(h_stored, 16)
                    dve.sem_inc(chain, 1)
                    dve.sem_inc(onehots, 2)
                    dve.wait_ge(iotas, 2)
                    LINKS = 56
                    with dve.Fori(0, TB) as b:
                        n = [0]

                        def do(ins):
                            n[0] += 1
                            ins.then_inc(chain, 1)

                        def all_so_far():
                            dve.wait_ge(chain, b * LINKS + (n[0] + 1))
                            dve.sem_inc(held, 1)
                        shape = [P, HEADS, TOPK, TOPK]
                        val = vals[:, bass.ds(b, 1)].rearrange("p o (h s) k -> p (o h) s k", s=2)
                        all_so_far()
                        do(dve.tensor_tensor(cand[:], val[:, :, 0].unsqueeze(3).to_broadcast(shape), val[:, :, 1].unsqueeze(2).to_broadcast(shape), ALU.add))
                        all_so_far()
                        cflat = [cand[:, h].rearrange("p a b -> p (a b)") for h in range(HEADS)]
                        for h in range(HEADS):
                            do(dve.max(best[:, h, 0:8], cflat[h]))
                        all_so_far()
                        for h in range(HEADS):
                            do(dve.match_replace(cand2[:, h], best[:, h, 0:8], cflat[h], LOWEST))
                        for h in range(HEADS):
                            do(dve.max_index(pos[:, h, 0:8], best[:, h, 0:8], cflat[h]))
                        all_so_far()
                        for h in range(HEADS):
                            do(dve.max(best[:, h, 8:16], cand2[:, h]))
                        all_so_far()
                        weight = picks[:, 2].rearrange("p (h k) -> p h k", k=TOPK)
                        dve.tensor_tensor(weight, best[:], best[:, :, 0:1].to_broadcast([P, HEADS, TOPK]), ALU.subtract).then_inc(exp_in, 1)
                        for h in range(HEADS):
                            do(dve.max_index(pos[:, h, 8:16], best[:, h, 8:16], cand2[:, h]))
                        all_so_far()
                        pflat = pos[:].rearrange("p h k -> p (h k)")
                        do(dve.tensor_single_scalar(pos_i[:, 0], pflat, 4, ALU.logical_shift_right))
                        do(dve.tensor_single_scalar(pos_i[:, 1], pflat, 15, ALU.bitwise_and))
                        all_so_far()
                        do(dve.tensor_copy(pos_h[:], pos_i[:]))
                        all_so_far()
                        half = lambda w: w.bitcast(F16)[:, 0:SEL * TOPK]
                        eq_flat = half(cand2[:].rearrange("p h c -> p (h c)"))
                        prod_flat = half(cand[:].rearrange("p h k a -> p (h k a)"))
                        eq = eq_flat.rearrange("p (k a) -> p k a", a=TOPK)
                        eq4 = eq_flat.rearrange("p (h k a) -> p h k a", h=HEADS, a=TOPK)
                        prod = prod_flat.rearrange("p (k a) -> p k a", a=TOPK)
                        prod4 = prod_flat.rearrange("p (h k a) -> p h k a", h=HEADS, a=TOPK)
                        idx = idxs[:, bass.ds(b, 1)].rearrange("p o (h s) k -> p (o h) s k", s=2)
                        for side in range(2):
                            do(dve.tensor_tensor(eq, pos_h[:, side].unsqueeze(2).to_broadcast([P, SEL, TOPK]),
                                                 iota16[:].unsqueeze(1).to_broadcast([P, SEL, TOPK]), ALU.is_equal))
                            all_so_far()
                            do(dve.tensor_tensor(prod4, eq4, idx[:, :, side].unsqueeze(2).to_broadcast(shape), ALU.mult))
                            all_so_far()
                            do(dve.tensor_reduce(picks[:, side], prod, AXX, ALU.add))
                        dve.wait_ge(exp_out, b + 1)
                        do(dve.tensor_reduce(norm[:, 0], weight, AXX, ALU.add))
                        all_so_far()
                        do(dve.reciprocal(norm[:, 1], norm[:, 0]))
                        all_so_far()
                        dve.tensor_tensor(weight, weight, norm[:, 1].unsqueeze(2).to_broadcast([P, HEADS, TOPK]), ALU.mult).then_inc(chosen, 1)
                        dve.wait_ge(turned, b + 1)
                        do(dve.tensor_copy(rows[:, 0:2].rearrange("k a t -> k (a t)"), ps[:, 4, 0:2 * P]))
                        do(dve.tensor_scalar(scaled[:], ps[:, 4, 2 * P:3 * P], WEIGHT_SCALE, None, ALU.mult))
                        all_so_far()
                        do(dve.tensor_copy(rows[:, 2], scaled[:]))
                        all_so_far()
                        do(dve.tensor_tensor(rows[:, 3], scaled[:], rows[:, 2], ALU.subtract))
                        all_so_far()
                        for q in range(GROUPS):
                            s = q % 2
                            row = lambda r: rows[:, r, q * GROUP:(q + 1) * GROUP].unsqueeze(1).to_broadcast([SEL, KEYS, GROUP])
                            dve.wait_ge(onehots, b * GROUPS + (q + 1))
                            dve.wait_ge(matrices, b * QUADS + (2 * q + 2))
                            dve.tensor_tensor(first[:, s], key_of[:], row(0), ALU.is_equal).then_inc(first_hot, 1)
                            dve.tensor_tensor(second[:, s], key_of[:], row(1), ALU.is_equal)
                            dve.wait_ge(first_hot, b * GROUPS + (q + 1))
                            dve.tensor_tensor(w_hi[:, s], first[:, s], row(2), ALU.mult)
                            dve.tensor_tensor(w_lo[:, s], first[:, s], row(3), ALU.mult).then_inc(onehots, 1)
                        dve.wait_ge(onehots, b * GROUPS + (GROUPS + 2))
                        assert n[0] == LINKS, n[0]

                @block.scalar
                def _(act):
                    def split(j, s):
                        act.wait_ge(u_loaded, j * 16 + 16)
                        act.activation(flat(u_hi, s), u_raw[:], ACT.Copy).then_inc(u_hi_done, 1)

                    def chunk(j, s):
                        act.wait_ge(hidden, j + 1)
                        act.wait_ge(h_stored, j * 16 + 16)
                        act.activation(gelu[:], hid[s], ACT.Gelu_apprx_tanh).then_inc(gelu_done, 1)
                        act.wait_ge(gelu_done, j + 3)
                        act.dma_start(self.h_scr[bass.ds(j, 1)].rearrange("o p t -> (o p) t"), gelu[:]).then_inc(h_stored, 16)
                        split(j + 2, s)
                    split(0, 0)
                    split(1, 1)
                    weight = picks[:, 2]

                    def block_of_tokens(b, j, odd):
                        chunk(j, odd)
                        act.wait_ge(exp_in, b + 1)
                        act.activation(weight, weight, ACT.Exp).then_inc(exp_out, 1)
                        chunk(j + 1, 1 - odd)
                        chunk(j + 2, odd)
                        act.wait_ge(stored, b * (16 * PIECES) + 16)
                        for q in range(QUADS):
                            act.wait_ge(matrices, b * QUADS + (q + 5))
                            act.activation(stage[:, :, q * QUAD:(q + 1) * QUAD].rearrange("j i t -> j t i"),
                                           ps[:, 4 + q % 4].rearrange("j (t i) -> j t i", i=KEYS), ACT.Copy).then_inc(staged, 1)
                            if q == QUADS // 2:
                                chunk(j + 3, 1 - odd)
                        chunk(j + 4, odd)
                    with act.Fori(0, TB // 2) as two:
                        for odd in range(2):
                            block_of_tokens(two * 2 + odd, two * (2 * PER_BLOCK) + odd * PER_BLOCK, odd)

                @block.tensor
                def _(pe):
                    pe.sem_inc(matrices, 4)
                    pe.sem_inc(staged, 4)
                    pe.sem_inc(gelu_done, 2)

                    def up_piece(s, k, half):
                        t = slice(half * HALF, (half + 1) * HALF)
                        return self.product3(pe, ps[:, 2 * s + half], u_hi[:, s, k], u_lo[:, s, k], h2_hi[:, k, t], h2_lo[:, k, t],
                                             k == 0, k == KT - 1)

                    def up_ready(j):
                        pe.wait_ge(u_split, j + 2)
                        pe.wait_ge(gelu_done, j + 1)
                    def block_of_tokens(b, j, odd):
                        for i in range(3):
                            up_ready(j + i)
                            for half in range(2):
                                for k in range(KT):
                                    last = up_piece((odd + i) % 2, k, half)
                            last.then_inc(hidden, 1)
                        pe.wait_ge(chosen, b + 1)
                        pe.wait_ge(staged, b * QUADS + 4)
                        for i in range(3):
                            last = pe.transpose(ps[:, 4, i * P:(i + 1) * P], picks[:, i], self.ident[:])
                        last.then_inc(turned, 1)
                        for q in range(GROUPS):
                            i, at = divmod(q, GROUPS // 2)
                            if at == 0:
                                up_ready(j + (3 + i))
                            for piece in (2 * at, 2 * at + 1):
                                last = up_piece((odd + 3 + i) % 2, piece % KT, piece // KT)
                            if at == GROUPS // 2 - 1:
                                last.then_inc(hidden, 1)
                            pe.wait_ge(onehots, b * GROUPS + (q + 3))
                            s = q % 2
                            for half in range(2):
                                quad = 2 * q + half
                                pe.wait_ge(staged, b * QUADS + (quad + 1))
                                for t in range(QUAD):
                                    to = ps[:, 4 + quad % 4, t * KEYS:(t + 1) * KEYS]
                                    tok = half * QUAD + t
                                    pe.matmul(to, second[:, s, :, tok], w_hi[:, s, :, tok], start=True, stop=False)
                                    last = pe.matmul(to, second[:, s, :, tok], w_lo[:, s, :, tok], start=False, stop=True)
                                last.then_inc(matrices, 1)
                    with pe.Fori(0, TB // 2) as two:
                        for odd in range(2):
                            block_of_tokens(two * 2 + odd, two * (2 * PER_BLOCK) + odd * PER_BLOCK, odd)

    def experts(self, h2_hi, h2_lo, y):
        nc, a, ps = self.nc, self.a, self.psum
        C = KEYS
        E = EARLY
        u_loaded = [self.sem(f"ex_u_loaded{i}") for i in range(2)]
        v_loaded = [self.sem(f"ex_v_loaded{i}") for i in range(2)]
        g_loaded = [self.sem(f"ex_g_loaded{i}") for i in range(2)]
        u_hi_done = self.sem("ex_u_hi")
        u_split = self.sem("ex_u_split")
        v_hi_done = self.sem("ex_v_hi")
        v_split = self.sem("ex_v_split")
        hidden = self.sem("ex_hidden")
        gelu_done = self.sem("ex_gelu")
        weighted = self.sem("ex_weighted")
        a_hi_done = self.sem("ex_a_hi")
        a_split = self.sem("ex_a_split")
        summed = self.sem("ex_summed")
        added = self.sem("ex_added")
        zeroed = self.sem("ex_zeroed")
        TILES = 2 * KT
        hid = [ps[:, 2 * s:2 * s + 2].rearrange("p b t -> p (b t)") for s in range(2)]
        with ExitStack() as c:
            u_raw = self.sb(c, "u_raw", [P, 2, D])
            u_hi = self.sb(c, "u_hi", [P, 2, KT, P], F32R)
            u_lo = self.sb(c, "u_lo", [P, 2, KT, P], F32R)
            v_raw = self.sb(c, "v_raw", [P, 2, D])
            v_hi = self.sb(c, "v_hi", [P, 4, D], F32R)
            v_lo = self.sb(c, "v_lo", [P, 4, D], F32R)
            g = self.sb(c, "g", [P, 2, T])
            act_hi = self.sb(c, "act_hi", [P, 4, T], F32R)
            act_lo = self.sb(c, "act_lo", [P, 4, T], F32R)
            flat = lambda w, s: w[:, s].rearrange("p k n -> p (k n)")

            def arrivals(j, s):
                return j * 8 + (16 - 8 * s)
            with nc.Block() as block:
                @block.sync
                def _(sp):
                    def fetch(src, at, to, arrived):
                        sp.dma_start(to, src[bass.ds(at, 1)].rearrange("o p n -> (o p) n")).then_inc(arrived, 16)

                    with sp.Fori(0, E // 2) as it:
                        at = [sp.snap(it * 2 + s) for s in range(2)]
                        free = [sp.snap(it * 2 + (s + 1)) for s in range(2)]
                        for s in range(2):
                            sp.wait_ge(a_split, free[s])
                            fetch(self.route_scr, at[s], g[:, s], g_loaded[s])
                            fetch(self.h_scr, at[s], u_raw[:, s], u_loaded[s])
                            sp.wait_ge(v_split, free[s])
                            fetch(a["peer_v"], at[s], v_raw[:, s], v_loaded[s])
                    for s in range(2):
                        sp.wait_ge(a_split, E + s + 1)
                        fetch(a["peer_uT"], E + s, u_raw[:, s], u_loaded[s])
                        fetch(self.route_scr, E + s, g[:, s], g_loaded[s])
                        sp.wait_ge(v_split, E + s + 1)
                        fetch(a["peer_v"], E + s, v_raw[:, s], v_loaded[s])
                    with sp.Fori(E // 2 + 1, C // 2) as it:
                        at = [sp.snap(it * 2 + s) for s in range(2)]
                        free = [sp.snap(it * 2 + (s + 1)) for s in range(2)]
                        u_free = [sp.snap(it * 2 + (s + 1 - E)) for s in range(2)]
                        for s in range(2):
                            sp.wait_ge(u_split, u_free[s])
                            fetch(a["peer_uT"], at[s], u_raw[:, s], u_loaded[s])
                            sp.wait_ge(a_split, free[s])
                            fetch(self.route_scr, at[s], g[:, s], g_loaded[s])
                            sp.wait_ge(v_split, free[s])
                            fetch(a["peer_v"], at[s], v_raw[:, s], v_loaded[s])

                @block.scalar
                def _(act):
                    def split_u(j, s):
                        act.wait_ge(u_loaded[s], arrivals(j, s))
                        act.activation(flat(u_hi, s), u_raw[:, s], ACT.Copy).then_inc(u_hi_done, 1)

                    def parts(j, ring):
                        s = ring % 2
                        act.wait_ge(weighted, j + 3)
                        act.activation(act_hi[:, ring], g[:, s], ACT.Copy).then_inc(a_hi_done, 1)
                        act.wait_ge(v_loaded[s], arrivals(j, s))
                        act.activation(v_hi[:, ring], v_raw[:, s], ACT.Copy).then_inc(v_hi_done, 1)

                    def late(j, ring, more=True):
                        s = ring % 2
                        act.wait_ge(hidden, j + (1 - E))
                        act.activation(hid[s], hid[s], ACT.Gelu_apprx_tanh).then_inc(gelu_done, 1)
                        if more:
                            split_u(j + 2, s)
                        parts(j, ring)
                    for i in range(4):
                        parts(i, i)
                    with act.Fori(0, E // 4 - 1) as it:
                        for i in range(4, 8):
                            act.wait_ge(summed, it * 2 * TILES + TILES * (i // 2 - 1))
                            parts(it * 4 + i, i % 4)
                    split_u(E, 0)
                    split_u(E + 1, 1)
                    late(E, 0)
                    late(E + 1, 1)
                    with act.Fori(0, (C - E) // 4 - 1) as it:
                        for i in range(2, 6):
                            late(it * 4 + (E + i), i % 4)
                    late(C - 2, 2, more=False)
                    late(C - 1, 3, more=False)

                @block.vector
                def _(dve):
                    dve.memset(y[:], 0.0).then_inc(zeroed, 1)
                    dve.sem_inc(u_split, 2)
                    dve.sem_inc(v_split, 2)
                    dve.sem_inc(weighted, 2)
                    dve.sem_inc(a_split, 2)

                    def split_u(j, s):
                        dve.wait_ge(u_hi_done, j + (1 - E))
                        dve.tensor_tensor(flat(u_lo, s), u_raw[:, s], flat(u_hi, s).bitcast(F32), ALU.subtract).then_inc(u_split, 1)

                    def weigh(j, s, values):
                        dve.wait_ge(g_loaded[s], arrivals(j, s))
                        dve.scalar_tensor_tensor(g[:, s], g[:, s], 1.0 / WEIGHT_SCALE, values, ALU.mult, ALU.mult).then_inc(weighted, 1)

                    def parts(j, ring):
                        s = ring % 2
                        dve.wait_ge(a_hi_done, j + 1)
                        dve.tensor_tensor(act_lo[:, ring], g[:, s], act_hi[:, ring].bitcast(F32), ALU.subtract).then_inc(a_split, 1)
                        dve.wait_ge(v_hi_done, j + 1)
                        dve.tensor_tensor(v_lo[:, ring], v_raw[:, s], v_hi[:, ring].bitcast(F32), ALU.subtract).then_inc(v_split, 1)

                    def early(j, ring, between=lambda: None):
                        s = ring % 2
                        dve.wait_ge(u_loaded[s], arrivals(j, s))
                        weigh(j, s, u_raw[:, s])
                        between()
                        parts(j, ring)

                    def late(j, ring, more=True, between=lambda: None):
                        s = ring % 2
                        dve.wait_ge(gelu_done, j + (1 - E))
                        weigh(j, s, hid[s])
                        if more:
                            split_u(j + 2, s)
                        between()
                        parts(j, ring)

                    def add(pair, tiles=range(TILES)):
                        for n in tiles:
                            k, half = divmod(n, 2)
                            to = y[:, k, half * HALF:(half + 1) * HALF]
                            dve.wait_ge(summed, pair * TILES + (n + 1))
                            dve.tensor_tensor(to, to, ps[:, 4 + n % 4], ALU.add).then_inc(added, 1)

                    def late_pair(first, ring, pair):
                        late(first, ring)
                        late(first + 1, ring + 1, between=lambda: add(pair, range(2)))
                        add(pair, range(2, TILES))
                    for i in range(4):
                        early(i, i)
                    dve.wait_ge(zeroed, 1)
                    add(0)
                    with dve.Fori(0, E // 4 - 1) as it:
                        for p2 in range(2):
                            pair = it * 2 + (1 + p2)
                            early(it * 4 + (4 + 2 * p2), 2 * p2, between=lambda: add(pair, range(3)))
                            add(pair, range(3, 8))
                            early(it * 4 + (5 + 2 * p2), 2 * p2 + 1, between=lambda: add(pair, range(8, 11)))
                            add(pair, range(11, TILES))
                    split_u(E, 0)
                    split_u(E + 1, 1)
                    late(E, 0)
                    late(E + 1, 1, between=lambda: add(E // 2 - 1, range(2)))
                    add(E // 2 - 1, range(2, TILES))
                    with dve.Fori(0, (C - E) // 4 - 1) as it:
                        late_pair(it * 4 + (E + 2), 2, it * 2 + E // 2)
                        late_pair(it * 4 + (E + 4), 0, it * 2 + (E // 2 + 1))
                    late(C - 2, 2, more=False)
                    late(C - 1, 3, more=False, between=lambda: add(C // 2 - 2, range(2)))
                    add(C // 2 - 2, range(2, TILES))
                    add(C // 2 - 1)

                @block.tensor
                def _(pe):
                    pe.sem_inc(added, 4)

                    def up(j, ring):
                        s = ring % 2
                        pe.wait_ge(u_split, j + (3 - E))
                        pe.wait_ge(weighted, j + 1)
                        for half in range(2):
                            t = slice(half * HALF, (half + 1) * HALF)
                            for k in range(KT):
                                last = self.product3(pe, ps[:, 2 * s + half], u_hi[:, s, k], u_lo[:, s, k],
                                                     h2_hi[:, k, t], h2_lo[:, k, t], k == 0, k == KT - 1)
                        last.then_inc(hidden, 1)

                    def down(pair, rings):
                        pe.wait_ge(a_split, pair * 2 + 4)
                        pe.wait_ge(v_split, pair * 2 + 4)
                        for n in range(TILES):
                            k, half = divmod(n, 2)
                            d = slice(k * P, (k + 1) * P)
                            t = slice(half * HALF, (half + 1) * HALF)
                            pe.wait_ge(added, pair * TILES + (n + 1))
                            for r in rings:
                                last = self.product3(pe, ps[:, 4 + n % 4], v_hi[:, r, d], v_lo[:, r, d],
                                                     act_hi[:, r, t], act_lo[:, r, t], r == rings[0], r == rings[1])
                            last.then_inc(summed, 1)
                    with pe.Fori(0, E // 4 - 1) as it:
                        down(it * 2, (0, 1))
                        down(it * 2 + 1, (2, 3))
                    down(E // 2 - 2, (0, 1))
                    up(E, 0)
                    up(E + 1, 1)
                    down(E // 2 - 1, (2, 3))
                    with pe.Fori(0, (C - E) // 4 - 1) as it:
                        up(it * 4 + (E + 2), 2)
                        up(it * 4 + (E + 3), 3)
                        down(it * 2 + E // 2, (0, 1))
                        up(it * 4 + (E + 4), 0)
                        up(it * 4 + (E + 5), 1)
                        down(it * 2 + (E // 2 + 1), (2, 3))
                    up(C - 2, 2)
                    up(C - 1, 3)
                    down(C // 2 - 2, (0, 1))
                    down(C // 2 - 1, (2, 3))


def _tiles(w):
    n = w.shape[1] // P
    return np.ascontiguousarray(w.reshape(KT, P, n, P).transpose(2, 1, 0, 3)).reshape(n, P, KT * P)


def _columns(v):
    return np.asarray(v).reshape(-1, P).T


def kernel(**inputs):
    import concourse.bacc as bacc
    from concourse.bass_utils import run_bass_kernel_spmd

    x = {k: np.asarray(v) for k, v in inputs.items()}
    rot = np.zeros((P, P), np.float32)
    freq = np.zeros((P, 1), np.float32)
    half = ROPE_DIM // 2
    inv = np.float32(ROPE_THETA) ** (-np.arange(0, ROPE_DIM, 2, dtype=np.float32) / np.float32(ROPE_DIM))
    for m in range(2):
        for i in range(half):
            r1, r2 = m * MAP_DIM + i, m * MAP_DIM + half + i
            rot[r2, r1] = -1.0
            rot[r1, r2] = 1.0
            freq[r1, 0] = freq[r2, 0] = inv[i]
    arrays = {
        "xT": x["x"][0].T,
        "c": x["c"],
        "positions": x["positions"],
        "w_adaT": x["w_ada"][0].T.reshape(NMOD, P, D).transpose(1, 0, 2),
        "b_ada": _columns(x["b_ada"][0]),
        "vecs": np.concatenate([_columns(x[n][0]) for n in ("g_pre_mix", "g_post_mix", "g_pre_ffn", "g_post_ffn", "gmlp_ln_g", "gmlp_ln_b")], 1),
        "g_subln": x["g_subln"][0][:, None],
        "lams": np.concatenate([x[n][0] for n in ("lambda_q1", "lambda_k1", "lambda_q2", "lambda_k2")])[None],
        "ident": np.eye(P, dtype=np.float32),
        "rotate": rot,
        "freq": freq,
        "w_in": _tiles(x["w_in"][0]),
        "w_attn": _tiles(x["w_attn_branch"][0]),
        "w_gmlp": _tiles(x["w_gmlp_branch"][0]),
        "w_out": _tiles(x["w_out"][0]),
        "w_peer": _tiles(x["w_peer_q"][0]),
        "w_spatial": x["w_spatial"][0].transpose(2, 0, 1).reshape(P, -1),
        "b_spatial": x["b_spatial"][0].reshape(1, -1),
        "keysT": x["peer_sub_keys"][0].reshape(SIDES, KEYS, P).transpose(2, 0, 1).reshape(P, -1),
        "peer_uT": x["peer_u"][0].reshape(KEYS, P, KT, P).transpose(0, 3, 2, 1).reshape(KEYS, P, D),
        "peer_v": x["peer_v"][0].reshape(KEYS, P, D),
    }
    arrays = {f"{k}_dram": np.ascontiguousarray(v) for k, v in arrays.items()}
    nc = bacc.Bacc("TRN2", target_bir_lowering=False, num_devices=1)
    aps = {k.removesuffix("_dram"): nc.dram_tensor(k, v.shape, mybir.dt.from_np(v.dtype), kind="ExternalInput").ap() for k, v in arrays.items()}
    aps["out"] = nc.dram_tensor("out", (D, T), F32, kind="ExternalOutput").ap()
    Layer(nc, aps).build()
    got = run_bass_kernel_spmd(nc, [arrays], core_ids=[0])
    return got.results[0]["out"].T[None]
```
